# Optimizing a Trainium2 kernel written in Bass

```python
import jax, jax.numpy as jnp
from jax import lax
import numpy as np
import math
import jax
import jax.numpy as jnp

D_MODEL = 1024
BATCH = 1
SEQ = 512
DEPTH = 1

LRU_WIDTH = D_MODEL * 5 // 4
LRU_HEADS = 10
LRU_HEAD_DIM = LRU_WIDTH // LRU_HEADS
LRU_C = 8.0
LRU_CONV = 4
POOL_WIDTH = D_MODEL
POOL_WINDOWS = (2, 4, 8, 16)
POOL_GROUPS = len(POOL_WINDOWS)
POOL_GROUP_DIM = POOL_WIDTH // POOL_GROUPS
N_BRANCHES = 2
IN_WIDTH = LRU_WIDTH + POOL_WIDTH + N_BRANCHES * D_MODEL
D_FF = D_MODEL * 11 // 4
FFN_CONV = 3
RMS_EPS = 1e-6


def rms_norm(x, g):
    x32 = x.astype(jnp.float32)
    y = x32 * lax.rsqrt(jnp.mean(x32 * x32, axis=-1, keepdims=True) + RMS_EPS)
    return (y * g.astype(jnp.float32)).astype(x.dtype)

def depthwise_conv(x, w, b, left):
    k_width = w.shape[0]
    s = x.shape[1]
    xp = jnp.pad(x, ((0, 0), (left, k_width - 1 - left), (0, 0)))
    y = b
    for k in range(k_width):
        y = y + w[k] * xp[:, k:k + s]
    return y

def block_diag(x, w, b):
    bsz, s, _ = x.shape
    h, i, j = w.shape
    y = jnp.einsum('bshi,hij->bshj', x.reshape(bsz, s, h, i), w)
    return y.reshape(bsz, s, h * j) + b

def _lin_combine(left, right):
    a_l, b_l = left
    a_r, b_r = right
    return a_l * a_r, a_r * b_l + b_r

def rglru_direction(xc, wa, ba, wx, bx, lam, reverse):
    x32 = xc.astype(jnp.float32)
    r = jax.nn.sigmoid(block_diag(xc, wa, ba).astype(jnp.float32))
    i = jax.nn.sigmoid(block_diag(xc, wx, bx).astype(jnp.float32))
    log_a = -LRU_C * r * jax.nn.softplus(-lam.astype(jnp.float32))
    a = jnp.exp(log_a)
    b_in = jnp.sqrt(-jnp.expm1(2.0 * log_a)) * (i * x32)
    _, h = lax.associative_scan(_lin_combine, (a, b_in), axis=1, reverse=reverse)
    return h

def multiscale_pool(u):
    bsz, s, width = u.shape
    u32 = u.astype(jnp.float32)
    csum = jnp.concatenate([jnp.zeros((bsz, 1, width), jnp.float32),
                            jnp.cumsum(u32, axis=1)], axis=1)
    t = jnp.arange(s)
    outs = []
    for g, w in enumerate(POOL_WINDOWS):
        sl = slice(g * POOL_GROUP_DIM, (g + 1) * POOL_GROUP_DIM)
        cg = csum[..., sl]
        lo = jnp.clip(t - w // 2, 0, s - 1)
        hi = jnp.clip(t + w // 2 - 1, 0, s - 1)
        win_sum = jnp.take(cg, hi + 1, axis=1) - jnp.take(cg, lo, axis=1)
        count = (hi - lo + 1).astype(jnp.float32)[None, :, None]
        outs.append(win_sum / count - u32[..., sl])
    return jnp.concatenate(outs, axis=-1).astype(u.dtype)

def first_inputs(seed: int = 0) -> dict:
    key = jax.random.key(seed)
    ks = jax.random.split(key, 32)
    f32 = jnp.float32
    L = DEPTH

    def nrm(k, shape, scale):
        return jax.random.normal(k, shape, f32) * scale

    def gain(k, shape):
        return 1.0 + 0.05 * jax.random.normal(k, shape, f32)

    def lru_lambda(k):
        u = jax.random.uniform(k, (L, LRU_WIDTH), f32, 0.9, 0.999)
        s = u ** (1.0 / LRU_C)
        return jnp.log(s) - jnp.log1p(-s)

    return {
        "x": jax.random.normal(ks[0], (BATCH, SEQ, D_MODEL), f32),
        "g_mix": gain(ks[1], (L, D_MODEL)),
        "w_in": nrm(ks[2], (L, D_MODEL, IN_WIDTH), D_MODEL ** -0.5),
        "b_gate": nrm(ks[3], (L, N_BRANCHES * D_MODEL), 0.01),
        "conv_a_w": nrm(ks[4], (L, LRU_CONV, LRU_WIDTH), LRU_CONV ** -0.5),
        "conv_a_b": nrm(ks[5], (L, LRU_WIDTH), 0.01),
        "wa_f": nrm(ks[6], (L, LRU_HEADS, LRU_HEAD_DIM, LRU_HEAD_DIM), LRU_HEAD_DIM ** -0.5),
        "ba_f": nrm(ks[7], (L, LRU_WIDTH), 0.01),
        "wx_f": nrm(ks[8], (L, LRU_HEADS, LRU_HEAD_DIM, LRU_HEAD_DIM), LRU_HEAD_DIM ** -0.5),
        "bx_f": nrm(ks[9], (L, LRU_WIDTH), 0.01),
        "lam_f": lru_lambda(ks[10]),
        "wa_b": nrm(ks[11], (L, LRU_HEADS, LRU_HEAD_DIM, LRU_HEAD_DIM), LRU_HEAD_DIM ** -0.5),
        "ba_b": nrm(ks[12], (L, LRU_WIDTH), 0.01),
        "wx_b": nrm(ks[13], (L, LRU_HEADS, LRU_HEAD_DIM, LRU_HEAD_DIM), LRU_HEAD_DIM ** -0.5),
        "bx_b": nrm(ks[14], (L, LRU_WIDTH), 0.01),
        "lam_b": lru_lambda(ks[15]),
        "w_pool": nrm(ks[16], (L, POOL_GROUPS, POOL_GROUP_DIM, POOL_GROUP_DIM), POOL_GROUP_DIM ** -0.5),
        "b_pool": nrm(ks[17], (L, POOL_WIDTH), 0.01),
        "pool_scale": gain(ks[18], (L, POOL_WIDTH)),
        "p_a": nrm(ks[19], (L, LRU_WIDTH, D_MODEL), LRU_WIDTH ** -0.5),
        "p_b": nrm(ks[20], (L, POOL_WIDTH, D_MODEL), POOL_WIDTH ** -0.5),
        "w_out": nrm(ks[21], (L, D_MODEL, D_MODEL), D_MODEL ** -0.5),
        "g_ffn": gain(ks[22], (L, D_MODEL)),
        "w_up": nrm(ks[23], (L, D_MODEL, 2 * D_FF), D_MODEL ** -0.5),
        "conv_f_w": nrm(ks[24], (L, FFN_CONV, 2 * D_FF), FFN_CONV ** -0.5),
        "conv_f_b": nrm(ks[25], (L, 2 * D_FF), 0.01),
        "w_down": nrm(ks[26], (L, D_FF, D_MODEL), D_FF ** -0.5),
        "g_final": gain(ks[27], (D_MODEL,)),
    }

def first_block(x, g_mix, w_in, b_gate, conv_a_w, conv_a_b, wa_f, ba_f, wx_f, bx_f, lam_f,
              wa_b, ba_b, wx_b, bx_b, lam_b, w_pool, b_pool, pool_scale, p_a, p_b, w_out,
              g_ffn, w_up, conv_f_w, conv_f_b, w_down, g_final):
    for l in range(DEPTH):
        h = rms_norm(x, g_mix[l])
        proj = h @ w_in[l]
        u_a = proj[..., :LRU_WIDTH]
        u_b = proj[..., LRU_WIDTH:LRU_WIDTH + POOL_WIDTH]
        gate_logits = proj[..., LRU_WIDTH + POOL_WIDTH:] + b_gate[l]

        xa = depthwise_conv(u_a, conv_a_w[l], conv_a_b[l], LRU_CONV // 2)
        h_fwd = rglru_direction(xa, wa_f[l], ba_f[l], wx_f[l], bx_f[l], lam_f[l], False)
        h_bwd = rglru_direction(xa, wa_b[l], ba_b[l], wx_b[l], bx_b[l], lam_b[l], True)
        y_a = (h_fwd + h_bwd).astype(x.dtype) @ p_a[l]

        pooled = multiscale_pool(u_b)
        y_b = (block_diag(pooled, w_pool[l], b_pool[l]) * pool_scale[l]) @ p_b[l]

        gates = jax.nn.sigmoid(gate_logits.astype(jnp.float32)).astype(x.dtype)
        merged = gates[..., :D_MODEL] * y_a + gates[..., D_MODEL:] * y_b
        x = x + merged @ w_out[l]

        h = rms_norm(x, g_ffn[l])
        up = depthwise_conv(h @ w_up[l], conv_f_w[l], conv_f_b[l], FFN_CONV // 2)
        act = jax.nn.gelu(up[..., :D_FF], approximate=True) * up[..., D_FF:]
        x = x + act @ w_down[l]
    return rms_norm(x, g_final)


SSM_WIDTH = 512
SSM_GROUP = 16
SSM_GROUPS = SSM_WIDTH // SSM_GROUP
SSM_STATE = 64
ATT_HEADS = 8
ATT_HEAD_DIM = 64
ATT_WIDTH = ATT_HEADS * ATT_HEAD_DIM
KV_LATENT = 128
IDX_HEADS = 4
IDX_HEAD_DIM = 64
TOPK_MAX = 256
Q_BLOCK = 128
FFN_HIDDEN = ((-(-8 * D_MODEL // 3) + 255) // 256) * 256
IN_SIZES = (SSM_WIDTH, ATT_WIDTH, KV_LATENT, IDX_HEADS * IDX_HEAD_DIM, IDX_HEAD_DIM, IDX_HEADS, D_MODEL, D_MODEL)
D_IN = sum(IN_SIZES)
EPS = 1e-6


def rms_norm_2(x, g):
    xf = x.astype(jnp.float32)
    y = xf * lax.rsqrt(jnp.mean(xf * xf, axis=-1, keepdims=True) + EPS)
    return (y * g.astype(jnp.float32)).astype(x.dtype)

def split_cols(z, sizes):
    offs = []
    o = 0
    for s in sizes[:-1]:
        o += s
        offs.append(o)
    return jnp.split(z, offs, axis=-1)

def s5_branch(xs, a_re, a_im, log_dt, b_re, b_im, c_re, c_im, d_skip, w_glu, b_glu):
    bsz, seq, _ = xs.shape
    xg = xs.reshape(bsz, seq, SSM_GROUPS, SSM_GROUP)
    dt = jnp.exp(log_dt)[:, None]
    mag = jnp.exp(a_re * dt)
    ang = a_im * dt
    lb_re = mag * jnp.cos(ang)
    lb_im = mag * jnp.sin(ang)
    den = a_re * a_re + a_im * a_im
    coef_re = ((lb_re - 1.0) * a_re + lb_im * a_im) / den
    coef_im = (lb_im * a_re - (lb_re - 1.0) * a_im) / den
    bb_re = coef_re[..., None] * b_re - coef_im[..., None] * b_im
    bb_im = coef_re[..., None] * b_im + coef_im[..., None] * b_re
    bu_re = jnp.einsum('blgc,gpc->blgp', xg, bb_re)
    bu_im = jnp.einsum('blgc,gpc->blgp', xg, bb_im)
    ar = jnp.broadcast_to(lb_re, bu_re.shape)
    ai = jnp.broadcast_to(lb_im, bu_im.shape)

    def combine(e1, e2):
        a1r, a1i, b1r, b1i = e1
        a2r, a2i, b2r, b2i = e2
        nar = a1r * a2r - a1i * a2i
        nai = a1r * a2i + a1i * a2r
        nbr = a2r * b1r - a2i * b1i + b2r
        nbi = a2r * b1i + a2i * b1r + b2i
        return (nar, nai, nbr, nbi)

    _, _, s_re, s_im = lax.associative_scan(combine, (ar, ai, bu_re, bu_im), axis=1)
    y = jnp.einsum('blgp,gcp->blgc', s_re, c_re) - jnp.einsum('blgp,gcp->blgc', s_im, c_im)
    y = y.reshape(bsz, seq, SSM_WIDTH) + d_skip * xs
    y = jax.nn.gelu(y)
    z = y @ w_glu + b_glu
    val, gate = jnp.split(z, 2, axis=-1)
    return val * jax.nn.sigmoid(gate)

def dsa_branch(q, c_kv, q_idx, k_idx, w_idx, w_uk, w_uv):
    bsz, seq = q.shape[0], q.shape[1]
    topk = min(TOPK_MAX, seq // 4)
    nblk = seq // Q_BLOCK
    q_lat = jnp.einsum('blhd,chd->blhc', q, w_uk) * (ATT_HEAD_DIM ** -0.5)
    w_idx = w_idx * (IDX_HEADS ** -0.5)
    q_idx = q_idx * (IDX_HEAD_DIM ** -0.5)

    def to_blocks(t):
        return jnp.moveaxis(t.reshape((bsz, nblk, Q_BLOCK) + t.shape[2:]), 1, 0)

    key_pos = jnp.arange(seq)

    def one_block(args):
        blk, ql, qi, wi = args
        q_pos = blk * Q_BLOCK + jnp.arange(Q_BLOCK)
        rel = jax.nn.relu(jnp.einsum('bqhd,bkd->bqhk', qi, k_idx).astype(jnp.float32))
        iscore = jnp.einsum('bqhk,bqh->bqk', rel, wi.astype(jnp.float32))
        causal = key_pos[None, :] <= q_pos[:, None]
        iscore = jnp.where(causal[None], iscore, -jnp.inf)
        _, sel = lax.top_k(iscore, topk)
        valid = sel <= q_pos[None, :, None]
        c_sel = jax.vmap(lambda cb, ib: cb[ib])(c_kv, sel)
        logits = jnp.einsum('bqhc,bqkc->bhqk', ql, c_sel).astype(jnp.float32)
        logits = jnp.where(valid[:, None], logits, -jnp.inf)
        p = jax.nn.softmax(logits, axis=-1).astype(c_sel.dtype)
        return jnp.einsum('bhqk,bqkc->bqhc', p, c_sel)

    o = lax.map(one_block, (jnp.arange(nblk), to_blocks(q_lat), to_blocks(q_idx), to_blocks(w_idx)))
    o = jnp.moveaxis(o, 0, 1).reshape(bsz, seq, ATT_HEADS, KV_LATENT)
    out = jnp.einsum('blhc,chd->blhd', o, w_uv)
    return out.reshape(bsz, seq, ATT_WIDTH)

def second_inputs(seed: int = 0) -> dict:
    key = jax.random.key(seed)
    ks = jax.random.split(key, 27)
    f32 = jnp.float32

    def nrm(k, shape, s):
        return jax.random.normal(k, shape, f32) * s

    def gain(k, shape):
        return 1.0 + 0.05 * jax.random.normal(k, shape, f32)

    G, P, Cg = SSM_GROUPS, SSM_STATE, SSM_GROUP
    a_im0 = jnp.broadcast_to(jnp.pi * jnp.arange(P, dtype=f32), (DEPTH, G, P))
    return {
        'x': nrm(ks[0], (BATCH, SEQ, D_MODEL), 1.0),
        'c': nrm(ks[1], (BATCH, D_MODEL), 1.0),
        'w_mod': nrm(ks[2], (DEPTH, D_MODEL, 6 * D_MODEL), 0.5 * D_MODEL ** -0.5),
        'b_mod': nrm(ks[3], (DEPTH, 6 * D_MODEL), 0.01),
        'norm1_g': gain(ks[4], (DEPTH, D_MODEL)),
        'w_in': nrm(ks[5], (DEPTH, D_MODEL, D_IN), D_MODEL ** -0.5),
        'ssm_a_re': -0.5 + nrm(ks[6], (DEPTH, G, P), 0.01),
        'ssm_a_im': a_im0 + nrm(ks[7], (DEPTH, G, P), 0.01),
        'ssm_log_dt': jax.random.uniform(ks[8], (DEPTH, G), f32, math.log(1e-3), math.log(1e-1)),
        'ssm_b_re': nrm(ks[9], (DEPTH, G, P, Cg), (2 * Cg) ** -0.5),
        'ssm_b_im': nrm(ks[10], (DEPTH, G, P, Cg), (2 * Cg) ** -0.5),
        'ssm_c_re': nrm(ks[11], (DEPTH, G, Cg, P), (2 * P) ** -0.5),
        'ssm_c_im': nrm(ks[12], (DEPTH, G, Cg, P), (2 * P) ** -0.5),
        'ssm_d': nrm(ks[13], (DEPTH, SSM_WIDTH), 1.0),
        'w_ssm_glu': nrm(ks[14], (DEPTH, SSM_WIDTH, 2 * D_MODEL), SSM_WIDTH ** -0.5),
        'b_ssm_glu': nrm(ks[15], (DEPTH, 2 * D_MODEL), 0.01),
        'kv_norm_g': gain(ks[16], (DEPTH, KV_LATENT)),
        'idx_k_norm_g': gain(ks[17], (DEPTH, IDX_HEAD_DIM)),
        'w_uk': nrm(ks[18], (DEPTH, KV_LATENT, ATT_HEADS, ATT_HEAD_DIM), KV_LATENT ** -0.5),
        'w_uv': nrm(ks[19], (DEPTH, KV_LATENT, ATT_HEADS, ATT_HEAD_DIM), KV_LATENT ** -0.5),
        'w_attn_proj': nrm(ks[20], (DEPTH, ATT_WIDTH, D_MODEL), ATT_WIDTH ** -0.5),
        'w_out': nrm(ks[21], (DEPTH, D_MODEL, D_MODEL), D_MODEL ** -0.5),
        'norm2_g': gain(ks[22], (DEPTH, D_MODEL)),
        'w_ffn_gate': nrm(ks[23], (DEPTH, D_MODEL, FFN_HIDDEN), D_MODEL ** -0.5),
        'w_ffn_up': nrm(ks[24], (DEPTH, D_MODEL, FFN_HIDDEN), D_MODEL ** -0.5),
        'w_ffn_down': nrm(ks[25], (DEPTH, FFN_HIDDEN, D_MODEL), FFN_HIDDEN ** -0.5),
        'final_g': gain(ks[26], (D_MODEL,)),
    }

def second_block(x, c, w_mod, b_mod, norm1_g, w_in, ssm_a_re, ssm_a_im, ssm_log_dt, ssm_b_re, ssm_b_im, ssm_c_re, ssm_c_im, ssm_d, w_ssm_glu, b_ssm_glu, kv_norm_g, idx_k_norm_g, w_uk, w_uv, w_attn_proj, w_out, norm2_g, w_ffn_gate, w_ffn_up, w_ffn_down, final_g):
    bsz, seq, _ = x.shape
    h = x
    cond = jax.nn.silu(c)
    for layer in range(DEPTH):
        mod = cond @ w_mod[layer] + b_mod[layer]
        shift1, scale1, gate1, shift2, scale2, gate2 = jnp.split(mod[:, None, :], 6, axis=-1)
        u = rms_norm_2(h, norm1_g[layer]) * (1.0 + scale1) + shift1
        xs, q, ckv, qi, ki, wi, ga, gb = split_cols(u @ w_in[layer], IN_SIZES)
        y_ssm = s5_branch(xs, ssm_a_re[layer], ssm_a_im[layer], ssm_log_dt[layer], ssm_b_re[layer], ssm_b_im[layer], ssm_c_re[layer], ssm_c_im[layer], ssm_d[layer], w_ssm_glu[layer], b_ssm_glu[layer])
        y_att = dsa_branch(q.reshape(bsz, seq, ATT_HEADS, ATT_HEAD_DIM), rms_norm_2(ckv, kv_norm_g[layer]), qi.reshape(bsz, seq, IDX_HEADS, IDX_HEAD_DIM), rms_norm_2(ki, idx_k_norm_g[layer]), wi, w_uk[layer], w_uv[layer]) @ w_attn_proj[layer]
        merged = jax.nn.sigmoid(ga) * y_ssm + jax.nn.sigmoid(gb) * y_att
        h = h + gate1 * (merged @ w_out[layer])
        u2 = rms_norm_2(h, norm2_g[layer]) * (1.0 + scale2) + shift2
        ffn = (jax.nn.silu(u2 @ w_ffn_gate[layer]) * (u2 @ w_ffn_up[layer])) @ w_ffn_down[layer]
        h = h + gate2 * ffn
    return rms_norm_2(h, final_g)


def setup_inputs(seed=0):
    out = dict(first_inputs(seed))
    for name, value in second_inputs(seed + 1).items():
        if name != "x":
            out[name + "_2"] = value
    return out


def reference(
    x, g_mix, w_in, b_gate, conv_a_w, conv_a_b, wa_f, ba_f, wx_f, bx_f, lam_f, wa_b, ba_b, wx_b,
    bx_b, lam_b, w_pool, b_pool, pool_scale, p_a, p_b, w_out, g_ffn, w_up, conv_f_w, conv_f_b,
    w_down, g_final, c_2, w_mod_2, b_mod_2, norm1_g_2, w_in_2, ssm_a_re_2, ssm_a_im_2,
    ssm_log_dt_2, ssm_b_re_2, ssm_b_im_2, ssm_c_re_2, ssm_c_im_2, ssm_d_2, w_ssm_glu_2,
    b_ssm_glu_2, kv_norm_g_2, idx_k_norm_g_2, w_uk_2, w_uv_2, w_attn_proj_2, w_out_2, norm2_g_2,
    w_ffn_gate_2, w_ffn_up_2, w_ffn_down_2, final_g_2,
):
    x = first_block(
        x, g_mix, w_in, b_gate, conv_a_w, conv_a_b, wa_f, ba_f, wx_f, bx_f, lam_f, wa_b, ba_b,
        wx_b, bx_b, lam_b, w_pool, b_pool, pool_scale, p_a, p_b, w_out, g_ffn, w_up, conv_f_w,
        conv_f_b, w_down, g_final,
    )
    return second_block(
        x, c_2, w_mod_2, b_mod_2, norm1_g_2, w_in_2, ssm_a_re_2, ssm_a_im_2, ssm_log_dt_2,
        ssm_b_re_2, ssm_b_im_2, ssm_c_re_2, ssm_c_im_2, ssm_d_2, w_ssm_glu_2, b_ssm_glu_2,
        kv_norm_g_2, idx_k_norm_g_2, w_uk_2, w_uv_2, w_attn_proj_2, w_out_2, norm2_g_2,
        w_ffn_gate_2, w_ffn_up_2, w_ffn_down_2, final_g_2,
    )


_drawn_inputs = setup_inputs


def setup_inputs(seed=0):
    import zlib

    import numpy as np

    out = dict(_drawn_inputs(seed))
    spreads = {}
    factors = {'b_gate': 8.0,
     'ba_f': 8.0,
     'bx_f': 8.0,
     'ba_b': 8.0,
     'bx_b': 8.0,
     'b_pool': 8.0,
     'conv_f_b': 7.528,
     'b_mod_2': 5.779,
     'norm1_g_2': 8.0,
     'ssm_a_re_2': 64.0,
     'ssm_a_im_2': 64.0,
     'ssm_log_dt_2': 64.0,
     'ssm_b_re_2': 64.0,
     'ssm_b_im_2': 64.0,
     'ssm_c_re_2': 64.0,
     'ssm_c_im_2': 64.0,
     'b_ssm_glu_2': 46.898,
     'kv_norm_g_2': 8.0,
     'idx_k_norm_g_2': 8.0,
     'norm2_g_2': 3.892}
    for name, (base, spread) in spreads.items():
        noise = np.random.default_rng([zlib.crc32(name.encode()), seed]).standard_normal(out[name].shape)
        drawn = base * np.exp(spread * noise) if base else spread * noise
        out[name] = jnp.asarray(drawn.astype(out[name].dtype))
    for name, factor in factors.items():
        out[name] = (out[name] * factor).astype(out[name].dtype)
    return out
```

```python
from contextlib import ExitStack

import numpy as np

import concourse.bass as bass
from concourse import mybir

F32 = mybir.dt.float32
F32R = mybir.dt.float32r
ALU = mybir.AluOpType
ACT = mybir.ActivationFunctionType
AX_X = mybir.AxisListType.X

S = 512
UB = 8
NRAW = 3
NHL = 3
LOOK = 2
NBLK = 1976
NUNIT = NBLK // UB
EPS = 1e-6
NEG = -3.0e38
BIG = 1.0e30

VECS = [
    ("g_mix", 8), ("b_gate", 16), ("conv_a_w", 40), ("conv_a_b", 10),
    ("ba_f", 10), ("bx_f", 10), ("ba_b", 10), ("bx_b", 10), ("lam_f", 10), ("lam_b", 10),
    ("b_pool", 8), ("pool_scale", 8), ("g_ffn", 8), ("conv_f_w", 132), ("conv_f_b", 44),
    ("g_final", 8), ("c_2", 8), ("b_mod_2", 48), ("norm1_g_2", 8), ("ssm_a_re_2", 16),
    ("ssm_a_im_2", 16), ("ssm_log_dt_2", 16), ("ssm_d_2", 4), ("b_ssm_glu_2", 16),
    ("kv_norm_g_2", 1), ("idx_k_norm_g_2", 1), ("norm2_g_2", 8), ("final_g_2", 8),
]
VOFF = {}
NV = 0
for _n, _c in VECS:
    VOFF[_n] = NV
    NV += _c


class Engine:

    def __init__(self, eng, sem):
        self.eng, self.sem, self.n, self.seen = eng, sem, 0, {}

    def wait(self, *marks):
        for m in marks:
            if m is None:
                continue
            if isinstance(m, list):
                self.wait(*m)
                continue
            sem, value = m
            if self.seen.get(id(sem), 0) < value:
                self.seen[id(sem)] = value
                self.eng.wait_ge(sem, value)

    def mark(self, ins):
        self.n += 1
        ins.then_inc(self.sem, 1)
        return (self.sem, self.n)

    def op(self, fn, *args, w=(), **kw):
        self.wait(*w)
        return self.mark(fn(*args, **kw))

    def now(self):
        return (self.sem, self.n) if self.n else None


class Slots:

    def __init__(self, views):
        self.views, self.free = views, [(v, []) for v in range(len(views))]
        self.low = len(views)

    def take(self):
        i, marks = self.free.pop(0)
        self.low = min(self.low, len(self.free))
        return Slot(self, i, marks)


class Slot:
    def __init__(self, pool, i, marks):
        self.pool, self.i, self.ap, self.old = pool, i, pool.views[i], marks

    def give(self, *marks):
        self.pool.free.append((self.i, [m for m in marks if m is not None]))


class Pair:

    def __init__(self, hi, lo):
        self.hi, self.lo, self.ready = hi, lo, None

    def give(self, *marks):
        self.hi.give(*marks)
        self.lo.give(*marks)


def build(nc, x_d, w_d, mod_d, vec_d, cst_d, inv_d, ssm_d, uk_d, out_d, plan, modplan):
    V, A, T, P = nc.vector, nc.scalar, nc.tensor, nc.gpsimd
    with ExitStack() as top:
        def sb(name, shape, dt=F32, ctx=top):
            return ctx.enter_context(nc.sbuf_tensor(name, shape, dt))

        def sem(name):
            return top.enter_context(nc.semaphore(name))

        pe = Engine(T, sem("s_pe"))
        dve = Engine(V, sem("s_dve"))
        act = Engine(A, sem("s_act"))
        pool = Engine(P, sem("s_pool"))
        sp = Engine(nc.sync, sem("s_sp"))
        s_raw = [sem(f"s_raw{i}") for i in range(NRAW)]
        s_mod = [sem(f"s_mod{i}") for i in range(2)]
        s_cst = sem("s_cst")
        s_x = sem("s_x")
        s_ssm = sem("s_ssm")
        s_inv = sem("s_inv")
        s_ki = sem("s_ki")
        s_out = sem("s_out")

        banks_t = [top.enter_context(nc.psum_tensor(f"ps{i}", [128, S], F32)) for i in range(8)]
        misc = banks_t[7]
        banks = Slots([b[:, :] for b in banks_t[:7]])

        raw = sb("raw", [128, NRAW, UB * 128])
        whi = sb("whi", [128, NHL, UB * 128], F32R)
        wlo = sb("wlo", [128, NHL, UB * 128], F32R)
        vec = sb("vec", [128, NV])
        cst = sb("cst", [128, 3, 128])
        ident, ones, tri = cst[:, 0, :], cst[:, 1, :], cst[:, 2, :]
        sml = sb("sml", [128, 512])
        xt = sb("xt", [128, 8, S])
        keep = sb("keep", [128, S])

        def vc(name, j=0, n=1):
            o = VOFF[name] + j
            return vec[:, o:o + n]

        unit_split = {}
        unit_done = {}

        def load_unit(u):
            if u >= NUNIT:
                return
            if u >= NRAW:
                sp.wait(unit_split[u - NRAW])
            nc.sync.dma_start(raw[:, u % NRAW, :], w_d[u]).then_inc(s_raw[u % NRAW], 16)

        def split_unit(u):
            if u >= NUNIT or u in unit_split:
                return
            landed = (s_raw[u % NRAW], 16 * (u // NRAW + 1))
            h, l, r = whi[:, u % NHL, :], wlo[:, u % NHL, :], raw[:, u % NRAW, :]
            used = unit_done[u - NHL] if u >= NHL else None
            hi_made = act.op(A.activation, h, r, ACT.Copy, w=[landed, used])
            lo_made = pool.op(P.tensor_tensor, l, r, h.bitcast(F32), ALU.subtract, w=[hi_made])
            unit_split[u] = lo_made
            load_unit(u + NRAW)

        def matmul3(out, whi_ap, wlo_ap, hi, lo, start, stop):
            T.matmul(out, whi_ap, hi, start=start, stop=False)
            T.matmul(out, whi_ap, lo, start=False, stop=False)
            return T.matmul(out, wlo_ap, hi, start=False, stop=stop)

        def group(blocks, pairs, out=None):
            bank = banks.take()
            pe.wait(*bank.old)
            n = len(blocks)
            for i, (b, p) in enumerate(zip(blocks, pairs)):
                k = len(plan)
                u, j = divmod(k, UB)
                if j == 0:
                    for a in range(LOOK + 1):
                        split_unit(u + a)
                    pe.wait(unit_split[u])
                plan.append(b)
                pe.wait(p.ready)
                c = slice(128 * j, 128 * j + 128)
                mm = matmul3(bank.ap, whi[:, u % NHL, c], wlo[:, u % NHL, c], p.hi.ap, p.lo.ap,
                             i == 0, i == n - 1)
                if j == UB - 1 or i == n - 1:
                    m = pe.mark(mm)
                    if j == UB - 1:
                        unit_done[u] = m
            bank.made = m
            return bank

        def kblocks(name, m, nk, k0=0):
            return [(name, k, m) for k in range(k0, k0 + nk)]

        def take_pair(R):
            return Pair(R.take(), R.take())

        def split(src, made, R, eng="pool", copy_on="act"):
            p = take_pair(R)
            if copy_on == "act":
                a = act.op(A.activation, p.hi.ap, src, ACT.Copy, w=[made, *p.hi.old])
            else:
                a = dve.op(V.tensor_copy, p.hi.ap, src, w=[made, *p.hi.old])
            hf = p.hi.ap.bitcast(F32)
            if eng == "pool":
                b = pool.op(P.tensor_tensor, p.lo.ap, src, hf, ALU.subtract, w=[a, *p.lo.old])
            else:
                b = dve.op(V.tensor_tensor, p.lo.ap, src, hf, ALU.subtract, w=[a, *p.lo.old])
            p.ready = b
            return p

        class Norm:

            def __init__(self, F):
                self.F, self.acc, self.m = F, None, None

            def add(self, ap, made):
                q = self.F.take()
                a = act.op(A.activation, q.ap, ap, ACT.Square, w=[made, *q.old])
                if self.acc is None:
                    self.acc, self.m = q, a
                else:
                    self.m = dve.op(V.tensor_tensor, self.acc.ap, self.acc.ap, q.ap, ALU.add,
                                    w=[a, self.m])
                    q.give(self.m)

            def rs(self, width, rows=128):
                b = banks.take()
                pe.wait(self.m, *b.old)
                mm = pe.mark(T.matmul(b.ap[0:rows], ones[0:rows, 0:rows], self.acc.ap[0:rows],
                                      start=True, stop=True))
                r = self.acc
                s = act.op(A.activation, r.ap[0:rows], b.ap[0:rows], ACT.Sqrt, bias=epsc,
                           scale=1.0 / width, w=[mm])
                b.give(s)
                self.m = dve.op(V.reciprocal, r.ap[0:rows], r.ap[0:rows], w=[s])
                return r, self.m

        A.dma_start(vec[:, :], vec_d).then_inc(s_cst, 16)
        A.dma_start(cst[:, 0, :], cst_d[0]).then_inc(s_cst, 16)
        A.dma_start(cst[:, 2, :], cst_d[1]).then_inc(s_cst, 16)
        cst_in = (s_cst, 48)
        for m in range(8):
            nc.sync.dma_start(xt[:, m, :], x_d[m]).then_inc(s_x, 16)
        for u in range(NRAW):
            load_unit(u)
        epsc = EPS
        ones_m = dve.op(V.memset, ones, 1.0)

        C8F, C8B, NC8F, NC8B, COND, PW, MOD, GS1, GS2 = 0, 10, 20, 30, 40, 48, 200, 248, 256
        RSUM, MX, NMX, M8, TMPV = 264, 268, 272, 276, 284

        t0 = sml[:, 300:320]
        t1 = sml[:, 320:340]
        t2 = sml[:, 340:360]
        t3 = sml[:, 360:380]
        lam = vc("lam_f", 0, 20)
        for e in (pe, dve, act, pool):
            e.wait(cst_in)
        m = dve.op(V.tensor_scalar, t0, lam, -1.0, None, ALU.mult, w=[cst_in])
        m = dve.op(V.tensor_tensor, t0, t0, lam, ALU.min, w=[m])
        m = act.op(A.activation, t1, t0, ACT.Exp, w=[m])
        m = dve.op(V.tensor_scalar, t2, t1, 2.0, None, ALU.add, w=[m])
        m = dve.op(V.reciprocal, t2, t2, w=[m])
        m = dve.op(V.tensor_tensor, t1, t1, t2, ALU.mult, w=[m])
        m = dve.op(V.tensor_tensor, t2, t1, t1, ALU.mult, w=[m])
        m = dve.op(V.memset, t3, 1.0 / 19.0, w=[m])
        for k in (17, 15, 13, 11, 9, 7, 5, 3, 1):
            m = dve.op(V.tensor_tensor, t3, t3, t2, ALU.mult, w=[m])
            m = dve.op(V.tensor_scalar, t3, t3, 1.0 / k, None, ALU.add, w=[m])
        m = dve.op(V.tensor_tensor, t3, t3, t1, ALU.mult, w=[m])
        m = dve.op(V.tensor_scalar, t2, lam, -1.0, 0.0, ALU.mult, ALU.max, w=[m])
        m = dve.op(V.scalar_tensor_tensor, t3, t3, 2.0, t2, ALU.mult, ALU.add, w=[m])
        m = dve.op(V.tensor_scalar, sml[:, C8F:C8F + 20], t3, 8.0, None, ALU.mult, w=[m])
        c8_m = dve.op(V.tensor_scalar, sml[:, NC8F:NC8F + 20], t3, -8.0, None, ALU.mult, w=[m])
        cond_m = act.op(A.activation, sml[:, COND:COND + 8], vc("c_2", 0, 8), ACT.Silu,
                        w=[cst_in])

        x_m = [(s_x, 16 * 8)] * 8
        with ExitStack() as c1:
            inv = sb("inv", [128, 4, S], ctx=c1)
            rt = sb("r1", [128, 53, S], F32R, ctx=c1)
            ft = sb("f1", [128, 15, S + 16], ctx=c1)
            R = Slots([rt[:, i, :] for i in range(53)])
            F = Slots([ft[:, i, 0:S] for i in range(15)])
            A.dma_start(inv[:, :, :], inv_d).then_inc(s_inv, 16)

            nrm = Norm(F)
            for m in range(8):
                nrm.add(xt[:, m, :], x_m[m])
            dve.wait(ones_m)
            pe.wait(ones_m)
            rs, rs_m = nrm.rs(1024)
            h = []
            for m in range(8):
                f = F.take()
                a = dve.op(V.scalar_tensor_tensor, f.ap, xt[:, m, :], vc("g_mix", m), rs.ap,
                           ALU.mult, ALU.mult, w=[rs_m, *f.old])
                p = split(f.ap, a, R, eng="dve" if m % 2 else "pool")
                f.give(p.ready)
                h.append(p)
            rs.give(a)

            def lru_in(i):
                b = group(kblocks("w_in", i, 8), h)
                xa = F.take()
                a = act.op(A.activation, xa.ap, b.ap, ACT.Identity, bias=vc("conv_a_b", i),
                           scale=vc("conv_a_w", 20 + i), w=[b.made, *xa.old])
                for k, (d, s) in ((0, (slice(2, S), slice(0, S - 2))),
                                  (1, (slice(1, S), slice(0, S - 1))),
                                  (3, (slice(0, S - 1), slice(1, S)))):
                    a = dve.op(V.scalar_tensor_tensor, xa.ap[:, d], b.ap[:, s],
                               vc("conv_a_w", 10 * k + i), xa.ap[:, d], ALU.mult, ALU.add, w=[a])
                b.give(a)
                p = split(xa.ap, a, R)
                return i, xa, p, a

            def lru_gates(i, xa, p, xa_m):
                banks4 = [group([(n, i, i)], [p]) for n in ("wa_f", "wx_f", "wa_b", "wx_b")]
                p.give(banks4[-1].made)
                rr, ii, th, q = [], [], [], []
                for d, (ba, bx) in enumerate((("ba_f", "bx_f"), ("ba_b", "bx_b"))):
                    for lst, b, n in ((rr, banks4[2 * d], ba), (ii, banks4[2 * d + 1], bx)):
                        f = F.take()
                        f.made = act.op(A.activation, f.ap, b.ap, ACT.Sigmoid, bias=vc(n, i),
                                        w=[b.made, *f.old])
                        b.give(f.made)
                        lst.append(f)
                for d in range(2):
                    f = F.take()
                    f.made = act.op(A.activation, f.ap, rr[d].ap, ACT.Tanh,
                                    scale=sml[:, C8F + 10 * d + i:C8F + 10 * d + i + 1],
                                    w=[rr[d].made, c8_m, *f.old])
                    th.append(f)
                for d in range(2):
                    rr[d].made = act.op(A.activation, rr[d].ap, rr[d].ap, ACT.Exp,
                                        scale=sml[:, NC8F + 10 * d + i:NC8F + 10 * d + i + 1],
                                        w=[th[d].made])
                for d in range(2):
                    f = F.take()
                    a = dve.op(V.tensor_scalar, f.ap, th[d].ap, 1.0, None, ALU.add,
                               w=[th[d].made, *f.old])
                    f.made = a
                    q.append(f)
                for d in range(2):
                    q[d].made = dve.op(V.reciprocal, q[d].ap, q[d].ap, w=[q[d].made])
                for d in range(2):
                    ii[d].made = pool.op(P.tensor_tensor, ii[d].ap, ii[d].ap, xa.ap, ALU.mult,
                                         w=[ii[d].made, xa_m])
                    q[d].made = dve.op(V.scalar_tensor_tensor, q[d].ap, th[d].ap, 2.0, q[d].ap,
                                       ALU.mult, ALU.mult, w=[q[d].made])
                    th[d].give(q[d].made)
                xa.give(ii[1].made, p.ready)
                for d in range(2):
                    q[d].made = act.op(A.activation, q[d].ap, q[d].ap, ACT.Sqrt, w=[q[d].made])
                for d in range(2):
                    q[d].made = dve.op(V.tensor_tensor, q[d].ap, q[d].ap, ii[d].ap, ALU.mult,
                                       w=[q[d].made, ii[d].made])
                    ii[d].give(q[d].made)
                m0 = dve.op(V.tensor_tensor_scan, q[0].ap, rr[0].ap, q[0].ap, 0.0, ALU.mult,
                            ALU.add, w=[q[0].made, rr[0].made])
                m1 = dve.op(V.tensor_tensor_scan, q[1].ap[:, ::-1], rr[1].ap[:, ::-1],
                            q[1].ap[:, ::-1], 0.0, ALU.mult, ALU.add, w=[q[1].made, rr[1].made])
                rr[0].give(m0)
                rr[1].give(m1)
                a = dve.op(V.tensor_tensor, q[0].ap, q[0].ap, q[1].ap, ALU.add, w=[m0, m1])
                q[1].give(a)
                hs = split(q[0].ap, a, R)
                q[0].give(hs.ready)
                return hs

            def pool_tile(t):
                w = (2, 4, 8, 16)[t // 2]
                b = group(kblocks("w_in", 10 + t, 8), h)
                i0, i1, i2 = F.take(), F.take(), F.take()
                L = S + w - 1
                f0, f1, f2 = (ft[:, x.i, :] for x in (i0, i1, i2))
                z = dve.op(V.memset, f0, 0.0, w=[*i0.old])
                u = act.op(A.activation, f0[:, w // 2:w // 2 + S], b.ap, ACT.Copy, w=[b.made, z])
                b.give(u)
                prev, n, made, k = f0, L, u, 1
                dst, olds = (f1, f2), (i1.old, i2.old)
                step = 0
                while k < w:
                    n -= k
                    d = dst[step % 2]
                    made = pool.op(P.tensor_tensor, d[:, 0:n], prev[:, 0:n], prev[:, k:k + n],
                                   ALU.add, w=[made, *olds[step % 2]])
                    prev, k, step = d, 2 * k, step + 1
                made = pool.op(P.tensor_tensor, prev[:, 0:S], prev[:, 0:S], inv[:, t // 2, :],
                               ALU.mult, w=[made, (s_inv, 16)])
                d, old = dst[step % 2], olds[step % 2]
                made = pool.op(P.tensor_tensor, d[:, 0:S], prev[:, 0:S],
                               f0[:, w // 2:w // 2 + S], ALU.subtract, w=[made, *old])
                p = split(d[:, 0:S], made, R, eng="dve")
                for x in (i0, i1, i2):
                    x.give(p.ready)
                return p

            def pool_mix(t, pooled):
                g = t // 2
                b = group([("w_pool", 2 * g + k, t) for k in range(2)], pooled[2 * g:2 * g + 2])
                f = F.take()
                a = dve.op(V.tensor_scalar, f.ap, b.ap, vc("b_pool", t), vc("pool_scale", t),
                           ALU.add, ALU.mult, w=[b.made, *f.old])
                b.give(a)
                if t % 2:
                    for x in pooled[2 * g:2 * g + 2]:
                        x.give(b.made)
                p = split(f.ap, a, R, eng="dve")
                f.give(p.ready)
                return p

            def branch_b(m, yb):
                by = group(kblocks("p_b", m, 8), yb)
                bg = group(kblocks("w_in", 26 + m, 8), h)
                f = F.take()
                a = act.op(A.activation, f.ap, bg.ap, ACT.Sigmoid, bias=vc("b_gate", 8 + m),
                           w=[bg.made, *f.old])
                bg.give(a)
                a = dve.op(V.tensor_tensor, xt[:, m, :], by.ap, f.ap, ALU.mult, w=[a, by.made])
                by.give(a)
                f.give(a)
                return a

            hs, pooled, yb, tb = [], [], [], []
            work = []
            for t in range(8):
                work.append(lambda t=t: pooled.append(pool_tile(t)))
            for t in range(8):
                work.append(lambda t=t: yb.append(pool_mix(t, pooled)))
            for m in range(8):
                work.append(lambda m=m: tb.append(branch_b(m, yb)))
            share = [2, 2, 2, 2, 4, 4, 2, 2, 2, 2]
            todo = None
            for i in range(11):
                nxt = lru_in(i) if i < 10 else None
                if i < 10:
                    for _ in range(share[i] // 2):
                        work.pop(0)()
                if todo is not None:
                    hs.append(lru_gates(*todo))
                if i < 10:
                    for _ in range(share[i] - share[i] // 2):
                        work.pop(0)()
                todo = nxt
            while work:
                work.pop(0)()
            for p in yb:
                p.give(pe.now())

            merged = []
            for m in range(8):
                bg = group(kblocks("w_in", 18 + m, 8), h)
                f = F.take()
                a = act.op(A.activation, f.ap, bg.ap, ACT.Sigmoid, bias=vc("b_gate", m),
                           w=[bg.made, *f.old])
                bg.give(a)
                by = group(kblocks("p_a", m, 10), hs)
                a = dve.op(V.tensor_tensor, f.ap, by.ap, f.ap, ALU.mult, w=[a, by.made])
                by.give(a)
                a = dve.op(V.tensor_tensor, f.ap, f.ap, xt[:, m, :], ALU.add, w=[a, tb[m]])
                sp.wait(a)
                nc.sync.dma_start(xt[:, m, :], x_d[m]).then_inc(s_x, 16)
                p = split(f.ap, a, R, eng="dve")
                f.give(p.ready)
                merged.append(p)
            x2 = (s_x, 16 * 16)

            nrm = Norm(F)
            for m in range(8):
                b = group(kblocks("w_out", m, 8), merged)
                x_m[m] = dve.op(V.tensor_tensor, xt[:, m, :], xt[:, m, :], b.ap, ALU.add,
                                w=[b.made, x2])
                b.give(x_m[m])
                nrm.add(xt[:, m, :], x_m[m])
            rs1, rs_m = nrm.rs(1024)
            rs_m = dve.op(V.tensor_copy, keep[:, :], rs1.ap, w=[rs_m])
            end1 = [e.now() for e in (pe, dve, act, pool)]

        def fresh(views, marks):
            s = Slots(views)
            s.free = [(i, list(marks)) for i, _ in s.free]
            return s

        def ffn_down(name, acts, finish):
            for m in range(8):
                b = group(kblocks(name, m, 22), acts)
                finish(m, b)

        with ExitStack() as c2:
            mr = sb("modraw", [128, 2, 1024], ctx=c2)
            rt = sb("r2", [128, 60, S], F32R, ctx=c2)
            ft = sb("f2", [128, 10, S], ctx=c2)
            R = fresh([rt[:, i, :] for i in range(60)], end1)
            F = fresh([ft[:, i, :] for i in range(10)], end1)
            mod_used = {}

            def load_mod(u):
                if u >= 48:
                    return
                act.wait(mod_used[u - 2] if u >= 2 else end1)
                A.dma_start(mr[:, u % 2, :], mod_d[u]).then_inc(s_mod[u % 2], 16)

            def mod_unit(u):
                pe.wait((s_mod[u % 2], 16 * (u // 2 + 1)), cond_m)
                for k in range(8):
                    mm = T.matmul(misc[:, u:u + 1], mr[:, u % 2, 128 * k:128 * k + 128],
                                  sml[:, COND + k:COND + k + 1], start=(k == 0), stop=(k == 7))
                mod_used[u] = pe.mark(mm)
                modplan.append(u)

            load_mod(0)
            load_mod(1)
            h = []
            for m in range(8):
                f = F.take()
                a = dve.op(V.scalar_tensor_tensor, f.ap, xt[:, m, :], vc("g_ffn", m), keep[:, :],
                           ALU.mult, ALU.mult, w=[rs_m, *f.old])
                p = split(f.ap, a, R, eng="dve" if m % 2 else "pool")
                f.give(p.ready)
                h.append(p)

            def up_tile(j):
                b = group(kblocks("w_up", j, 8), h)
                f = F.take()
                a = act.op(A.activation, f.ap, b.ap, ACT.Identity, bias=vc("conv_f_b", j),
                           scale=vc("conv_f_w", 44 + j), w=[b.made, *f.old])
                a = dve.op(V.scalar_tensor_tensor, f.ap[:, 1:S], b.ap[:, 0:S - 1],
                           vc("conv_f_w", j), f.ap[:, 1:S], ALU.mult, ALU.add, w=[a])
                a = dve.op(V.scalar_tensor_tensor, f.ap[:, 0:S - 1], b.ap[:, 1:S],
                           vc("conv_f_w", 88 + j), f.ap[:, 0:S - 1], ALU.mult, ALU.add, w=[a])
                b.give(a)
                f.made = a
                return f

            acts = []
            for j in range(22):
                g = up_tile(j)
                mod_unit(2 * j)
                load_mod(2 * j + 2)
                g.made = act.op(A.activation, g.ap, g.ap, ACT.Gelu_apprx_tanh, w=[g.made])
                v = up_tile(22 + j)
                mod_unit(2 * j + 1)
                load_mod(2 * j + 3)
                a = dve.op(V.tensor_tensor, g.ap, g.ap, v.ap, ALU.mult, w=[g.made, v.made])
                v.give(a)
                p = split(g.ap, a, R, eng="dve" if j % 2 else "pool")
                g.give(p.ready)
                acts.append(p)
            for u in range(44, 48):
                mod_unit(u)
                load_mod(u + 2)
            mod_m = dve.op(V.tensor_tensor, sml[:, MOD:MOD + 48], misc[:, 0:48],
                           vc("b_mod_2", 0, 48), ALU.add, w=[mod_used[47]])

            nrm = Norm(F)

            def add_x(m, b):
                x_m[m] = dve.op(V.tensor_tensor, xt[:, m, :], xt[:, m, :], b.ap, ALU.add,
                                w=[b.made, x_m[m]])
                b.give(x_m[m])
                nrm.add(xt[:, m, :], x_m[m])

            ffn_down("w_down", acts, add_x)
            rs1, rs_m = nrm.rs(1024)
            nrm = Norm(F)
            for m in range(8):
                x_m[m] = dve.op(V.scalar_tensor_tensor, xt[:, m, :], xt[:, m, :],
                                vc("g_final", m), rs1.ap, ALU.mult, ALU.mult, w=[rs_m, x_m[m]])
                nrm.add(xt[:, m, :], x_m[m])
            rs1, rs_m = nrm.rs(1024)
            rs_m = dve.op(V.tensor_copy, keep[:, :], rs1.ap, w=[rs_m])
            end2 = [e.now() for e in (pe, dve, act, pool)]

        gs_m = dve.op(V.scalar_tensor_tensor, sml[:, GS1:GS1 + 8], sml[:, MOD + 8:MOD + 16], 1.0,
                      vc("norm1_g_2", 0, 8), ALU.add, ALU.mult, w=[mod_m])
        gs2_m = dve.op(V.scalar_tensor_tensor, sml[:, GS2:GS2 + 8], sml[:, MOD + 32:MOD + 40],
                       1.0, vc("norm2_g_2", 0, 8), ALU.add, ALU.mult, w=[mod_m])

        def modulated(R, F, gs, shift, rsap, marks):
            out = []
            for m in range(8):
                f = F.take()
                a = dve.op(V.scalar_tensor_tensor, f.ap, xt[:, m, :], sml[:, gs + m:gs + m + 1],
                           rsap, ALU.mult, ALU.mult, w=[*marks, x_m[m], *f.old])
                p = take_pair(R)
                sh = sml[:, MOD + shift + m:MOD + shift + m + 1]
                b = act.op(A.activation, p.hi.ap, f.ap, ACT.Identity, bias=sh,
                           w=[a, *p.hi.old])
                p.ready = dve.op(V.scalar_tensor_tensor, p.lo.ap, f.ap, sh,
                                 p.hi.ap.bitcast(F32), ALU.add, ALU.subtract, w=[b, *p.lo.old])
                f.give(p.ready)
                out.append(p)
            return out

        with ExitStack() as c3:
            rt = sb("r3", [128, 32, S], F32R, ctx=c3)
            R = fresh([rt[:, i, :] for i in range(32)], end2)
            c4 = c3.enter_context(ExitStack())
            ssm = sb("ssm", [128, 4, 16, 32], ctx=c4)
            uk = sb("uk", [128, 2, 512], ctx=c4)
            tab = sb("tab", [128, 2, 16, 32], ctx=c4)
            bt = sb("bt", [128, 2, 4, 128], ctx=c4)
            masks = sb("masks", [128, 1280], ctx=c4)
            pt = sb("pt", [128, 4, S], ctx=c4)
            NF = 24
            ft = sb("f3", [128, NF, S], ctx=c4)
            F = fresh([ft[:, i, :] for i in range(NF)], end2)
            sp.wait(*end2)
            nc.sync.dma_start(ssm[:, :, :, :], ssm_d).then_inc(s_ssm, 16)
            nc.sync.dma_start(uk[:, :, :], uk_d).then_inc(s_ssm, 16)
            ssm_in = (s_ssm, 32)
            for e in (dve, act, pool, pe):
                e.wait(*end2)

            u = modulated(R, F, GS1, 0, keep[:, :], [rs_m, gs_m])

            def cols(k):
                return sml[:, 300 + 16 * k:316 + 16 * k]

            are, aim = vc("ssm_a_re_2", 0, 16), vc("ssm_a_im_2", 0, 16)
            mag = sml[:, 460:476]
            cre, cim = sml[:, 476:492], sml[:, 492:508]
            d = dve.op
            TT, TS, STT = V.tensor_tensor, V.tensor_scalar, V.scalar_tensor_tensor
            dt, ang, k_, r_ = cols(0), cols(1), cols(2), cols(3)
            m = act.op(A.activation, dt, vc("ssm_log_dt_2", 0, 16), ACT.Exp, w=[c8_m])
            m = d(TT, ang, are, dt, ALU.mult, w=[m])
            mg = act.op(A.activation, mag, ang, ACT.Exp, w=[m])
            m = d(TT, ang, aim, dt, ALU.mult, w=[mg])
            magic = 12582912.0
            m = d(TS, k_, ang, float(1.0 / (2 * np.pi)), magic, ALU.mult, ALU.add, w=[m])
            m = d(TS, k_, k_, -magic, None, ALU.add, w=[m])
            P1 = 6.28125
            P2 = float(np.float32(2 * np.pi - P1))
            P2 = float(np.frombuffer(np.uint32(np.frombuffer(np.float32(P2).tobytes(), np.uint32)[0]
                                               & 0xFFFFE000).tobytes(), np.float32)[0])
            P3 = float(2 * np.pi - P1 - P2)
            m = d(STT, r_, k_, -P1, ang, ALU.mult, ALU.add, w=[m])
            m = d(STT, r_, k_, -P2, r_, ALU.mult, ALU.add, w=[m])
            m = d(STT, r_, k_, -P3, r_, ALU.mult, ALU.add, w=[m])
            PI = 3.1415925
            m = d(TS, r_, r_, PI, -PI, ALU.min, ALU.max, w=[m])
            m = d(TS, k_, r_, -1.0, None, ALU.mult, w=[m])
            m = d(TT, k_, k_, r_, ALU.min, w=[m])
            m = d(TS, k_, k_, float(np.pi / 2), None, ALU.add, w=[m])
            pc = [sml[:, PW + 16 * l:PW + 16 * l + 16] for l in range(9)]
            ps = [sb(f"ps_{l}", [128, 16], ctx=c4)[:, :] for l in range(9)]
            s1 = act.op(A.activation, ps[0], r_, ACT.Sin, w=[m])
            s2 = act.op(A.activation, pc[0], k_, ACT.Sin, w=[m])
            lre, lim, den, ta, tb_ = cols(4), cols(5), cols(6), cols(7), cols(8)
            m = d(TT, lre, mag, pc[0], ALU.mult, w=[s1, s2, mg])
            m = d(TT, lim, mag, ps[0], ALU.mult, w=[m])
            m = d(TS, lre, lre, -1.0, None, ALU.add, w=[m])
            m = d(TT, den, are, are, ALU.mult, w=[m])
            m = d(TT, ta, aim, aim, ALU.mult, w=[m])
            m = d(TT, den, den, ta, ALU.add, w=[m])
            m = d(V.reciprocal, den, den, w=[m])
            m = d(TT, ta, lre, are, ALU.mult, w=[m])
            m = d(TT, tb_, lim, aim, ALU.mult, w=[m])
            m = d(TT, ta, ta, tb_, ALU.add, w=[m])
            m = d(TT, cre, ta, den, ALU.mult, w=[m])
            m = d(TT, ta, lim, are, ALU.mult, w=[m])
            m = d(TT, tb_, lre, aim, ALU.mult, w=[m])
            m = d(TT, ta, ta, tb_, ALU.subtract, w=[m])
            m = d(TT, cim, ta, den, ALU.mult, w=[m])
            for l in range(8):
                m = d(TT, ta, pc[l], pc[l], ALU.mult, w=[m])
                m = d(TT, tb_, ps[l], ps[l], ALU.mult, w=[m])
                m = d(TT, pc[l + 1], ta, tb_, ALU.subtract, w=[m])
                m = d(STT, ps[l + 1], pc[l], 2.0, ps[l], ALU.mult, ALU.mult, w=[m])

            def bc(ap, n):
                return ap.unsqueeze(2).broadcast_to([128, 16, n])

            ctab, stab = tab[:, 0], tab[:, 1]
            m = d(V.memset, ctab[:, :, 0:1], 1.0, w=[m])
            m = d(V.memset, stab[:, :, 0:1], 0.0, w=[m])
            tf = F.take()
            tv = tf.ap.rearrange("p (s n) -> p s n", s=16)
            m = d(TT, tv[:, :, 0:1], ctab[:, :, 0:1], ctab[:, :, 0:1], ALU.mult, w=[m, *tf.old])
            for l in range(5):
                n = 1 << l
                lo_, hi_ = slice(0, n), slice(n, 2 * n)
                q1, q2 = tv[:, :, 0:n], tv[:, :, 16:16 + n]
                m = d(TT, ctab[:, :, hi_], ctab[:, :, lo_], bc(pc[l], n), ALU.mult, w=[m])
                m = d(TT, q1, stab[:, :, lo_], bc(ps[l], n), ALU.mult, w=[m])
                m = d(TT, ctab[:, :, hi_], ctab[:, :, hi_], q1, ALU.subtract, w=[m])
                m = d(TT, stab[:, :, hi_], stab[:, :, lo_], bc(pc[l], n), ALU.mult, w=[m])
                m = d(TT, q2, ctab[:, :, lo_], bc(ps[l], n), ALU.mult, w=[m])
                m = d(TT, stab[:, :, hi_], stab[:, :, hi_], q2, ALU.add, w=[m])
            t2f = F.take()
            t2v = t2f.ap.rearrange("p (s n) -> p s n", s=16)
            bre, bim = ssm[:, 0], ssm[:, 1]
            m = d(TT, tv, bre, bc(cim, 32), ALU.mult, w=[m, ssm_in])
            m = d(TT, t2v, bim, bc(cim, 32), ALU.mult, w=[m, *t2f.old])
            m = d(TT, bre, bre, bc(cre, 32), ALU.mult, w=[m])
            m = d(TT, bim, bim, bc(cre, 32), ALU.mult, w=[m])
            m = d(TT, bre, bre, t2v, ALU.subtract, w=[m])
            m = d(TT, bim, bim, tv, ALU.add, w=[m])
            m = d(TS, ssm[:, 3], ssm[:, 3], -1.0, None, ALU.mult, w=[m])
            tf.give(m)
            t2f.give(m)
            for c in range(2):
                b = banks.take()
                pe.wait(*b.old, m)
                for j in range(4):
                    mm = T.transpose(b.ap[:, 128 * j:128 * j + 128], ssm[:, c, 4 * j:4 * j + 4, :]
                                     .rearrange("p s n -> p (s n)"), ident)
                bt_m = act.op(A.activation, bt[:, c].rearrange("p j n -> p (j n)"), b.ap, ACT.Copy,
                              w=[pe.mark(mm)])
                b.give(bt_m)
            s5_m = m

            xs = []
            for j in range(4):
                b = group(kblocks("w_in_2", j, 8), u)
                f = F.take()
                f.made = act.op(A.activation, f.ap, b.ap, ACT.Copy, w=[b.made, *f.old])
                b.give(f.made)
                xs.append(f)
            ys = []

            def s5():
                pend = []

                def finish(j):
                    yb_ = pend.pop(0)
                    a = dve.op(STT, xs[j].ap, xs[j].ap, vc("ssm_d_2", j), yb_.ap, ALU.mult,
                               ALU.add, w=[yb_.made, xs[j].made])
                    yb_.give(a)
                    a = act.op(A.activation, xs[j].ap, xs[j].ap, ACT.Gelu_apprx_tanh, w=[a])
                    p = split(xs[j].ap, a, R)
                    xs[j].give(p.ready)
                    ys.append(p)

                ybank = None
                for s in range(16):
                    j, i = divmod(s, 4)
                    rows = slice(32 * i, 32 * i + 32)
                    bb = []
                    for c in range(2):
                        b = banks.take()
                        pe.wait(*b.old, xs[j].made, bt_m)
                        b.made = pe.mark(T.matmul(b.ap, bt[rows, c, j, :], xs[j].ap[rows],
                                                  start=True, stop=True))
                        bb.append(b)
                    tc, ts = F.take(), F.take()
                    a = act.op(A.activation, tc.ap[:, 0:32], ctab[:, s], ACT.Copy,
                               w=[s5_m, *tc.old])
                    b2 = act.op(A.activation, ts.ap[:, 0:32], stab[:, s], ACT.Copy,
                                w=[s5_m, *ts.old])
                    q1, q2 = F.take(), F.take()
                    wq = [*q1.old, *q2.old]
                    ma = mb = None
                    for l in range(5, 9):
                        n = 1 << l
                        lo_, hi_ = slice(0, n), slice(n, 2 * n)
                        pcl, psl = pc[l][:, s:s + 1], ps[l][:, s:s + 1]
                        m1 = d(TS, q1.ap[:, lo_], ts.ap[:, lo_], psl, None, ALU.mult,
                               w=[a, b2, *wq])
                        m2 = d(TS, q2.ap[:, lo_], tc.ap[:, lo_], psl, None, ALU.mult, w=[])
                        wq = []
                        a = d(STT, tc.ap[:, hi_], tc.ap[:, lo_], pcl, q1.ap[:, lo_], ALU.mult,
                              ALU.subtract, w=[m1])
                        b2 = d(STT, ts.ap[:, hi_], ts.ap[:, lo_], pcl, q2.ap[:, lo_], ALU.mult,
                               ALU.add, w=[m2])
                    q3, q4 = F.take(), F.take()
                    a1 = d(TT, q1.ap, bb[0].ap, tc.ap, ALU.mult, w=[bb[0].made, a, b2])
                    a2 = d(TT, q2.ap, bb[1].ap, ts.ap, ALU.mult, w=[bb[1].made])
                    a3 = d(TT, q3.ap, bb[1].ap, tc.ap, ALU.mult, w=[*q3.old])
                    a4 = d(TT, q4.ap, bb[0].ap, ts.ap, ALU.mult, w=[*q4.old])
                    bb[0].give(a4)
                    bb[1].give(a3)
                    b1 = pool.op(P.tensor_tensor, q1.ap, q1.ap, q2.ap, ALU.add, w=[a1, a2])
                    b3 = pool.op(P.tensor_tensor, q3.ap, q3.ap, q4.ap, ALU.subtract, w=[a3, a4])
                    yield
                    mg_b = mag[:, s:s + 1].broadcast_to([128, S])
                    z1 = d(V.tensor_tensor_scan, q1.ap, mg_b, q1.ap, 0.0, ALU.mult, ALU.add,
                           w=[b1])
                    z2 = d(V.tensor_tensor_scan, q3.ap, mg_b, q3.ap, 0.0, ALU.mult, ALU.add,
                           w=[b3])
                    a2 = d(TT, q2.ap, ts.ap, q3.ap, ALU.mult, w=[z2])
                    a4 = d(TT, q4.ap, ts.ap, q1.ap, ALU.mult, w=[z1])
                    a1 = d(TT, q1.ap, tc.ap, q1.ap, ALU.mult, w=[a4])
                    a3 = d(TT, q3.ap, tc.ap, q3.ap, ALU.mult, w=[a2])
                    tc.give(a3)
                    ts.give(a4)
                    b1 = pool.op(P.tensor_tensor, q1.ap, q1.ap, q2.ap, ALU.subtract, w=[a1, a2])
                    b3 = pool.op(P.tensor_tensor, q3.ap, q3.ap, q4.ap, ALU.add, w=[a3, a4])
                    q2.give(b1)
                    q4.give(b3)
                    yield
                    if i == 0:
                        ybank = banks.take()
                        pe.wait(*ybank.old)
                    pe.wait(b1, b3)
                    T.matmul(ybank.ap[rows], ssm[:, 2, s, :], q1.ap, start=True, stop=False,
                             tile_position=(0, 32 * i))
                    ybank.made = pe.mark(T.matmul(ybank.ap[rows], ssm[:, 3, s, :], q3.ap,
                                                  start=False, stop=True,
                                                  tile_position=(0, 32 * i)))
                    q1.give(ybank.made)
                    q3.give(ybank.made)
                    if i == 3:
                        pend.append(ybank)
                        finish(j)
                    yield

            att = []

            def dsa():
                qt = []
                for j in range(4):
                    b = group(kblocks("w_in_2", 4 + j, 8), u)
                    f = F.take()
                    f.made = act.op(A.activation, f.ap, b.ap, ACT.Copy, scale=0.125,
                                    w=[b.made, *f.old])
                    b.give(f.made)
                    qt.append(f)
                    yield
                b = group(kblocks("w_in_2", 8, 8), u)
                ck = F.take()
                m = act.op(A.activation, ck.ap, b.ap, ACT.Copy, w=[b.made, *ck.old])
                b.give(m)
                n1 = Norm(F)
                n1.add(ck.ap, m)
                qi = []
                for j in range(2):
                    b = group(kblocks("w_in_2", 9 + j, 8), u)
                    f = F.take()
                    f.made = act.op(A.activation, f.ap, b.ap, ACT.Copy, scale=0.125,
                                    w=[b.made, *f.old])
                    b.give(f.made)
                    qi.append(f)
                r, rm = n1.rs(128)
                ck_m = dve.op(STT, ck.ap, ck.ap, vc("kv_norm_g_2"), r.ap, ALU.mult, ALU.mult,
                              w=[rm])
                r.give(ck_m)
                yield
                b = group(kblocks("w_in_2", 11, 8), u)
                kw = F.take()
                m = act.op(A.activation, kw.ap, b.ap, ACT.Copy, w=[b.made, *kw.old])
                b.give(m)
                n2 = Norm(F)
                n2.add(kw.ap, m)
                b = banks.take()
                pe.wait(*b.old, m)
                for t in range(4):
                    mm = T.transpose(b.ap[:, 128 * t:128 * t + 128],
                                     kw.ap[:, 128 * t:128 * t + 128], ident)
                mm = pe.mark(mm)
                wi = sml[:, TMPV:TMPV + 16].rearrange("p (t n) -> p t n", t=4)
                wi_m = act.op(A.activation, wi, b.ap.rearrange("p (t n) -> p t n", t=4)
                              [:, :, 64:68], ACT.Copy, scale=0.5, w=[mm])
                b.give(wi_m)
                r, rm = n2.rs(64, rows=64)
                ki_m = dve.op(STT, kw.ap[0:64], kw.ap[0:64], vc("idx_k_norm_g_2")[0:64],
                              r.ap[0:64], ALU.mult, ALU.mult, w=[rm, mm])
                r.give(ki_m)
                sp.wait(ki_m, wi_m, mm)
                nc.sync.dma_start(kw.ap[64:128], kw.ap[0:64]).then_inc(s_ki, 16)
                ki_m = (s_ki, 16)
                b = banks.take()
                pe.wait(*b.old, ck_m)
                for t in range(4):
                    mm = T.transpose(b.ap[:, 128 * t:128 * t + 128],
                                     ck.ap[:, 128 * t:128 * t + 128], ident)
                nat = F.take()
                nat_m = act.op(A.activation, nat.ap, b.ap, ACT.Copy, w=[pe.mark(mm), *nat.old])
                b.give(nat_m)
                yield
                moff = [0, 128, 384, 768]
                mk_m = [dve.op(TS, masks[:, 0:128], tri, 3.3e-9, None, ALU.mult)]
                for t in range(1, 4):
                    kmax = 128 * (t + 1)
                    sc, wk, e1 = F.take(), F.take(), F.take()
                    am = None
                    for hh in range(4):
                        rows = slice(64 * (hh % 2), 64 * (hh % 2) + 64)
                        b = banks.take()
                        pe.wait(*b.old, qi[hh // 2].made, ki_m)
                        mm = pe.mark(T.matmul(b.ap[:, 0:kmax], qi[hh // 2].ap[rows,
                                              128 * t:128 * t + 128], kw.ap[rows, 0:kmax],
                                              start=True, stop=True))
                        wcol = sml[:, TMPV + 4 * t + hh:TMPV + 4 * t + hh + 1]
                        if hh == 0:
                            am = dve.op(TS, sc.ap[:, 0:kmax], b.ap[:, 0:kmax], 0.0, wcol,
                                        ALU.max, ALU.mult, w=[mm, wi_m, *sc.old])
                            b.give(am)
                        else:
                            f = F.take()
                            rm = act.op(A.activation, f.ap[:, 0:kmax], b.ap[:, 0:kmax], ACT.Relu,
                                        w=[mm, *f.old])
                            b.give(rm)
                            am = dve.op(STT, sc.ap[:, 0:kmax], f.ap[:, 0:kmax], wcol,
                                        sc.ap[:, 0:kmax], ALU.mult, ALU.add, w=[rm, am])
                            f.give(am)
                    am = dve.op(TT, sc.ap[:, kmax - 128:kmax], sc.ap[:, kmax - 128:kmax], tri,
                                ALU.add, w=[am])
                    cur = sc.ap[:, 0:kmax]
                    m8 = sml[:, M8:M8 + 8]
                    for rnd in range(16):
                        am = dve.op(V.max, m8, cur, w=[am, *(wk.old if rnd == 0 else [])])
                        if rnd < 15:
                            am = dve.op(V.match_replace, wk.ap[:, 0:kmax], m8, cur, -3.4e38,
                                        w=[am])
                            cur = wk.ap[:, 0:kmax]
                        if rnd % 4 == 3:
                            yield
                    thr = m8[:, 7:8]
                    o = moff[t]
                    mk = masks[:, o:o + kmax]
                    need = sml[:, MX:MX + 1]
                    am = dve.op(TS, mk, sc.ap[:, 0:kmax], thr, None, ALU.is_gt, ALU.add,
                                accum_out=need, w=[am])
                    em = dve.op(TS, e1.ap[:, 0:kmax], sc.ap[:, 0:kmax], thr, None, ALU.is_equal,
                                w=[*e1.old])
                    am = dve.op(TS, need, need, -1.0, 128.0, ALU.mult, ALU.add, w=[am])
                    em = dve.op(V.tensor_tensor_scan, wk.ap[:, 0:kmax], e1.ap[:, 0:kmax],
                                e1.ap[:, 0:kmax], 0.0, ALU.add, ALU.max, w=[em])
                    em = dve.op(STT, e1.ap[:, 0:kmax], wk.ap[:, 0:kmax], need, e1.ap[:, 0:kmax],
                                ALU.is_le, ALU.mult, w=[em, am])
                    em = dve.op(TT, mk, mk, e1.ap[:, 0:kmax], ALU.add, w=[em])
                    em = dve.op(TS, mk, mk, -1.0, BIG, ALU.add, ALU.mult, w=[em])
                    mk_m.append(em)
                    for f in (sc, wk, e1):
                        f.give(em)
                    yield
                for f in qi:
                    f.give(pe.now())
                kw.give(pe.now())
                pt_free = None
                abank = None
                for hh in range(8):
                    rows = slice(64 * (hh % 2), 64 * (hh % 2) + 64)
                    b = banks.take()
                    pe.wait(*b.old, qt[hh // 2].made, ssm_in)
                    mm = pe.mark(T.matmul(b.ap, uk[rows, 0, 128 * (hh // 2):128 * (hh // 2) + 128],
                                          qt[hh // 2].ap[rows], start=True, stop=True))
                    ql = F.take()
                    qm = act.op(A.activation, ql.ap, b.ap, ACT.Copy, w=[mm, *ql.old])
                    b.give(qm)
                    if hh % 2:
                        qt[hh // 2].give(mm)
                    pv_w = []
                    for t in range(4):
                        kmax = 128 * (t + 1)
                        b = banks.take()
                        pe.wait(*b.old, qm, ck_m)
                        mm = pe.mark(T.matmul(b.ap[:, 0:kmax], ql.ap[:, 128 * t:128 * t + 128],
                                              ck.ap[:, 0:kmax], start=True, stop=True))
                        f = F.take()
                        mx, nm, rsm = (sml[:, c + t:c + t + 1] for c in (MX, NMX, RSUM))
                        a = dve.op(V.tensor_tensor_reduce, f.ap[:, 0:kmax], b.ap[:, 0:kmax],
                                   masks[:, moff[t]:moff[t] + kmax], 1.0, NEG, ALU.add, ALU.max,
                                   mx, w=[mm, mk_m[t], *f.old, act.now(), dve.now()])
                        b.give(a)
                        a = dve.op(TS, nm, mx, -1.0, None, ALU.mult, w=[a])
                        a = act.op(A.activation, f.ap[:, 0:kmax], f.ap[:, 0:kmax], ACT.Exp,
                                   bias=nm, accum_out=rsm, w=[a])
                        a = dve.op(V.reciprocal, rsm, rsm, w=[a])
                        a = dve.op(TS, f.ap[:, 0:kmax], f.ap[:, 0:kmax], rsm, None, ALU.mult,
                                   w=[a])
                        b = banks.take()
                        pe.wait(*b.old, a)
                        for k in range(t + 1):
                            mm = T.transpose(b.ap[:, 128 * k:128 * k + 128],
                                             f.ap[:, 128 * k:128 * k + 128], ident)
                        mm = pe.mark(mm)
                        f.give(mm)
                        a = act.op(A.activation, pt[:, 0:t + 1, 128 * t:128 * t + 128],
                                   b.ap[:, 0:kmax].rearrange("p (k n) -> p k n", n=128), ACT.Copy,
                                   w=[mm, pt_free])
                        b.give(a)
                        pv_w.append(a)
                        if t % 2:
                            yield
                    ql.give(pe.now())
                    b = banks.take()
                    pe.wait(*b.old, *pv_w, nat_m)
                    for k in range(4):
                        mm = T.matmul(b.ap[:, 128 * k:S], nat.ap[:, 128 * k:128 * k + 128],
                                      pt[:, k, 128 * k:S], start=(k == 0), stop=(k == 3))
                    mm = pe.mark(mm)
                    pt_free = mm
                    o_ = F.take()
                    om = act.op(A.activation, o_.ap, b.ap, ACT.Copy, w=[mm, *o_.old])
                    b.give(om)
                    if hh % 2 == 0:
                        abank = banks.take()
                        pe.wait(*abank.old)
                    pe.wait(om)
                    mm = pe.mark(T.matmul(abank.ap[rows], uk[:, 1, 64 * hh:64 * hh + 64], o_.ap,
                                          start=True, stop=True,
                                          tile_position=(0, 64 * (hh % 2))))
                    o_.give(mm)
                    if hh % 2:
                        p = take_pair(R)
                        a = act.op(A.activation, p.hi.ap, abank.ap, ACT.Copy,
                                   w=[mm, *p.hi.old])
                        p.ready = dve.op(TT, p.lo.ap, abank.ap, p.hi.ap.bitcast(F32),
                                         ALU.subtract, w=[a, *p.lo.old])
                        abank.give(p.ready)
                        att.append(p)
                    yield

            runs = [dsa(), s5()]
            while runs:
                for g in list(runs):
                    done = False
                    try:
                        next(g)
                    except StopIteration:
                        done = True
                    if done:
                        runs.remove(g)
            end3 = [e.now() for e in (pe, dve, act, pool)]
            c4.close()

            r4 = sb("r4", [128, 16, S], F32R, ctx=c3)
            f4 = sb("f4", [128, 12, S], ctx=c3)
            R2 = fresh([r4[:, i, :] for i in range(16)], end3)
            F = fresh([f4[:, i, :] for i in range(12)], end3)
            merged = []
            for m in range(8):
                def gate(name, mt, nk, src, bias):
                    b = group(kblocks(name, mt, nk), src)
                    f = F.take()
                    a = act.op(A.activation, f.ap, b.ap, ACT.Sigmoid, bias=bias,
                               w=[b.made, *f.old])
                    b.give(a)
                    return f, a
                zero = 0.0
                f1, a1 = gate("w_ssm_glu_2", 8 + m, 4, ys, vc("b_ssm_glu_2", 8 + m))
                bv = group(kblocks("w_ssm_glu_2", m, 4), ys)
                a1 = dve.op(STT, f1.ap, bv.ap, vc("b_ssm_glu_2", m), f1.ap, ALU.add, ALU.mult,
                            w=[a1, bv.made])
                bv.give(a1)
                f2, a2 = gate("w_in_2", 12 + m, 8, u, zero)
                a1 = dve.op(TT, f1.ap, f1.ap, f2.ap, ALU.mult, w=[a1, a2])
                f2.give(a1)
                f3, a3 = gate("w_in_2", 20 + m, 8, u, zero)
                ba = group(kblocks("w_attn_proj_2", m, 4), att)
                a3 = dve.op(TT, f3.ap, ba.ap, f3.ap, ALU.mult, w=[a3, ba.made])
                ba.give(a3)
                a = dve.op(TT, f1.ap, f1.ap, f3.ap, ALU.add, w=[a1, a3])
                f3.give(a)
                p = split(f1.ap, a, R2, eng="dve")
                f1.give(p.ready)
                merged.append(p)
            nrm = Norm(F)

            def gated_add(gcol, m, b):
                x_m[m] = dve.op(STT, xt[:, m, :], b.ap, sml[:, MOD + gcol + m:MOD + gcol + m + 1],
                                xt[:, m, :], ALU.mult, ALU.add, w=[b.made, x_m[m], mod_m])
                b.give(x_m[m])
                nrm.add(xt[:, m, :], x_m[m])

            for m in range(8):
                gated_add(16, m, group(kblocks("w_out_2", m, 8), merged))
            rs1, rs_m = nrm.rs(1024)
            rs_m = dve.op(V.tensor_copy, keep[:, :], rs1.ap, w=[rs_m])
            end4 = [e.now() for e in (pe, dve, act, pool)]

        with ExitStack() as c5:
            rt = sb("r5", [128, 60, S], F32R, ctx=c5)
            ft = sb("f5", [128, 12, S], ctx=c5)
            R = fresh([rt[:, i, :] for i in range(60)], end4)
            F = fresh([ft[:, i, :] for i in range(12)], end4)
            h = modulated(R, F, GS2, 24, keep[:, :], [rs_m, gs2_m])
            acts = []
            for j in range(22):
                b = group(kblocks("w_ffn_gate_2", j, 8), h)
                f = F.take()
                a = act.op(A.activation, f.ap, b.ap, ACT.Silu, w=[b.made, *f.old])
                b.give(a)
                b = group(kblocks("w_ffn_up_2", j, 8), h)
                a = dve.op(TT, f.ap, b.ap, f.ap, ALU.mult, w=[a, b.made])
                b.give(a)
                p = split(f.ap, a, R, eng="dve")
                f.give(p.ready)
                acts.append(p)
            nrm = Norm(F)
            ffn_down("w_ffn_down_2", acts, lambda m, b: gated_add(40, m, b))
            rs1, rs_m = nrm.rs(1024)
            for m in range(8):
                a = dve.op(STT, xt[:, m, :], xt[:, m, :], vc("final_g_2", m), rs1.ap, ALU.mult,
                           ALU.mult, w=[rs_m, x_m[m]])
                sp.wait(a)
                nc.sync.dma_start(out_d[m], xt[:, m, :]).then_inc(s_out, 16)
            nc.sync.wait_ge(s_out, 16 * 8)
        assert len(plan) == NBLK, len(plan)


def lay_out(inputs, plan):
    f = {k: np.asarray(v) for k, v in inputs.items()}
    one = {k: v[0] for k, v in f.items() if k not in ("x", "g_final", "final_g_2", "c_2")}

    ki = np.zeros((1024, 3584), np.float32)
    w = one["w_in_2"]
    ki[:, 0:1408] = w[:, 0:1408]
    ki[:, 1408:1476] = w[:, 1408:1476]
    ki[:, 1536:3584] = w[:, 1476:3524]
    mats = {n: one[n] for n in ("w_in", "p_a", "p_b", "w_out", "w_up", "w_down", "w_ssm_glu_2",
                                "w_attn_proj_2", "w_out_2", "w_ffn_gate_2", "w_ffn_up_2",
                                "w_ffn_down_2")}
    mats["w_in_2"] = ki
    stream = np.zeros((NUNIT, 128, UB * 128), np.float32)
    for n, (name, k, m) in enumerate(plan):
        u, j = divmod(n, UB)
        if name in ("wa_f", "wx_f", "wa_b", "wx_b"):
            blk = one[name][k]
        elif name == "w_pool":
            blk = one[name][k // 2, 128 * (k % 2):128 * (k % 2) + 128,
                            128 * (m % 2):128 * (m % 2) + 128]
        else:
            blk = mats[name][128 * k:128 * k + 128, 128 * m:128 * m + 128]
        stream[u, :, 128 * j:128 * j + 128] = blk

    vec = np.zeros((128, NV), np.float32)

    def put(name, a):
        a = np.asarray(a).reshape(-1, 128).T
        vec[:, VOFF[name]:VOFF[name] + a.shape[1]] = a

    for name, n in VECS:
        if name == "ssm_log_dt_2":
            put(name, np.repeat(one[name], 64))
        elif name == "idx_k_norm_g_2":
            vec[0:64, VOFF[name]] = one[name]
        elif name in ("g_final", "final_g_2", "c_2"):
            put(name, f[name])
        else:
            put(name, one[name])

    cst = np.zeros((2, 128, 128), np.float32)
    cst[0] = np.eye(128)
    cst[1] = np.where(np.arange(128)[None, :] <= np.arange(128)[:, None], 0.0, NEG)
    t = np.arange(S)
    inv = np.zeros((128, 4, S), np.float32)
    for g, wd in enumerate((2, 4, 8, 16)):
        lo = np.clip(t - wd // 2, 0, S - 1)
        hi = np.clip(t + wd // 2 - 1, 0, S - 1)
        inv[:, g, :] = (1.0 / (hi - lo + 1)).astype(np.float32)

    ssm = np.zeros((128, 4, 16, 32), np.float32)
    for c, name in enumerate(("ssm_b_re_2", "ssm_b_im_2", "ssm_c_re_2", "ssm_c_im_2")):
        a = one[name] if c < 2 else one[name].transpose(0, 2, 1)
        a = a.reshape(16, 2, 64, 16)
        for g in range(2):
            ssm[64 * g:64 * g + 64, c, :, 16 * g:16 * g + 16] = a[:, g].transpose(1, 0, 2)
    uk = np.zeros((128, 2, 512), np.float32)
    uk[:, 0, :] = one["w_uk_2"].transpose(1, 2, 0).reshape(4, 128, 128).transpose(1, 0, 2)\
        .reshape(128, 512)
    uk[:, 1, :] = one["w_uv_2"].reshape(128, 512)
    mod = one["w_mod_2"].reshape(8, 128, 48, 128).transpose(2, 1, 0, 3).reshape(48, 128, 1024)
    x = f["x"][0].T.reshape(8, 128, S)
    arrays = {"x": x, "w": stream, "mod": mod, "vec": vec, "cst": cst, "inv": inv, "ssm": ssm,
              "uk": uk}
    return {k: np.ascontiguousarray(a) for k, a in arrays.items()}


SHAPES = {"x": (8, 128, S), "w": (NUNIT, 128, UB * 128), "mod": (48, 128, 1024),
          "vec": (128, NV), "cst": (2, 128, 128), "inv": (128, 4, S), "ssm": (128, 4, 16, 32),
          "uk": (128, 2, 512)}


def program(nc):
    aps = [nc.dram_tensor(f"in_{n}", s, F32, kind="ExternalInput").ap() for n, s in SHAPES.items()]
    out = nc.dram_tensor("out_t", (8, 128, S), F32, kind="ExternalOutput").ap()
    plan, modplan = [], []
    build(nc, *aps, out, plan, modplan)
    return plan


def kernel(**inputs):
    from concourse import bacc
    from concourse.bass_utils import run_bass_kernel_spmd

    nc = bacc.Bacc("TRN2", target_bir_lowering=False, num_devices=1)
    plan = program(nc)
    arrays = {f"in_{k}": v for k, v in lay_out(inputs, plan).items()}
    r = run_bass_kernel_spmd(nc, [arrays], core_ids=[0])
    y = r.results[0]["out_t"]
    return np.ascontiguousarray(np.asarray(y).reshape(1024, S).T)[None]
```

```python
from contextlib import ExitStack

import numpy as np

import concourse.bass as bass
from concourse import mybir

F32 = mybir.dt.float32
F32R = mybir.dt.float32r
ALU = mybir.AluOpType
ACT = mybir.ActivationFunctionType
AX_X = mybir.AxisListType.X

S = 512
UB = 8
NRAW = 3
NHL = 3
LOOK = 2
NBLK = 1976
NUNIT = NBLK // UB
EPS = 1e-6
NEG = -3.0e38
BIG = 1.0e30

VECS = [
    ("g_mix", 8), ("b_gate", 16), ("conv_a_w", 40), ("conv_a_b", 10),
    ("ba_f", 10), ("bx_f", 10), ("ba_b", 10), ("bx_b", 10), ("lam_f", 10), ("lam_b", 10),
    ("b_pool", 8), ("pool_scale", 8), ("g_ffn", 8), ("conv_f_w", 132), ("conv_f_b", 44),
    ("g_final", 8), ("c_2", 8), ("b_mod_2", 48), ("norm1_g_2", 8), ("ssm_a_re_2", 16),
    ("ssm_a_im_2", 16), ("ssm_log_dt_2", 16), ("ssm_d_2", 4), ("b_ssm_glu_2", 16),
    ("kv_norm_g_2", 1), ("idx_k_norm_g_2", 1), ("norm2_g_2", 8), ("final_g_2", 8),
]
VOFF = {}
NV = 0
for _n, _c in VECS:
    VOFF[_n] = NV
    NV += _c


class Engine:

    def __init__(self, eng, sem):
        self.eng, self.sem, self.n, self.seen = eng, sem, 0, {}

    def wait(self, *marks):
        for m in marks:
            if m is None:
                continue
            if isinstance(m, list):
                self.wait(*m)
                continue
            sem, value = m
            if self.seen.get(id(sem), 0) < value:
                self.seen[id(sem)] = value
                self.eng.wait_ge(sem, value)

    def mark(self, ins):
        self.n += 1
        ins.then_inc(self.sem, 1)
        return (self.sem, self.n)

    def op(self, fn, *args, w=(), **kw):
        self.wait(*w)
        return self.mark(fn(*args, **kw))

    def now(self):
        return (self.sem, self.n) if self.n else None


class Banks:

    def __init__(self, aps):
        self.free = [(a, []) for a in aps]
        self.low = len(aps)

    def take(self):
        ap, old = self.free.pop(0)
        self.low = min(self.low, len(self.free))
        return Bank(self, ap, old)


class Bank:
    def __init__(self, pool, ap, old):
        self.pool, self.ap, self.old, self.made = pool, ap, old, None

    def give(self, *marks):
        self.pool.free.append((self.ap, list(marks)))


class Places:

    def __init__(self, nc, base, n):
        self.nc, self.base, self.seen = nc, base, {}
        self.free = [(i, []) for i in range(n)]
        self.low = n

    def tensors(self, i, n):
        if (i, n) not in self.seen:
            self.seen[i, n] = [self.nc.alloc_sbuf_tensor_at(f"pl_{k}{i}_{n}", [128, n * S], t,
                                                            offset=self.base + 4 * S * i)[:, :]
                               for k, t in (("f", F32), ("r", F32R))]
        return self.seen[i, n]

    def take(self):
        i, old = self.free.pop(0)
        self.low = min(self.low, len(self.free))
        return Place(self, i, 1, old)

    def run(self, n):
        have = dict(self.free)
        start = next(i for i in sorted(have) if all(i + k in have for k in range(n)))
        old = [m for k in range(n) for m in have[start + k]]
        self.free = [(i, m) for i, m in self.free if not start <= i < start + n]
        self.low = min(self.low, len(self.free))
        return Place(self, start, n, old)


    def row(self, n):
        p = self.run(n)
        return [Place(self, p.i + k, 1, p.old) for k in range(n)]


class Place:
    def __init__(self, pool, i, n, old):
        self.pool, self.i, self.n, self.old = pool, i, n, old
        self.ap, self.r = pool.tensors(i, n)
        self.made = None

    def give(self, *marks):
        for k in range(self.n):
            self.pool.free.append((self.i + k, list(marks)))


class Pair:

    def __init__(self, pool, two=None):
        self.hi, self.lo = two or (pool.take(), pool.take())
        self.hi_made = self.lo_made = None

    def give(self, *marks):
        self.hi.give(*marks)
        self.lo.give(*marks)


def build(nc, x_d, w_d, mod_d, vec_d, cst_d, inv_d, ssm_d, uk_d, spill_d, out_d, plan):
    V, A, T, P = nc.vector, nc.scalar, nc.tensor, nc.gpsimd
    TT, TS, STT, SCAN = V.tensor_tensor, V.tensor_scalar, V.scalar_tensor_tensor, V.tensor_tensor_scan
    with ExitStack() as top:
        def sb(name, shape, dt=F32):
            return top.enter_context(nc.sbuf_tensor(name, shape, dt))

        def sem(name):
            return top.enter_context(nc.semaphore(name))

        pe = Engine(T, sem("s_pe"))
        dve = Engine(V, sem("s_dve"))
        act = Engine(A, sem("s_act"))
        pool = Engine(P, sem("s_pool"))
        sp = Engine(nc.sync, sem("s_sp"))
        d = dve.op
        s_raw = [sem(f"s_raw{i}") for i in range(NRAW)]
        s_mod = [sem(f"s_mod{i}") for i in range(2)]
        s_x = [sem(f"s_x{i}") for i in range(8)]
        s_vec, s_cst, s_ssm, s_inv, s_ki, s_out = (sem(n) for n in (
            "s_vec", "s_cst", "s_ssm", "s_inv", "s_ki", "s_out"))
        s_sp = [sem(f"s_sp{i}") for i in range(16)]

        banks_t = [top.enter_context(nc.psum_tensor(f"ps{i}", [128, S], F32)) for i in range(8)]
        misc = banks_t[7]
        banks = Banks([b[:, :] for b in banks_t[:7]])

        raw = sb("raw", [128, NRAW, UB * 128])
        whi = sb("whi", [128, NHL, UB * 128], F32R)
        wlo = sb("wlo", [128, NHL, UB * 128], F32R)
        vec = sb("vec", [128, NV])
        cst = sb("cst", [128, 3, 128])
        ident, ones, tri = cst[:, 0, :], cst[:, 1, :], cst[:, 2, :]
        sml = sb("sml", [128, 900])
        base = (nc.sbuf_base + 31) // 32 * 32
        n_pl = (nc.sbuf_usable_end - base) // (4 * S)
        places = Places(nc, base, n_pl)
        take = places.take

        def vc(name, j=0, n=1):
            o = VOFF[name] + j
            return vec[:, o:o + n]

        used_cols = [0]

        def sc(n):
            o = used_cols[0]
            used_cols[0] += n
            assert used_cols[0] <= 900
            return sml[:, o:o + n]

        unit_split = {}
        unit_done = {}

        def load_unit(u):
            if u >= NUNIT:
                return
            if u >= NRAW:
                sp.wait(unit_split[u - NRAW])
            nc.sync.dma_start(raw[:, u % NRAW, :], w_d[u]).then_inc(s_raw[u % NRAW], 16)

        def split_unit(u):
            if u >= NUNIT or u in unit_split:
                return
            landed = (s_raw[u % NRAW], 16 * (u // NRAW + 1))
            h, l, r = whi[:, u % NHL, :], wlo[:, u % NHL, :], raw[:, u % NRAW, :]
            used = unit_done[u - NHL] if u >= NHL else None
            hi_made = act.op(A.activation, h, r, ACT.Copy, w=[landed, used])
            lo_made = pool.op(P.tensor_tensor, l, r, h.bitcast(F32), ALU.subtract, w=[hi_made])
            unit_split[u] = lo_made
            load_unit(u + NRAW)

        def block(b, p, out, start, stop, mark):
            u, j = divmod(len(plan), UB)
            if j == 0:
                for a in range(LOOK + 1):
                    split_unit(u + a)
                pe.wait(unit_split[u])
            plan.append(b)
            c = slice(128 * j, 128 * j + 128)
            wh, wl = whi[:, u % NHL, c], wlo[:, u % NHL, c]
            pe.wait(p.hi_made)
            T.matmul(out, wh, p.hi.r, start=start, stop=False)
            T.matmul(out, wl, p.hi.r, start=False, stop=False)
            pe.wait(p.lo_made)
            mm = T.matmul(out, wh, p.lo.r, start=False, stop=stop)
            if j == UB - 1 or mark:
                m = pe.mark(mm)
                if j == UB - 1:
                    unit_done[u] = m
                return m

        def group(blocks, pairs):
            bank = banks.take()
            pe.wait(*bank.old)
            n = len(blocks)
            for i, (b, p) in enumerate(zip(blocks, pairs)):
                m = block(b, p, bank.ap, i == 0, i == n - 1, i == n - 1)
            bank.made = m
            return bank

        def groups(lists, pairs):
            bs = [banks.take() for _ in lists]
            n = len(pairs)
            for i, p in enumerate(pairs):
                for b, l in zip(bs, lists):
                    if i == 0:
                        pe.wait(*b.old)
                    b.made = block(l[i], p, b.ap, i == 0, i == n - 1, i == n - 1)
            return bs

        def kblocks(name, m, nk):
            return [(name, k, m) for k in range(nk)]

        ready = {}

        def ahead(keys, pairs):
            for k, b in zip(keys, groups([kblocks(n, m, len(pairs)) for n, m in keys], pairs)):
                ready[k] = b

        def tile(name, m, nk, pairs):
            if (name, m) in ready:
                return ready.pop((name, m))
            return group(kblocks(name, m, nk), pairs)

        def split(src, made, lo_on="pool", hi_on="act", two=None):
            p = Pair(places, two)
            if hi_on == "act":
                p.hi_made = act.op(A.activation, p.hi.r, src, ACT.Copy, w=[made, *p.hi.old])
            else:
                p.hi_made = d(V.tensor_copy, p.hi.r, src, w=[made, *p.hi.old])
            e, f = (pool, P.tensor_tensor) if lo_on == "pool" else (dve, TT)
            p.lo_made = e.op(f, p.lo.r, src, p.hi.r.bitcast(F32), ALU.subtract,
                             w=[p.hi_made, *p.lo.old])
            return p

        class Norm:

            def __init__(self):
                self.acc, self.m = None, None

            def add(self, ap, made, scale=1.0, last=False):
                if last:
                    A.preload_act_table(ACT.Sqrt)
                q = take()
                a = act.op(A.activation, q.ap, ap, ACT.Square, scale=scale, w=[made, *q.old])
                if self.acc is None:
                    self.acc, self.m = q, a
                else:
                    self.m = d(TT, self.acc.ap, self.acc.ap, q.ap, ALU.add, w=[a, self.m])
                    q.give(self.m)

        def col_sums(norms, rows=128):
            b = banks.take()
            pe.wait(*b.old, *[n.m for n in norms], ones_m)
            for i, n in enumerate(norms):
                for t in range(4):
                    c = 4 * i + t
                    mm = T.matmul(b.ap[:, c:c + 1], n.acc.ap[0:rows, 128 * t:128 * t + 128],
                                  ones[0:rows, 0:1], start=True, stop=True)
            b.made = pe.mark(mm)
            for n in norms:
                n.acc.give(b.made)
            return b

        def rows_of(cols, made):
            f = take()
            m = d(TT, f.ap.rearrange("p (t n) -> p t n", t=4),
                  ident.unsqueeze(1).broadcast_to([128, 4, 128]),
                  cols.unsqueeze(2).broadcast_to([128, 4, 128]), ALU.mult, w=[made, *f.old])
            b = banks.take()
            pe.wait(*b.old, m)
            b.made = pe.mark(T.matmul(b.ap, ones, f.ap, start=True, stop=True))
            f.give(b.made)
            return b

        def inv_rms(n, width, rows=128):
            b = col_sums([n], rows)
            r = sc(4)
            m = act.op(A.activation, r, b.ap[:, 0:4], ACT.Sqrt, bias=EPS, scale=1.0 / width,
                       w=[b.made])
            b.give(m)
            m = d(V.reciprocal, r, r, w=[m])
            return rows_of(r, m)

        def normed(xs, gain, bank, keys, shift=None):
            out = []
            row = places.row(16)
            for m in range(8):
                two = row[2 * m:2 * m + 2]
                f = take()
                a = d(STT, f.ap, xs[m].ap, gain(m), bank.ap, ALU.mult, ALU.mult,
                      w=[bank.made, xs[m].made, *f.old])
                if shift is None:
                    p = split(f.ap, a, lo_on="dve" if m % 2 else "pool", two=two)
                else:
                    p = Pair(places, two)
                    p.hi_made = act.op(A.activation, p.hi.r, f.ap, ACT.Identity, bias=shift(m),
                                       w=[a, *p.hi.old])
                    p.lo_made = d(STT, p.lo.r, f.ap, shift(m), p.hi.r.bitcast(F32), ALU.add,
                                  ALU.subtract, w=[p.hi_made, *p.lo.old])
                f.give(p.lo_made)
                out.append(p)
            bank.give(a)
            ahead(keys, out)
            return out

        x = [take() for _ in range(8)]
        for m in range(8):
            (A if m < 4 else nc.sync).dma_start(x[m].ap, x_d[m]).then_inc(s_x[m], 16)
            x[m].made = (s_x[m], 16)
        P.dma_start(vec[:, :], vec_d).then_inc(s_vec, 16)
        P.dma_start(cst[:, 0, :], cst_d[0]).then_inc(s_cst, 16)
        P.dma_start(cst[:, 2, :], cst_d[1]).then_inc(s_cst, 16)
        vec_in, cst_in = (s_vec, 16), (s_cst, 32)
        inv_p = places.run(4)
        inv = inv_p.ap.rearrange("p (g n) -> p g n", g=4)
        for u in range(NRAW):
            load_unit(u)
        nc.sync.dma_start(inv, inv_d).then_inc(s_inv, 16)
        ones_m = d(V.memset, ones, 1.0)

        nrm = Norm()
        for m in range(8):
            nrm.add(x[m].ap, x[m].made, last=m == 7)
        dve.wait(vec_in, cst_in)
        act.wait(vec_in, cst_in)
        pe.wait(cst_in)
        rs = inv_rms(nrm, 1024)
        for k in range(2):
            split_unit(k)
        h = normed(x, lambda m: vc("g_mix", m), rs,
                   [("w_in", 0), ("w_in", 10), ("w_in", 1), ("w_in", 11)])

        t0, t1, t2, t3 = sc(20), sc(20), sc(20), sc(20)
        half8, neg8 = sc(20), sc(20)
        lam = vc("lam_f", 0, 20)
        m = d(TS, t0, lam, -1.0, None, ALU.mult)
        m = d(TT, t0, t0, lam, ALU.min, w=[m])
        m = act.op(A.activation, t1, t0, ACT.Exp, w=[m])
        m = d(TS, t2, t1, 2.0, None, ALU.add, w=[m])
        m = d(V.reciprocal, t2, t2, w=[m])
        m = d(TT, t1, t1, t2, ALU.mult, w=[m])
        m = d(TT, t2, t1, t1, ALU.mult, w=[m])
        m = d(V.memset, t3, 1.0 / 19.0, w=[m])
        for k in (17, 15, 13, 11, 9, 7, 5, 3, 1):
            m = d(TT, t3, t3, t2, ALU.mult, w=[m])
            m = d(TS, t3, t3, 1.0 / k, None, ALU.add, w=[m])
        m = d(TT, t3, t3, t1, ALU.mult, w=[m])
        m = d(TS, t2, lam, -1.0, 0.0, ALU.mult, ALU.max, w=[m])
        m = d(STT, t3, t3, 2.0, t2, ALU.mult, ALU.add, w=[m])
        m = d(TS, half8, t3, 4.0, None, ALU.mult, w=[m])
        c8_m = d(TS, neg8, t3, -8.0, None, ALU.mult, w=[m])

        def lru_in(i):
            b = tile("w_in", i, 8, h)
            xa = take()
            a = act.op(A.activation, xa.ap, b.ap, ACT.Identity, bias=vc("conv_a_b", i),
                       scale=vc("conv_a_w", 20 + i), w=[b.made, *xa.old])
            for k, (o, s) in ((0, (slice(2, S), slice(0, S - 2))),
                              (1, (slice(1, S), slice(0, S - 1))),
                              (3, (slice(0, S - 1), slice(1, S)))):
                a = d(STT, xa.ap[:, o], b.ap[:, s], vc("conv_a_w", 10 * k + i), xa.ap[:, o],
                      ALU.mult, ALU.add, w=[a])
            b.give(a)
            xa.made = a
            return i, xa, split(xa.ap, a, lo_on="dve", hi_on="dve")

        def lru_gates(i, xa, p):
            gb = [group([(n, i, i)], [p]) for n in ("wa_f", "wa_b", "wx_f", "wx_b")]
            p.give(gb[-1].made)
            rr, ii, th = [], [], []
            for lst, b, n in ((rr, gb[0], "ba_f"), (rr, gb[1], "ba_b"), (ii, gb[2], "bx_f"),
                              (ii, gb[3], "bx_b")):
                f = take()
                f.made = act.op(A.activation, f.ap, b.ap, ACT.Sigmoid, bias=vc(n, i),
                                w=[b.made, *f.old])
                b.give(f.made)
                lst.append(f)
            for k in range(2):
                f = take()
                c = slice(10 * k + i, 10 * k + i + 1)
                f.made = act.op(A.activation, f.ap, rr[k].ap, ACT.Tanh, scale=half8[:, c],
                                w=[rr[k].made, c8_m, *f.old])
                th.append(f)
                ii[k].made = d(TT, ii[k].ap, ii[k].ap, xa.ap, ALU.mult, w=[ii[k].made, xa.made])
            xa.give(ii[1].made, p.lo_made)
            for k in range(2):
                c = slice(10 * k + i, 10 * k + i + 1)
                rr[k].made = act.op(A.activation, rr[k].ap, rr[k].ap, ACT.Exp, scale=neg8[:, c],
                                    w=[th[k].made])
            for k in range(2):
                th[k].made = act.op(A.activation, th[k].ap, th[k].ap, ACT.Sqrt, w=[th[k].made])
            for k in range(2):
                th[k].made = d(STT, th[k].ap, rr[k].ap, 1.0, th[k].ap, ALU.add, ALU.mult,
                               w=[rr[k].made, th[k].made])
            for k in range(2):
                th[k].made = d(TT, th[k].ap, th[k].ap, ii[k].ap, ALU.mult,
                               w=[th[k].made, ii[k].made])
                ii[k].give(th[k].made)
            m0 = d(SCAN, th[0].ap, rr[0].ap, th[0].ap, 0.0, ALU.mult, ALU.add, w=[th[0].made])
            m1 = d(SCAN, th[1].ap[:, ::-1], rr[1].ap[:, ::-1], th[1].ap[:, ::-1], 0.0, ALU.mult,
                   ALU.add, w=[th[1].made])
            rr[0].give(m0)
            rr[1].give(m1)
            a = d(TT, th[0].ap, th[0].ap, th[1].ap, ALU.add, w=[m0, m1])
            th[1].give(a)
            hs = split(th[0].ap, a, lo_on="dve", hi_on="dve")
            th[0].give(hs.lo_made)
            return hs

        def pool_tile(t):
            w = (2, 4, 8, 16)[t // 2]
            b = tile("w_in", 10 + t, 8, h)
            pl = places.run(4)
            f0, f1, f2 = (pl.ap[:, 600 * k:600 * k + S + 16] for k in range(3))
            z = d(V.memset, f0, 0.0, w=[*pl.old])
            u = act.op(A.activation, f0[:, w // 2:w // 2 + S], b.ap, ACT.Copy, w=[b.made, z])
            b.give(u)
            prev, n, made, k, step = f0, S + w - 1, u, 1, 0
            while k < w:
                n -= k
                o = (f1, f2)[step % 2]
                made = d(TT, o[:, 0:n], prev[:, 0:n], prev[:, k:k + n], ALU.add, w=[made])
                prev, k, step = o, 2 * k, step + 1
            made = d(TT, prev[:, 0:S], prev[:, 0:S], inv[:, t // 2, :], ALU.mult,
                     w=[made, (s_inv, 16)])
            made = d(TT, prev[:, 0:S], prev[:, 0:S], f0[:, w // 2:w // 2 + S], ALU.subtract,
                     w=[made])
            p = split(prev[:, 0:S], made, lo_on="dve", hi_on="dve")
            pl.give(p.lo_made)
            return p

        def pool_mix(t):
            g = t // 2
            b = group([("w_pool", 2 * g + k, t) for k in range(2)], pooled[2 * g:2 * g + 2])
            f = take()
            a = d(TS, f.ap, b.ap, vc("b_pool", t), vc("pool_scale", t), ALU.add, ALU.mult,
                  w=[b.made, *f.old])
            b.give(a)
            if t % 2:
                for q in pooled[2 * g:2 * g + 2]:
                    q.give(b.made)
            p = split(f.ap, a, lo_on="dve", hi_on="dve")
            f.give(p.lo_made)
            return p

        def branch_b(m):
            bg = group(kblocks("w_in", 26 + m, 8), h)
            f = take()
            f.made = act.op(A.activation, f.ap, bg.ap, ACT.Sigmoid, bias=vc("b_gate", 8 + m),
                            w=[bg.made, *f.old])
            bg.give(f.made)
            by = group(kblocks("p_b", m, 8), yb)
            f.made = d(TT, f.ap, by.ap, f.ap, ALU.mult, w=[f.made, by.made])
            by.give(f.made)
            return f

        hs, pooled, yb, tb = [], [], [], []
        work = [lambda t=t: pooled.append(pool_tile(t)) for t in range(8)]
        work += [lambda t=t: yb.append(pool_mix(t)) for t in range(8)]
        work += [lambda m=m: tb.append(branch_b(m)) for m in range(8)]
        share = [2, 2, 2, 2, 4, 4, 2, 2, 2, 2, 0]
        for m in range(8):
            x[m].give(*[e.now() for e in (act, dve)])
        todo = None
        for i in range(11):
            n = share[i]
            if n == 2 and len(work) > 8:
                work.pop(0)()
                n -= 1
            nxt = lru_in(i) if i < 10 else None
            for _ in range(n // 2):
                work.pop(0)()
            if todo is not None:
                hs.append(lru_gates(*todo))
            for _ in range(n - n // 2):
                work.pop(0)()
            todo = nxt
        assert not work
        for p in yb:
            p.give(pe.now())
        inv_p.give(dve.now())

        merged = []
        x = []
        for m in range(8):
            bg = group(kblocks("w_in", 18 + m, 8), h)
            f = take()
            a = act.op(A.activation, f.ap, bg.ap, ACT.Sigmoid, bias=vc("b_gate", m),
                       w=[bg.made, *f.old])
            bg.give(a)
            by = group(kblocks("p_a", m, 10), hs)
            a = d(TT, f.ap, by.ap, f.ap, ALU.mult, w=[a, by.made])
            by.give(a)
            a = d(TT, f.ap, f.ap, tb[m].ap, ALU.add, w=[a])
            tb[m].give(a)
            p = split(f.ap, a, lo_on="dve", hi_on="dve")
            f.give(p.lo_made)
            merged.append(p)
            q = take()
            sp.wait(*q.old)
            nc.sync.dma_start(q.ap, x_d[m]).then_inc(s_x[m], 16)
            q.made = (s_x[m], 32)
            x.append(q)
        for p in hs + h:
            p.give(pe.now())

        nrm = Norm()
        for m in range(8):
            b = group(kblocks("w_out", m, 8), merged)
            x[m].made = d(TT, x[m].ap, x[m].ap, b.ap, ALU.add, w=[b.made, x[m].made])
            b.give(x[m].made)
            nrm.add(x[m].ap, x[m].made, last=m == 7)
        for p in merged:
            p.give(pe.now())

        cond = sc(8)
        mod = sc(48)
        mod_used = {}
        mring, macc = places.run(4), places.run(2)
        mod_n = [0]

        def load_mod(u):
            if u < 48:
                sp.wait(*(mring.old if u < 2 else [mod_used[u - 2]]))
                nc.sync.dma_start(mring.ap[:, 1024 * (u % 2):1024 * (u % 2) + 1024],
                                  mod_d[u]).then_inc(s_mod[u % 2], 16)

        def next_mod():
            u = mod_n[0]
            if u == 48:
                return
            mod_n[0] += 1
            j, k = divmod(u, 8)
            r, c = mring.ap[:, 1024 * (u % 2):1024 * (u % 2) + 1024], cond[:, k:k + 1]
            landed = (s_mod[u % 2], 16 * (u // 2 + 1))
            if k == 0:
                mod_used[u] = d(TS, macc.ap, r, c, None, ALU.mult,
                                w=[landed, cond_m, macc.old if j == 0 else mod_summed[j - 1]])
            else:
                mod_used[u] = d(STT, macc.ap, r, c, macc.ap, ALU.mult, ALU.add,
                                w=[landed, mod_used[u - 1]])
            if u >= 1:
                load_mod(u + 1)
            if k == 7:
                mod_todo.append(j)

        def sum_mod():
            while mod_todo:
                j = mod_todo.pop()
                pe.wait(mod_used[8 * j + 7])
                for q in range(8):
                    mm = T.matmul(misc[:, 8 * j + q:8 * j + q + 1],
                                  macc.ap[:, 128 * q:128 * q + 128], ones[:, 0:1],
                                  start=True, stop=True)
                mod_summed[j] = pe.mark(mm)

        mod_todo, mod_summed = [], {}
        load_mod(0)
        load_mod(1)
        rs = inv_rms(nrm, 1024)
        h = normed(x, lambda m: vc("g_ffn", m), rs,
                   [("w_up", 0), ("w_up", 22), ("w_up", 1), ("w_up", 23)])
        cond_m = act.op(A.activation, cond, vc("c_2", 0, 8), ACT.Silu)

        def up_tile(j):
            b = tile("w_up", j, 8, h)
            f = take()
            a = act.op(A.activation, f.ap, b.ap, ACT.Identity, bias=vc("conv_f_b", j),
                       scale=vc("conv_f_w", 44 + j), w=[b.made, *f.old])
            a = d(STT, f.ap[:, 1:S], b.ap[:, 0:S - 1], vc("conv_f_w", j), f.ap[:, 1:S], ALU.mult,
                  ALU.add, w=[a])
            a = d(STT, f.ap[:, 0:S - 1], b.ap[:, 1:S], vc("conv_f_w", 88 + j),
                  f.ap[:, 0:S - 1], ALU.mult, ALU.add, w=[a])
            b.give(a)
            f.made = a
            return f

        acts = []
        for j in range(22):
            g = up_tile(j)
            sum_mod()
            next_mod()
            v = up_tile(22 + j)
            sum_mod()
            next_mod()
            g.made = act.op(A.activation, g.ap, g.ap, ACT.Gelu_apprx_tanh, w=[g.made])
            a = d(TT, g.ap, g.ap, v.ap, ALU.mult, w=[g.made, v.made])
            v.give(a)
            p = split(g.ap, a, lo_on="pool")
            g.give(p.lo_made)
            acts.append(p)
        for p in h:
            p.give(pe.now())
        s5p = places.run(8)
        ssm = s5p.ap[:, 0:2048].rearrange("p (c s n) -> p c s n", c=4, s=16)
        tab = s5p.ap[:, 2048:3072].rearrange("p (c s n) -> p c s n", c=2, s=16)
        bt = s5p.ap[:, 3072:4096].rearrange("p (c j n) -> p c j n", c=2, j=4)
        ukp = places.run(2)
        uk = ukp.ap.rearrange("p (c n) -> p c n", c=2)
        sp.wait(*s5p.old, *ukp.old)
        dve.wait(*s5p.old)
        nc.sync.dma_start(ssm, ssm_d).then_inc(s_ssm, 16)
        nc.sync.dma_start(uk, uk_d).then_inc(s_ssm, 16)
        ssm_in = (s_ssm, 32)
        mag = sc(16)
        pc = [sc(16) for _ in range(9)]
        ps = [sc(16) for _ in range(9)]
        ctab, stab = tab[:, 0], tab[:, 1]
        s5c = {}

        def s5_constants():
            are, aim = vc("ssm_a_re_2", 0, 16), vc("ssm_a_im_2", 0, 16)
            dt, ang, k_, r_, lre, lim, den, ta, tb_, cre, cim = (sc(16) for _ in range(11))
            m = act.op(A.activation, dt, vc("ssm_log_dt_2", 0, 16), ACT.Exp)
            m = d(TT, ang, are, dt, ALU.mult, w=[m])
            mg = act.op(A.activation, mag, ang, ACT.Exp, w=[m])
            m = d(TT, ang, aim, dt, ALU.mult, w=[mg])
            yield
            magic = 12582912.0
            p1, p2 = 6.28125, 0.00193500518798828125
            p3 = 2 * np.pi - p1 - p2
            m = d(TS, k_, ang, float(1.0 / (2 * np.pi)), magic, ALU.mult, ALU.add, w=[m])
            m = d(TS, k_, k_, -magic, None, ALU.add, w=[m])
            m = d(STT, r_, k_, -p1, ang, ALU.mult, ALU.add, w=[m])
            m = d(STT, r_, k_, -p2, r_, ALU.mult, ALU.add, w=[m])
            m = d(STT, r_, k_, -p3, r_, ALU.mult, ALU.add, w=[m])
            m = d(TS, r_, r_, 3.1415925, -3.1415925, ALU.min, ALU.max, w=[m])
            m = d(TS, k_, r_, -1.0, None, ALU.mult, w=[m])
            m = d(TT, k_, k_, r_, ALU.min, w=[m])
            m = d(TS, k_, k_, float(np.pi / 2), None, ALU.add, w=[m])
            s1 = act.op(A.activation, ps[0], r_, ACT.Sin, w=[m])
            s2 = act.op(A.activation, pc[0], k_, ACT.Sin, w=[m])
            yield
            m = d(TT, lre, mag, pc[0], ALU.mult, w=[s1, s2, mg])
            m = d(TT, lim, mag, ps[0], ALU.mult, w=[m])
            m = d(TS, lre, lre, -1.0, None, ALU.add, w=[m])
            m = d(TT, den, are, are, ALU.mult, w=[m])
            m = d(TT, ta, aim, aim, ALU.mult, w=[m])
            m = d(TT, den, den, ta, ALU.add, w=[m])
            m = d(V.reciprocal, den, den, w=[m])
            m = d(TT, ta, lre, are, ALU.mult, w=[m])
            m = d(TT, tb_, lim, aim, ALU.mult, w=[m])
            m = d(TT, ta, ta, tb_, ALU.add, w=[m])
            m = d(TT, cre, ta, den, ALU.mult, w=[m])
            m = d(TT, ta, lim, are, ALU.mult, w=[m])
            m = d(TT, tb_, lre, aim, ALU.mult, w=[m])
            m = d(TT, ta, ta, tb_, ALU.subtract, w=[m])
            m = d(TT, cim, ta, den, ALU.mult, w=[m])
            yield
            for l in range(8):
                m = d(TT, ta, pc[l], pc[l], ALU.mult, w=[m])
                m = d(TT, tb_, ps[l], ps[l], ALU.mult, w=[m])
                m = d(TT, pc[l + 1], ta, tb_, ALU.subtract, w=[m])
                m = d(STT, ps[l + 1], pc[l], 2.0, ps[l], ALU.mult, ALU.mult, w=[m])
                if l == 3:
                    yield
            yield

            def bc(ap, n):
                return ap.unsqueeze(2).broadcast_to([128, 16, n])

            m = d(V.memset, ctab[:, :, 0:1], 1.0, w=[m])
            m = d(V.memset, stab[:, :, 0:1], 0.0, w=[m])
            tf, t2f = take(), take()
            tv = tf.ap.rearrange("p (s n) -> p s n", s=16)
            t2v = t2f.ap.rearrange("p (s n) -> p s n", s=16)
            dve.wait(*tf.old, *t2f.old)
            for l in range(5):
                n = 1 << l
                lo_, hi_ = slice(0, n), slice(n, 2 * n)
                q1, q2 = tv[:, :, 0:n], t2v[:, :, 0:n]
                m = d(TT, ctab[:, :, hi_], ctab[:, :, lo_], bc(pc[l], n), ALU.mult, w=[m])
                m = d(TT, q1, stab[:, :, lo_], bc(ps[l], n), ALU.mult, w=[m])
                m = d(TT, ctab[:, :, hi_], ctab[:, :, hi_], q1, ALU.subtract, w=[m])
                m = d(TT, stab[:, :, hi_], stab[:, :, lo_], bc(pc[l], n), ALU.mult, w=[m])
                m = d(TT, q2, ctab[:, :, lo_], bc(ps[l], n), ALU.mult, w=[m])
                m = d(TT, stab[:, :, hi_], stab[:, :, hi_], q2, ALU.add, w=[m])
            yield
            bre, bim = ssm[:, 0], ssm[:, 1]
            m = d(TT, tv, bre, bc(cim, 32), ALU.mult, w=[m, ssm_in])
            m = d(TT, t2v, bim, bc(cim, 32), ALU.mult, w=[m])
            m = d(TT, bre, bre, bc(cre, 32), ALU.mult, w=[m])
            m = d(TT, bim, bim, bc(cre, 32), ALU.mult, w=[m])
            m = d(TT, bre, bre, t2v, ALU.subtract, w=[m])
            m = d(TT, bim, bim, tv, ALU.add, w=[m])
            m = d(TS, ssm[:, 3], ssm[:, 3], -1.0, None, ALU.mult, w=[m])
            tf.give(m)
            t2f.give(m)
            yield
            for c in range(2):
                b = banks.take()
                pe.wait(*b.old, m)
                for j in range(4):
                    mm = T.transpose(b.ap[:, 128 * j:128 * j + 128],
                                     ssm[:, c, 4 * j:4 * j + 4, :].rearrange("p s n -> p (s n)"),
                                     ident)
                a = act.op(A.activation, bt[:, c].rearrange("p j n -> p (j n)"), b.ap,
                           ACT.Copy, w=[pe.mark(mm), *(s5p.old if c == 0 else [])])
                b.give(a)
            s5c["bt"], s5c["tab"] = a, m

        gs1, gs2 = sc(8), sc(8)
        consts = s5_constants()
        nrm, nrm_g = Norm(), Norm()
        for m in range(8):
            b = group(kblocks("w_down", m, 22), acts)
            x[m].made = d(TT, x[m].ap, x[m].ap, b.ap, ALU.add, w=[b.made, x[m].made])
            b.give(x[m].made)
            nrm_g.add(x[m].ap, x[m].made, scale=vc("g_final", m))
            nrm.add(x[m].ap, x[m].made, last=m == 7)
            if m < 4:
                sum_mod()
                next_mod()
            if m == 4:
                sum_mod()
                mring.give(mod_used[47])
                macc.give(mod_summed[5])
                mod_m = d(TT, mod, misc[:, 0:48], vc("b_mod_2", 0, 48), ALU.add, w=[mod_summed[5]])
                banks.free.append((misc[:, :], [mod_m]))

                gs_m = d(STT, gs1, mod[:, 8:16], 1.0, vc("norm1_g_2", 0, 8), ALU.add, ALU.mult,
                         w=[mod_m])
                gs_m = d(TT, gs1, gs1, vc("g_final", 0, 8), ALU.mult, w=[gs_m])
                gs2_m = d(STT, gs2, mod[:, 32:40], 1.0, vc("norm2_g_2", 0, 8), ALU.add, ALU.mult,
                          w=[mod_m])
            next(consts, None)
            if m > 0:
                next(consts, None)
        for p in acts:
            p.give(pe.now())
        for _ in consts:
            pass

        b = col_sums([nrm, nrm_g])
        r1, r2 = sc(4), sc(4)
        m = act.op(A.activation, r1, b.ap[:, 0:4], ACT.Sqrt, bias=EPS, scale=1.0 / 1024,
                   w=[b.made])
        m1 = d(V.reciprocal, r1, r1, w=[m])
        m = d(TT, r2, r1, r1, ALU.mult, w=[m1])
        m = d(TT, r2, b.ap[:, 4:8], r2, ALU.mult, w=[m])
        b.give(m)
        m = act.op(A.activation, r2, r2, ACT.Sqrt, bias=EPS, scale=1.0 / 1024, w=[m])
        m = d(V.reciprocal, r2, r2, w=[m])
        m = d(TT, r2, r2, r1, ALU.mult, w=[m])
        rs = rows_of(r2, m)
        dve.wait(gs_m)
        u = normed(x, lambda m: gs1[:, m:m + 1], rs, [("w_in_2", m) for m in range(4)],
                   shift=lambda m: mod[:, m:m + 1])
        rs = rows_of(r1, m1)
        for m in range(8):
            x[m].made = d(STT, x[m].ap, x[m].ap, vc("g_final", m), rs.ap, ALU.mult, ALU.mult,
                          w=[rs.made, x[m].made])
        rs.give(x[7].made)

        xs = []
        for j in range(4):
            b = tile("w_in_2", j, 8, u)
            f = take()
            f.made = act.op(A.activation, f.ap, b.ap, ACT.Copy, w=[b.made, *f.old])
            b.give(f.made)
            xs.append(f)
        ys = []

        def s5():
            ybank = None
            for s in range(16):
                j, i = divmod(s, 4)
                rows = slice(32 * i, 32 * i + 32)
                tc, ts, q1, q2 = take(), take(), take(), take()
                a = act.op(A.activation, tc.ap[:, 0:32], ctab[:, s], ACT.Copy,
                           w=[s5c["tab"], *tc.old])
                b2 = act.op(A.activation, ts.ap[:, 0:32], stab[:, s], ACT.Copy, w=[*ts.old])
                wq = [*q1.old, *q2.old]
                for l in range(5, 9):
                    n = 1 << l
                    lo_, hi_ = slice(0, n), slice(n, 2 * n)
                    pcl, psl = pc[l][:, s:s + 1], ps[l][:, s:s + 1]
                    m1 = d(TS, q1.ap[:, lo_], ts.ap[:, lo_], psl, None, ALU.mult, w=[a, b2, *wq])
                    m2 = d(TS, q2.ap[:, lo_], tc.ap[:, lo_], psl, None, ALU.mult)
                    wq = []
                    a = d(STT, tc.ap[:, hi_], tc.ap[:, lo_], pcl, q1.ap[:, lo_], ALU.mult,
                          ALU.subtract, w=[m1])
                    b2 = d(STT, ts.ap[:, hi_], ts.ap[:, lo_], pcl, q2.ap[:, lo_], ALU.mult,
                           ALU.add, w=[m2])
                bb = []
                for c in range(2):
                    b = banks.take()
                    pe.wait(*b.old, xs[j].made, s5c["bt"])
                    b.made = pe.mark(T.matmul(b.ap, bt[rows, c, j, :], xs[j].ap[rows],
                                              start=True, stop=True))
                    bb.append(b)
                yield
                q3, q4 = take(), take()
                a1 = d(TT, q1.ap, bb[0].ap, tc.ap, ALU.mult, w=[bb[0].made, a, b2])
                a2 = d(TT, q2.ap, bb[1].ap, ts.ap, ALU.mult, w=[bb[1].made])
                a3 = d(TT, q3.ap, bb[1].ap, tc.ap, ALU.mult, w=[*q3.old])
                a4 = d(TT, q4.ap, bb[0].ap, ts.ap, ALU.mult, w=[*q4.old])
                bb[0].give(a4)
                bb[1].give(a3)
                b1 = pool.op(P.tensor_tensor, q1.ap, q1.ap, q2.ap, ALU.add, w=[a1, a2])
                b3 = pool.op(P.tensor_tensor, q3.ap, q3.ap, q4.ap, ALU.subtract, w=[a3, a4])
                yield
                mg_b = mag[:, s:s + 1].broadcast_to([128, S])
                z1 = d(SCAN, q1.ap, mg_b, q1.ap, 0.0, ALU.mult, ALU.add, w=[b1])
                z2 = d(SCAN, q3.ap, mg_b, q3.ap, 0.0, ALU.mult, ALU.add, w=[b3])
                a2 = d(TT, q2.ap, ts.ap, q3.ap, ALU.mult, w=[z2])
                a4 = d(TT, q4.ap, ts.ap, q1.ap, ALU.mult, w=[z1])
                a1 = d(TT, q1.ap, tc.ap, q1.ap, ALU.mult, w=[a4])
                a3 = d(TT, q3.ap, tc.ap, q3.ap, ALU.mult, w=[a2])
                tc.give(a3)
                ts.give(a4)
                b1 = pool.op(P.tensor_tensor, q1.ap, q1.ap, q2.ap, ALU.subtract, w=[a1, a2])
                b3 = pool.op(P.tensor_tensor, q3.ap, q3.ap, q4.ap, ALU.add, w=[a3, a4])
                q2.give(b1)
                q4.give(b3)
                yield
                if i == 0:
                    ybank = banks.take()
                    pe.wait(*ybank.old)
                pe.wait(b1, b3)
                T.matmul(ybank.ap[rows], ssm[:, 2, s, :], q1.ap, start=True, stop=False,
                         tile_position=(0, 32 * i))
                mm = pe.mark(T.matmul(ybank.ap[rows], ssm[:, 3, s, :], q3.ap, start=False,
                                      stop=True, tile_position=(0, 32 * i)))
                q1.give(mm)
                q3.give(mm)
                if i == 3:
                    a = d(STT, xs[j].ap, xs[j].ap, vc("ssm_d_2", j), ybank.ap, ALU.mult,
                          ALU.add, w=[mm, xs[j].made])
                    ybank.give(a)
                    a = act.op(A.activation, xs[j].ap, xs[j].ap, ACT.Gelu_apprx_tanh, w=[a])
                    p = split(xs[j].ap, a)
                    xs[j].give(p.lo_made)
                    ys.append(p)
            s5p.give(pe.now(), dve.now(), act.now())

        att = []

        def proj(m, scale=1.0):
            b = tile("w_in_2", m, 8, u)
            f = take()
            f.made = act.op(A.activation, f.ap, b.ap, ACT.Copy, scale=scale, w=[b.made, *f.old])
            b.give(f.made)
            return f

        def dsa():
            qi = [proj(9, 0.125), proj(10, 0.125)]
            yield
            kw = proj(11)
            n2 = Norm()
            n2.add(kw.ap, kw.made)
            yield
            b = banks.take()
            pe.wait(*b.old, kw.made)
            for t in range(4):
                mm = T.transpose(b.ap[:, 128 * t:128 * t + 128], kw.ap[:, 128 * t:128 * t + 128],
                                 ident)
            mm = pe.mark(mm)
            wi_c = sc(16)
            wi = wi_c.rearrange("p (t n) -> p t n", t=4)
            wi_m = act.op(A.activation, wi, b.ap.rearrange("p (t n) -> p t n", t=4)[:, :, 64:68],
                          ACT.Copy, scale=0.5, w=[mm])
            b.give(wi_m)
            r = inv_rms(n2, 64, rows=64)
            ki_m = d(STT, kw.ap[0:64], kw.ap[0:64], vc("idx_k_norm_g_2")[0:64], r.ap[0:64],
                     ALU.mult, ALU.mult, w=[r.made, mm])
            r.give(ki_m)
            sp.wait(ki_m, wi_m, mm)
            nc.sync.dma_start(kw.ap[64:128], kw.ap[0:64]).then_inc(s_ki, 16)
            ki_m = (s_ki, 16)
            yield
            mp = places.run(3)
            masks = mp.ap
            moff = [0, 128, 384, 768]
            m8 = sc(8)
            need = sc(1)
            mk_m = [d(TS, masks[:, 0:128], tri, 3.3e-9, None, ALU.mult, w=[*mp.old])]
            ck = nat = None
            qt = []
            for t in (3, 2, 1):
                kmax = 128 * (t + 1)
                scr, wk, e1 = take(), take(), take()
                am = None
                for hh in range(4):
                    rows = slice(64 * (hh % 2), 64 * (hh % 2) + 64)
                    b = banks.take()
                    pe.wait(*b.old, qi[hh // 2].made, ki_m)
                    mm = pe.mark(T.matmul(b.ap[:, 0:kmax],
                                          qi[hh // 2].ap[rows, 128 * t:128 * t + 128],
                                          kw.ap[rows, 0:kmax], start=True, stop=True))
                    wcol = wi_c[:, 4 * t + hh:4 * t + hh + 1]
                    if hh == 0:
                        am = d(TS, scr.ap[:, 0:kmax], b.ap[:, 0:kmax], 0.0, wcol, ALU.max,
                               ALU.mult, w=[mm, wi_m, *scr.old])
                        b.give(am)
                    else:
                        f = take()
                        rm = act.op(A.activation, f.ap[:, 0:kmax], b.ap[:, 0:kmax], ACT.Relu,
                                    w=[mm, *f.old])
                        b.give(rm)
                        am = d(STT, scr.ap[:, 0:kmax], f.ap[:, 0:kmax], wcol,
                               scr.ap[:, 0:kmax], ALU.mult, ALU.add, w=[rm, am])
                        f.give(am)
                am = d(TT, scr.ap[:, kmax - 128:kmax], scr.ap[:, kmax - 128:kmax], tri, ALU.add,
                       w=[am])
                cur = scr.ap[:, 0:kmax]
                dve.wait(*wk.old, *e1.old)
                for rnd in range(16):
                    am = d(V.max, m8, cur, w=[am])
                    if rnd < 15:
                        am = d(V.match_replace, wk.ap[:, 0:kmax], m8, cur, -3.4e38, w=[am])
                        cur = wk.ap[:, 0:kmax]
                    if rnd in (2, 5, 8, 11, 14):
                        if t == 3 and rnd == 2:
                            ck = proj(8)
                            n1 = Norm()
                            n1.add(ck.ap, ck.made)
                        elif t == 3 and rnd == 5:
                            r = inv_rms(n1, 128)
                            ck.made = d(STT, ck.ap, ck.ap, vc("kv_norm_g_2"), r.ap, ALU.mult,
                                        ALU.mult, w=[r.made])
                            r.give(ck.made)
                        elif t == 3 and rnd == 8:
                            b = banks.take()
                            pe.wait(*b.old, ck.made)
                            for k in range(4):
                                mm = T.transpose(b.ap[:, 128 * k:128 * k + 128],
                                                 ck.ap[:, 128 * k:128 * k + 128], ident)
                            nat = take()
                            nat.made = act.op(A.activation, nat.ap, b.ap, ACT.Copy,
                                              w=[pe.mark(mm), *nat.old])
                            b.give(nat.made)
                        yield
                thr = m8[:, 7:8]
                mk = masks[:, moff[t]:moff[t] + kmax]
                am = d(TS, mk, scr.ap[:, 0:kmax], thr, None, ALU.is_gt, ALU.add, accum_out=need,
                       w=[am])
                em = d(TS, e1.ap[:, 0:kmax], scr.ap[:, 0:kmax], thr, None, ALU.is_equal)
                am = d(TS, need, need, -1.0, 128.0, ALU.mult, ALU.add, w=[am])
                em = d(SCAN, wk.ap[:, 0:kmax], e1.ap[:, 0:kmax], e1.ap[:, 0:kmax], 0.0, ALU.add,
                       ALU.max, w=[em])
                em = d(STT, e1.ap[:, 0:kmax], wk.ap[:, 0:kmax], need, e1.ap[:, 0:kmax],
                       ALU.is_le, ALU.mult, w=[em, am])
                em = d(TT, mk, mk, e1.ap[:, 0:kmax], ALU.add, w=[em])
                em = d(TS, mk, mk, -1.0, BIG, ALU.add, ALU.mult, w=[em])
                mk_m.insert(1, em)
                for f in (scr, wk, e1):
                    f.give(em)
                qt.append(proj(4 + len(qt), 0.125))
                yield
            qt.append(proj(7, 0.125))
            for f in qi:
                f.give(pe.now())
            kw.give(pe.now())
            pp = places.run(4)
            pt = pp.ap.rearrange("p (k n) -> p k n", k=4)
            pt_free = pp.old
            abank = None
            q_made = None

            def latent(hh):
                rows = slice(64 * (hh % 2), 64 * (hh % 2) + 64)
                b = banks.take()
                pe.wait(*b.old, qt[hh // 2].made, ssm_in)
                mm = pe.mark(T.matmul(b.ap, uk[rows, 0, 128 * (hh // 2):128 * (hh // 2) + 128],
                                      qt[hh // 2].ap[rows], start=True, stop=True))
                ql = take()
                ql.made = act.op(A.activation, ql.ap, b.ap, ACT.Copy, w=[mm, *ql.old])
                b.give(ql.made)
                if hh % 2:
                    qt[hh // 2].give(mm)
                return ql

            ql = latent(0)
            yield
            stat = [[sc(4) for _ in range(3)] for _ in range(2)]
            stat_free = [[], []]
            for hh in range(8):
                rows = slice(64 * (hh % 2), 64 * (hh % 2) + 64)
                mx, nm, rsm = stat[hh % 2]
                fs = [None] * 4
                for tt in ((3, 2), (1, 0)):
                    bs = {}
                    for t in tt:
                        b = banks.take()
                        pe.wait(*b.old, ql.made, ck.made)
                        b.made = pe.mark(T.matmul(b.ap[:, 0:128 * (t + 1)],
                                                  ql.ap[:, 128 * t:128 * t + 128],
                                                  ck.ap[:, 0:128 * (t + 1)],
                                                  start=True, stop=True))
                        bs[t] = b
                    for t in tt:
                        kmax = 128 * (t + 1)
                        c = slice(t, t + 1)
                        f = fs[t] = take()
                        b = bs[t]
                        a = d(V.tensor_tensor_reduce, f.ap[:, 0:kmax], b.ap[:, 0:kmax],
                              masks[:, moff[t]:moff[t] + kmax], 1.0, NEG, ALU.add, ALU.max,
                              mx[:, c], w=[b.made, mk_m[t], *f.old, *stat_free[hh % 2]])
                        b.give(a)
                        a = d(TS, nm[:, c], mx[:, c], -1.0, None, ALU.mult, w=[a])
                        f.made = act.op(A.activation, f.ap[:, 0:kmax], f.ap[:, 0:kmax], ACT.Exp,
                                        bias=nm[:, c], accum_out=rsm[:, c], w=[a])
                if hh < 7:
                    nql = latent(hh + 1)
                yield
                for t in (3, 2, 1, 0):
                    kmax = 128 * (t + 1)
                    c = slice(t, t + 1)
                    fs[t].made = d(V.reciprocal, rsm[:, c], rsm[:, c], w=[fs[t].made])
                for t in (3, 2, 1, 0):
                    kmax = 128 * (t + 1)
                    c = slice(t, t + 1)
                    fs[t].made = d(TS, fs[t].ap[:, 0:kmax], fs[t].ap[:, 0:kmax], rsm[:, c], None,
                                   ALU.mult, w=[fs[t].made])
                stat_free[hh % 2] = [fs[0].made, act.now()]
                ql.give(pe.now())
                yield
                pv_w = []
                for t in (3, 2, 1, 0):
                    kmax = 128 * (t + 1)
                    b = banks.take()
                    pe.wait(*b.old, fs[t].made)
                    for k in range(t + 1):
                        mm = T.transpose(b.ap[:, 128 * k:128 * k + 128],
                                         fs[t].ap[:, 128 * k:128 * k + 128], ident)
                    mm = pe.mark(mm)
                    fs[t].give(mm)
                    a = act.op(A.activation, pt[:, 0:t + 1, 128 * t:128 * t + 128],
                               b.ap[:, 0:kmax].rearrange("p (k n) -> p k n", n=128), ACT.Copy,
                               w=[mm, *pt_free])
                    b.give(a)
                    pv_w.append(a)
                yield
                b = banks.take()
                pe.wait(*b.old, *pv_w, nat.made)
                for k in range(4):
                    mm = T.matmul(b.ap[:, 128 * k:S], nat.ap[:, 128 * k:128 * k + 128],
                                  pt[:, k, 128 * k:S], start=(k == 0), stop=(k == 3))
                mm = pe.mark(mm)
                pt_free = [mm]
                o_ = take()
                om = act.op(A.activation, o_.ap, b.ap, ACT.Copy, w=[mm, *o_.old])
                b.give(om)
                yield
                if hh % 2 == 0:
                    abank = banks.take()
                    pe.wait(*abank.old)
                pe.wait(om)
                mm = pe.mark(T.matmul(abank.ap[rows], uk[:, 1, 64 * hh:64 * hh + 64], o_.ap,
                                      start=True, stop=True, tile_position=(0, 64 * (hh % 2))))
                o_.give(mm)
                if hh % 2:
                    p = Pair(places)
                    p.hi_made = act.op(A.activation, p.hi.r, abank.ap, ACT.Copy,
                                       w=[mm, *p.hi.old])
                    p.lo_made = d(TT, p.lo.r, abank.ap, p.hi.r.bitcast(F32), ALU.subtract,
                                  w=[p.hi_made, *p.lo.old])
                    abank.give(p.lo_made)
                    att.append(p)
                ql = nql
            ck.give(pe.now())
            nat.give(pe.now())
            pp.give(pt_free[0])
            ukp.give(pe.now())
            mp.give(dve.now())

        def gates():
            for k in range(16):
                b = tile("w_in_2", 12 + k, 8, u)
                f = take()
                f.made = act.op(A.activation, f.ap, b.ap, ACT.Sigmoid, w=[b.made, *f.old])
                b.give(f.made)
                act.wait(f.made)
                A.dma_start(spill_d[k], f.ap).then_inc(s_sp[k], 16)
                f.give((s_sp[k], 16))
                yield

        schedule(dsa(), s5(), gates())
        for p in u:
            p.give(pe.now())

        merged = []

        def reload(k):
            f = take()
            sp.wait((s_sp[k], 16), *f.old)
            nc.sync.dma_start(f.ap, spill_d[k]).then_inc(s_sp[k], 16)
            f.made = (s_sp[k], 32)
            return f

        sg = {k: reload(k) for k in (0, 8, 1, 9)}
        for m in range(8):
            if m + 2 < 8:
                sg[m + 2], sg[m + 10] = reload(m + 2), reload(m + 10)
            b = group(kblocks("w_ssm_glu_2", 8 + m, 4), ys)
            f = take()
            a = act.op(A.activation, f.ap, b.ap, ACT.Sigmoid, bias=vc("b_ssm_glu_2", 8 + m),
                       w=[b.made, *f.old])
            b.give(a)
            b = group(kblocks("w_ssm_glu_2", m, 4), ys)
            a = d(STT, f.ap, b.ap, vc("b_ssm_glu_2", m), f.ap, ALU.add, ALU.mult,
                  w=[a, b.made])
            b.give(a)
            fa, fb = sg[m], sg[8 + m]
            a = pool.op(P.tensor_tensor, f.ap, f.ap, fa.ap, ALU.mult, w=[a, fa.made])
            fa.give(a)
            b = group(kblocks("w_attn_proj_2", m, 4), att)
            c = d(TT, fb.ap, b.ap, fb.ap, ALU.mult, w=[b.made, fb.made])
            b.give(c)
            a = d(TT, f.ap, f.ap, fb.ap, ALU.add, w=[a, c])
            fb.give(a)
            p = split(f.ap, a, lo_on="dve")
            f.give(p.lo_made)
            merged.append(p)
        for p in ys + att:
            p.give(pe.now())

        nrm = Norm()

        def gated_add(gcol, m, b):
            x[m].made = d(STT, x[m].ap, b.ap, mod[:, gcol + m:gcol + m + 1], x[m].ap, ALU.mult,
                          ALU.add, w=[b.made, x[m].made])
            b.give(x[m].made)
            nrm.add(x[m].ap, x[m].made, last=m == 7)

        for m in range(8):
            gated_add(16, m, group(kblocks("w_out_2", m, 8), merged))
        for p in merged:
            p.give(pe.now())
        rs = inv_rms(nrm, 1024)
        dve.wait(gs2_m)
        h = normed(x, lambda m: gs2[:, m:m + 1], rs,
                   [("w_ffn_gate_2", 0), ("w_ffn_up_2", 0), ("w_ffn_gate_2", 1),
                    ("w_ffn_up_2", 1)], shift=lambda m: mod[:, 24 + m:25 + m])
        acts = []
        for j in range(22):
            b = tile("w_ffn_gate_2", j, 8, h)
            f = take()
            a = act.op(A.activation, f.ap, b.ap, ACT.Silu, w=[b.made, *f.old])
            b.give(a)
            b = tile("w_ffn_up_2", j, 8, h)
            a = d(TT, f.ap, b.ap, f.ap, ALU.mult, w=[a, b.made])
            b.give(a)
            p = split(f.ap, a, lo_on="dve")
            f.give(p.lo_made)
            acts.append(p)
        for p in h:
            p.give(pe.now())
        nrm = Norm()
        for m in range(8):
            gated_add(40, m, group(kblocks("w_ffn_down_2", m, 22), acts))
        rs = inv_rms(nrm, 1024)
        for m in range(8):
            a = d(STT, x[m].ap, x[m].ap, vc("final_g_2", m), rs.ap, ALU.mult, ALU.mult,
                  w=[rs.made, x[m].made])
            e, q = (act, A) if m % 2 else (sp, nc.sync)
            e.wait(a)
            q.dma_start(out_d[m], x[m].ap).then_inc(s_out, 16)
        for k in range(16):
            nc.sync.wait_ge(s_sp[k], 32)
        nc.sync.wait_ge(s_out, 16 * 8)
        assert len(plan) == NBLK, len(plan)


def schedule(dsa, s5, gates):
    steps = 0
    live = [dsa, s5]
    while live:
        for g in list(live):
            if next(g, "end") == "end":
                live.remove(g)
            steps += 1
            if steps % 5 == 4:
                next(gates, None)
    for _ in gates:
        pass


def lay_out(inputs, plan):
    f = {k: np.asarray(v) for k, v in inputs.items()}
    one = {k: v[0] for k, v in f.items() if k not in ("x", "g_final", "final_g_2", "c_2")}

    ki = np.zeros((1024, 3584), np.float32)
    w = one["w_in_2"]
    ki[:, 0:1408] = w[:, 0:1408]
    ki[:, 1408:1476] = w[:, 1408:1476]
    ki[:, 1536:3584] = w[:, 1476:3524]
    mats = {n: one[n] for n in ("w_in", "p_a", "p_b", "w_out", "w_up", "w_down", "w_ssm_glu_2",
                                "w_attn_proj_2", "w_out_2", "w_ffn_gate_2", "w_ffn_up_2",
                                "w_ffn_down_2")}
    mats["w_in_2"] = ki
    stream = np.zeros((NUNIT, 128, UB * 128), np.float32)
    for n, (name, k, m) in enumerate(plan):
        u, j = divmod(n, UB)
        if name in ("wa_f", "wx_f", "wa_b", "wx_b"):
            blk = one[name][k]
        elif name == "w_pool":
            blk = one[name][k // 2, 128 * (k % 2):128 * (k % 2) + 128,
                            128 * (m % 2):128 * (m % 2) + 128]
        else:
            blk = mats[name][128 * k:128 * k + 128, 128 * m:128 * m + 128]
        stream[u, :, 128 * j:128 * j + 128] = blk

    vec = np.zeros((128, NV), np.float32)

    def put(name, a):
        a = np.asarray(a).reshape(-1, 128).T
        vec[:, VOFF[name]:VOFF[name] + a.shape[1]] = a

    for name, n in VECS:
        if name == "ssm_log_dt_2":
            put(name, np.repeat(one[name], 64))
        elif name == "idx_k_norm_g_2":
            vec[0:64, VOFF[name]] = one[name]
        elif name in ("g_final", "final_g_2", "c_2"):
            put(name, f[name])
        else:
            put(name, one[name])

    cst = np.zeros((2, 128, 128), np.float32)
    cst[0] = np.eye(128)
    cst[1] = np.where(np.arange(128)[None, :] <= np.arange(128)[:, None], 0.0, NEG)
    t = np.arange(S)
    inv = np.zeros((128, 4, S), np.float32)
    for g, wd in enumerate((2, 4, 8, 16)):
        lo = np.clip(t - wd // 2, 0, S - 1)
        hi = np.clip(t + wd // 2 - 1, 0, S - 1)
        inv[:, g, :] = (1.0 / (hi - lo + 1)).astype(np.float32)

    ssm = np.zeros((128, 4, 16, 32), np.float32)
    for c, name in enumerate(("ssm_b_re_2", "ssm_b_im_2", "ssm_c_re_2", "ssm_c_im_2")):
        a = one[name] if c < 2 else one[name].transpose(0, 2, 1)
        a = a.reshape(16, 2, 64, 16)
        for g in range(2):
            ssm[64 * g:64 * g + 64, c, :, 16 * g:16 * g + 16] = a[:, g].transpose(1, 0, 2)
    uk = np.zeros((128, 2, 512), np.float32)
    uk[:, 0, :] = one["w_uk_2"].transpose(1, 2, 0).reshape(4, 128, 128).transpose(1, 0, 2)\
        .reshape(128, 512)
    uk[:, 1, :] = one["w_uv_2"].reshape(128, 512)
    mod = one["w_mod_2"].reshape(8, 128, 6, 1024).transpose(2, 0, 1, 3).reshape(48, 128, 1024)
    x = f["x"][0].T.reshape(8, 128, S)
    arrays = {"x": x, "w": stream, "mod": mod, "vec": vec, "cst": cst, "inv": inv, "ssm": ssm,
              "uk": uk}
    return {k: np.ascontiguousarray(a) for k, a in arrays.items()}


SHAPES = {"x": (8, 128, S), "w": (NUNIT, 128, UB * 128), "mod": (48, 128, 1024),
          "vec": (128, NV), "cst": (2, 128, 128), "inv": (128, 4, S), "ssm": (128, 4, 16, 32),
          "uk": (128, 2, 512)}


def program(nc):
    aps = [nc.dram_tensor(f"in_{n}", s, F32, kind="ExternalInput").ap() for n, s in SHAPES.items()]
    out = nc.dram_tensor("out_t", (8, 128, S), F32, kind="ExternalOutput").ap()
    spill = nc.dram_tensor("spill", (16, 128, S), F32, kind="Internal").ap()
    plan = []
    build(nc, *aps, spill, out, plan)
    return plan


def kernel(**inputs):
    from concourse import bacc
    from concourse.bass_utils import run_bass_kernel_spmd

    nc = bacc.Bacc("TRN2", target_bir_lowering=False, num_devices=1)
    plan = program(nc)
    arrays = {f"in_{k}": v for k, v in lay_out(inputs, plan).items()}
    r = run_bass_kernel_spmd(nc, [arrays], core_ids=[0])
    y = r.results[0]["out_t"]
    return np.ascontiguousarray(np.asarray(y).reshape(1024, S).T)[None]
```

```python
from itertools import chain
from contextlib import ExitStack

import numpy as np

import concourse.bass as bass
from concourse import mybir

F32 = mybir.dt.float32
F32R = mybir.dt.float32r
ALU = mybir.AluOpType
ACT = mybir.ActivationFunctionType

S = 512
UB = 8
NRAW = 3
NHL = 3
LOOK = 2
NBLK = 1976
NUNIT = NBLK // UB
EPS = 1e-6
GATE_STOPS = (1, 3, 5)
S5_LATE = 1
FILL = (0.95, 0.5, 1.2)
S5_PACE = (1.1, 1.55)
UP_STEPS = (0, 0, 1, 1, 0, 1) + (0, 1, 1, 0, 1) * 3 + (0,)
GATES_A = (0, 1, 1, 1, 1, 1, 1, 1, 0, 0, 0)
SHARE = (2, 2, 2, 2, 4, 4, 2, 2, 2, 1, 1)
GLU_ON = ("dve", "dve")
NORM_LO = ("dve", "dve")
NORM_HI = ("act", "act")
YS_ON = ("act", "pool")
MERGE_HI = "act"
FFN2_HI = "act"

MOD_FROM = 3
MOD_TWICE = 6
NEG = -3.0e38
BIG = 1.0e30

VECS = [
    ("g_mix", 8), ("b_gate", 16), ("conv_a_w", 40), ("conv_a_b", 10),
    ("ba_f", 10), ("bx_f", 10), ("ba_b", 10), ("bx_b", 10), ("lam_f", 10), ("lam_b", 10),
    ("b_pool", 8), ("pool_scale", 8), ("g_ffn", 8), ("conv_f_w", 132), ("conv_f_b", 44),
    ("g_final", 8), ("c_2", 8), ("b_mod_2", 48), ("norm1_g_2", 8), ("ssm_a_re_2", 16),
    ("ssm_a_im_2", 16), ("ssm_log_dt_2", 16), ("ssm_d_2", 4), ("b_ssm_glu_2", 16),
    ("kv_norm_g_2", 1), ("idx_k_norm_g_2", 1), ("norm2_g_2", 8), ("final_g_2", 8),
]
VOFF = {}
NV = 0
for _n, _c in VECS:
    VOFF[_n] = NV
    NV += _c


class Engine:

    def __init__(self, eng, sem):
        self.eng, self.sem, self.n, self.seen = eng, sem, 0, {}

    def wait(self, *marks):
        for m in marks:
            if m is None:
                continue
            if isinstance(m, list):
                self.wait(*m)
                continue
            sem, value = m
            if self.seen.get(id(sem), 0) < value:
                self.seen[id(sem)] = value
                self.eng.wait_ge(sem, value)

    def mark(self, ins):
        self.n += 1
        ins.then_inc(self.sem, 1)
        return (self.sem, self.n)

    def op(self, fn, *args, w=(), **kw):
        self.wait(*w)
        return self.mark(fn(*args, **kw))

    def now(self):
        return (self.sem, self.n) if self.n else None


class Banks:

    def __init__(self, aps):
        self.free = [(a, []) for a in aps]
        self.low = len(aps)

    def take(self):
        ap, old = self.free.pop(0)
        self.low = min(self.low, len(self.free))
        return Bank(self, ap, old)


class Bank:
    def __init__(self, pool, ap, old):
        self.pool, self.ap, self.old, self.made = pool, ap, old, None

    def give(self, *marks):
        self.pool.free.append((self.ap, list(marks)))


class Places:

    def __init__(self, nc, base, n):
        self.nc, self.base, self.seen = nc, base, {}
        self.free = [(i, []) for i in range(n)]
        self.low = n

    def tensors(self, i, n):
        if (i, n) not in self.seen:
            self.seen[i, n] = [self.nc.alloc_sbuf_tensor_at(f"pl_{k}{i}_{n}", [128, n * S], t,
                                                            offset=self.base + 4 * S * i)[:, :]
                               for k, t in (("f", F32), ("r", F32R))]
        return self.seen[i, n]

    def take(self):
        i, old = self.free.pop(0)
        self.low = min(self.low, len(self.free))
        return Place(self, i, 1, old)

    def run(self, n):
        have = dict(self.free)
        start = next(i for i in sorted(have) if all(i + k in have for k in range(n)))
        old = [m for k in range(n) for m in have[start + k]]
        self.free = [(i, m) for i, m in self.free if not start <= i < start + n]
        self.low = min(self.low, len(self.free))
        return Place(self, start, n, old)


    def row(self, n):
        p = self.run(n)
        return [Place(self, p.i + k, 1, p.old) for k in range(n)]


class Place:
    def __init__(self, pool, i, n, old):
        self.pool, self.i, self.n, self.old = pool, i, n, old
        self.ap, self.r = pool.tensors(i, n)
        self.made = None

    def give(self, *marks):
        for k in range(self.n):
            self.pool.free.append((self.i + k, list(marks)))


class Pair:

    def __init__(self, pool, two=None):
        self.hi, self.lo = two or (pool.take(), pool.take())
        self.hi_made = self.lo_made = None

    def give(self, *marks):
        self.hi.give(*marks)
        self.lo.give(*marks)


def build(nc, x_d, w_d, mod_d, vec_d, cst_d, inv_d, ssm_d, uk_d, spill_d, tab_d, out_d, plan):
    V, A, T, P = nc.vector, nc.scalar, nc.tensor, nc.gpsimd
    TT, TS, STT, SCAN = V.tensor_tensor, V.tensor_scalar, V.scalar_tensor_tensor, V.tensor_tensor_scan
    with ExitStack() as top:
        def sb(name, shape, dt=F32):
            return top.enter_context(nc.sbuf_tensor(name, shape, dt))

        def sem(name):
            return top.enter_context(nc.semaphore(name))

        pe = Engine(T, sem("s_pe"))
        dve = Engine(V, sem("s_dve"))
        act = Engine(A, sem("s_act"))
        pool = Engine(P, sem("s_pool"))
        sp = Engine(nc.sync, sem("s_sp"))
        d = dve.op
        s_raw = [sem(f"s_raw{i}") for i in range(NRAW)]
        s_mod = [sem(f"s_mod{i}") for i in range(2)]
        s_x = [sem(f"s_x{i}") for i in range(8)]
        s_vec, s_cst, s_ssm, s_inv, s_ki, s_out = (sem(n) for n in (
            "s_vec", "s_cst", "s_ssm", "s_inv", "s_ki", "s_out"))
        s_tw = sem("s_tw")
        s_tr = [sem(f"s_tr{i}") for i in range(3)]
        s_sp = [sem(f"s_sp{i}") for i in range(16)]

        banks_t = [top.enter_context(nc.psum_tensor(f"ps{i}", [128, S], F32)) for i in range(8)]
        misc = banks_t[7]
        banks = Banks([b[:, :] for b in banks_t[:7]])

        raw = sb("raw", [128, NRAW, UB * 128])
        whi = sb("whi", [128, NHL, UB * 128], F32R)
        wlo = sb("wlo", [128, NHL, UB * 128], F32R)
        vec = sb("vec", [128, NV])
        cst = sb("cst", [128, 3, 128])
        ident, ones, tri = cst[:, 0, :], cst[:, 1, :], cst[:, 2, :]
        sml = sb("sml", [128, 900])
        base = (nc.sbuf_base + 31) // 32 * 32
        n_pl = (nc.sbuf_usable_end - base) // (4 * S)
        places = Places(nc, base, n_pl)
        take = places.take

        def vc(name, j=0, n=1):
            o = VOFF[name] + j
            return vec[:, o:o + n]

        used_cols = [0]

        def sc(n):
            o = used_cols[0]
            used_cols[0] += n
            assert used_cols[0] <= 900
            return sml[:, o:o + n]

        unit_split = {}
        unit_done = {}

        def load_unit(u):
            if u >= NUNIT:
                return
            if u >= NRAW:
                sp.wait(unit_split[u - NRAW])
            nc.sync.dma_start(raw[:, u % NRAW, :], w_d[u]).then_inc(s_raw[u % NRAW], 16)

        def split_unit(u):
            if u >= NUNIT or u in unit_split:
                return
            landed = (s_raw[u % NRAW], 16 * (u // NRAW + 1))
            h, l, r = whi[:, u % NHL, :], wlo[:, u % NHL, :], raw[:, u % NRAW, :]
            used = unit_done[u - NHL] if u >= NHL else None
            hi_made = act.op(A.activation, h, r, ACT.Copy, w=[landed, used])
            lo_made = pool.op(P.tensor_tensor, l, r, h.bitcast(F32), ALU.subtract, w=[hi_made])
            unit_split[u] = lo_made
            load_unit(u + NRAW)

        def split_ahead():
            u = -(-len(plan) // UB)
            for k in range(u, u + NHL):
                if k < NHL or k - NHL in unit_done:
                    split_unit(k)

        def block(b, p, out, start, stop, mark):
            u, j = divmod(len(plan), UB)
            if j == 0:
                for a in range(LOOK + 1):
                    split_unit(u + a)
                pe.wait(unit_split[u])
            plan.append(b)
            c = slice(128 * j, 128 * j + 128)
            wh, wl = whi[:, u % NHL, c], wlo[:, u % NHL, c]
            pe.wait(p.hi_made)
            T.matmul(out, wh, p.hi.r, start=start, stop=False)
            T.matmul(out, wl, p.hi.r, start=False, stop=False)
            pe.wait(p.lo_made)
            mm = T.matmul(out, wh, p.lo.r, start=False, stop=stop)
            if j == UB - 1 or mark:
                m = pe.mark(mm)
                if j == UB - 1:
                    unit_done[u] = m
                return m

        def group(blocks, pairs):
            bank = banks.take()
            pe.wait(*bank.old)
            n = len(blocks)
            for i, (b, p) in enumerate(zip(blocks, pairs)):
                m = block(b, p, bank.ap, i == 0, i == n - 1, i == n - 1)
            bank.made = m
            return bank

        def groups(lists, pairs):
            bs = [banks.take() for _ in lists]
            n = len(pairs)
            for i, p in enumerate(pairs):
                for b, l in zip(bs, lists):
                    if i == 0:
                        pe.wait(*b.old)
                    b.made = block(l[i], p, b.ap, i == 0, i == n - 1, i == n - 1)
            return bs

        def kblocks(name, m, nk):
            return [(name, k, m) for k in range(nk)]

        ready = {}

        def ahead(keys, pairs):
            for k, b in zip(keys, groups([kblocks(n, m, len(pairs)) for n, m in keys], pairs)):
                ready[k] = b

        def tile(name, m, nk, pairs):
            if (name, m) in ready:
                return ready.pop((name, m))
            return group(kblocks(name, m, nk), pairs)

        def split(src, made, lo_on="pool", hi_on="act", two=None):
            p = Pair(places, two)
            if hi_on == "act":
                p.hi_made = act.op(A.activation, p.hi.r, src, ACT.Copy, w=[made, *p.hi.old])
            else:
                p.hi_made = d(V.tensor_copy, p.hi.r, src, w=[made, *p.hi.old])
            e, f = (pool, P.tensor_tensor) if lo_on == "pool" else (dve, TT)
            p.lo_made = e.op(f, p.lo.r, src, p.hi.r.bitcast(F32), ALU.subtract,
                             w=[p.hi_made, *p.lo.old])
            return p

        class Norm:

            def __init__(self):
                self.acc, self.m = None, None

            def add(self, ap, made, scale=1.0, last=False):
                if last:
                    A.preload_act_table(ACT.Sqrt)
                q = take()
                a = act.op(A.activation, q.ap, ap, ACT.Square, scale=scale, w=[made, *q.old])
                if self.acc is None:
                    self.acc, self.m = q, a
                else:
                    self.m = d(TT, self.acc.ap, self.acc.ap, q.ap, ALU.add, w=[a, self.m])
                    q.give(self.m)

        def col_sums(norms, rows=128):
            b = banks.take()
            pe.wait(*b.old, *[n.m for n in norms], ones_m)
            for i, n in enumerate(norms):
                for t in range(4):
                    c = 4 * i + t
                    mm = T.matmul(b.ap[:, c:c + 1], n.acc.ap[0:rows, 128 * t:128 * t + 128],
                                  ones[0:rows, 0:1], start=True, stop=True)
            b.made = pe.mark(mm)
            for n in norms:
                n.acc.give(b.made)
            return b

        def rows_of(cols, made):
            f = take()
            m = d(TT, f.ap.rearrange("p (t n) -> p t n", t=4),
                  ident.unsqueeze(1).broadcast_to([128, 4, 128]),
                  cols.unsqueeze(2).broadcast_to([128, 4, 128]), ALU.mult, w=[made, *f.old])
            b = banks.take()
            pe.wait(*b.old, m)
            b.made = pe.mark(T.matmul(b.ap, ones, f.ap, start=True, stop=True))
            f.give(b.made)
            return b

        def inv_rms_steps(n, width, rows=128):
            b = col_sums([n], rows)
            r = sc(4)
            m = act.op(A.activation, r, b.ap[:, 0:4], ACT.Sqrt, bias=EPS, scale=1.0 / width,
                       w=[b.made])
            b.give(m)
            yield
            m = d(V.reciprocal, r, r, w=[m])
            f = take()
            m = d(TT, f.ap.rearrange("p (t n) -> p t n", t=4),
                  ident.unsqueeze(1).broadcast_to([128, 4, 128]),
                  r.unsqueeze(2).broadcast_to([128, 4, 128]), ALU.mult, w=[m, *f.old])
            yield
            b = banks.take()
            pe.wait(*b.old, m)
            b.made = pe.mark(T.matmul(b.ap, ones, f.ap, start=True, stop=True))
            f.give(b.made)
            return b

        def inv_rms(n, width, rows=128):
            b = col_sums([n], rows)
            r = sc(4)
            m = act.op(A.activation, r, b.ap[:, 0:4], ACT.Sqrt, bias=EPS, scale=1.0 / width,
                       w=[b.made])
            b.give(m)
            m = d(V.reciprocal, r, r, w=[m])
            return rows_of(r, m)

        def normed(xs, gain, bank, keys, shift=None):
            split_ahead()
            out = []
            row = places.row(16)
            for m in range(8):
                two = row[2 * m:2 * m + 2]
                f = take()
                a = d(STT, f.ap, xs[m].ap, gain(m), bank.ap, ALU.mult, ALU.mult,
                      w=[bank.made, xs[m].made, *f.old])
                if shift is None:
                    p = split(f.ap, a, lo_on=NORM_LO[m % 2], hi_on=NORM_HI[m % 2], two=two)
                else:
                    p = Pair(places, two)
                    p.hi_made = act.op(A.activation, p.hi.r, f.ap, ACT.Identity, bias=shift(m),
                                       w=[a, *p.hi.old])
                    p.lo_made = d(STT, p.lo.r, f.ap, shift(m), p.hi.r.bitcast(F32), ALU.add,
                                  ALU.subtract, w=[p.hi_made, *p.lo.old])
                f.give(p.lo_made)
                out.append(p)
            bank.give(a)
            ahead(keys, out)
            return out

        x = [take() for _ in range(8)]
        for m in range(8):
            (A if m < 4 else nc.sync).dma_start(x[m].ap, x_d[m]).then_inc(s_x[m], 16)
            x[m].made = (s_x[m], 16)
        P.dma_start(vec[:, :], vec_d).then_inc(s_vec, 16)
        P.dma_start(cst[:, 0, :], cst_d[0]).then_inc(s_cst, 16)
        P.dma_start(cst[:, 2, :], cst_d[1]).then_inc(s_cst, 16)
        vec_in, cst_in = (s_vec, 16), (s_cst, 32)
        inv_p = places.run(4)
        inv = inv_p.ap.rearrange("p (g n) -> p g n", g=4)
        for u in range(NRAW):
            load_unit(u)
        nc.sync.dma_start(inv, inv_d).then_inc(s_inv, 16)
        ones_m = d(V.memset, ones, 1.0)

        nrm = Norm()
        for m in range(8):
            nrm.add(x[m].ap, x[m].made, last=m == 7)
        dve.wait(vec_in, cst_in)
        act.wait(vec_in, cst_in)
        pe.wait(cst_in)
        rs = inv_rms(nrm, 1024)
        t0, t1, t2, t3 = sc(20), sc(20), sc(20), sc(20)
        half8, neg8 = sc(20), sc(20)
        lam = vc("lam_f", 0, 20)
        sp_m = d(TS, t0, lam, -1.0, None, ALU.mult)
        sp_m = d(TT, t0, t0, lam, ALU.min, w=[sp_m])
        sp_m = act.op(A.activation, t1, t0, ACT.Exp, w=[sp_m])
        h = normed(x, lambda m: vc("g_mix", m), rs,
                   [("w_in", 0), ("w_in", 10), ("w_in", 1), ("w_in", 11)])

        m = d(TS, t2, t1, 2.0, None, ALU.add, w=[sp_m])
        m = d(V.reciprocal, t2, t2, w=[m])
        m = d(TT, t1, t1, t2, ALU.mult, w=[m])
        m = d(TT, t2, t1, t1, ALU.mult, w=[m])
        m = d(V.memset, t3, 1.0 / 19.0, w=[m])
        for k in (17, 15, 13, 11, 9, 7, 5, 3, 1):
            m = d(TT, t3, t3, t2, ALU.mult, w=[m])
            m = d(TS, t3, t3, 1.0 / k, None, ALU.add, w=[m])
        m = d(TT, t3, t3, t1, ALU.mult, w=[m])
        m = d(TS, t2, lam, -1.0, 0.0, ALU.mult, ALU.max, w=[m])
        m = d(STT, t3, t3, 2.0, t2, ALU.mult, ALU.add, w=[m])
        m = d(TS, half8, t3, 4.0, None, ALU.mult, w=[m])
        c8_m = d(TS, neg8, t3, -8.0, None, ALU.mult, w=[m])

        def lru_in(i):
            b = tile("w_in", i, 8, h)
            xa = take()
            a = act.op(A.activation, xa.ap, b.ap, ACT.Identity, bias=vc("conv_a_b", i),
                       scale=vc("conv_a_w", 20 + i), w=[b.made, *xa.old])
            for k, (o, s) in ((0, (slice(2, S), slice(0, S - 2))),
                              (1, (slice(1, S), slice(0, S - 1))),
                              (3, (slice(0, S - 1), slice(1, S)))):
                a = d(STT, xa.ap[:, o], b.ap[:, s], vc("conv_a_w", 10 * k + i), xa.ap[:, o],
                      ALU.mult, ALU.add, w=[a])
            b.give(a)
            xa.made = a
            return i, xa, split(xa.ap, a, lo_on="dve", hi_on="dve")

        def lru_gates(i, xa, p):
            gb = [group([(n, i, i)], [p]) for n in ("wa_f", "wa_b", "wx_f", "wx_b")]
            p.give(gb[-1].made)
            rr, ii, th = [], [], []
            for lst, b, n in ((rr, gb[0], "ba_f"), (rr, gb[1], "ba_b"), (ii, gb[2], "bx_f"),
                              (ii, gb[3], "bx_b")):
                f = take()
                f.made = act.op(A.activation, f.ap, b.ap, ACT.Sigmoid, bias=vc(n, i),
                                w=[b.made, *f.old])
                b.give(f.made)
                lst.append(f)
            for k in range(2):
                f = take()
                c = slice(10 * k + i, 10 * k + i + 1)
                f.made = act.op(A.activation, f.ap, rr[k].ap, ACT.Tanh, scale=half8[:, c],
                                w=[rr[k].made, c8_m, *f.old])
                th.append(f)
                ii[k].made = d(TT, ii[k].ap, ii[k].ap, xa.ap, ALU.mult, w=[ii[k].made, xa.made])
            xa.give(ii[1].made, p.lo_made)
            for k in range(2):
                c = slice(10 * k + i, 10 * k + i + 1)
                rr[k].made = act.op(A.activation, rr[k].ap, rr[k].ap, ACT.Exp, scale=neg8[:, c],
                                    w=[th[k].made])
            for k in range(2):
                th[k].made = act.op(A.activation, th[k].ap, th[k].ap, ACT.Sqrt, w=[th[k].made])
            for k in range(2):
                th[k].made = d(STT, th[k].ap, rr[k].ap, 1.0, th[k].ap, ALU.add, ALU.mult,
                               w=[rr[k].made, th[k].made])
            for k in range(2):
                th[k].made = d(TT, th[k].ap, th[k].ap, ii[k].ap, ALU.mult,
                               w=[th[k].made, ii[k].made])
                ii[k].give(th[k].made)
            m0 = d(SCAN, th[0].ap, rr[0].ap, th[0].ap, 0.0, ALU.mult, ALU.add, w=[th[0].made])
            m1 = d(SCAN, th[1].ap[:, ::-1], rr[1].ap[:, ::-1], th[1].ap[:, ::-1], 0.0, ALU.mult,
                   ALU.add, w=[th[1].made])
            rr[0].give(m0)
            rr[1].give(m1)
            a = d(TT, th[0].ap, th[0].ap, th[1].ap, ALU.add, w=[m0, m1])
            th[1].give(a)
            hs = split(th[0].ap, a, lo_on="dve", hi_on="dve")
            th[0].give(hs.lo_made)
            return hs

        def pool_tile(t):
            w = (2, 4, 8, 16)[t // 2]
            b = tile("w_in", 10 + t, 8, h)
            pl = places.run(4)
            f0, f1, f2 = (pl.ap[:, 600 * k:600 * k + S + 16] for k in range(3))
            z = d(V.memset, f0, 0.0, w=[*pl.old])
            u = act.op(A.activation, f0[:, w // 2:w // 2 + S], b.ap, ACT.Copy, w=[b.made, z])
            b.give(u)
            prev, n, made, k, step = f0, S + w - 1, u, 1, 0
            while k < w:
                n -= k
                o = (f1, f2)[step % 2]
                made = d(TT, o[:, 0:n], prev[:, 0:n], prev[:, k:k + n], ALU.add, w=[made])
                prev, k, step = o, 2 * k, step + 1
            made = d(TT, prev[:, 0:S], prev[:, 0:S], inv[:, t // 2, :], ALU.mult,
                     w=[made, (s_inv, 16)])
            made = d(TT, prev[:, 0:S], prev[:, 0:S], f0[:, w // 2:w // 2 + S], ALU.subtract,
                     w=[made])
            p = split(prev[:, 0:S], made, lo_on="dve", hi_on="dve")
            pl.give(p.lo_made)
            return p

        def pool_mix(t):
            g = t // 2
            b = group([("w_pool", 2 * g + k, t) for k in range(2)], pooled[2 * g:2 * g + 2])
            f = take()
            a = d(TS, f.ap, b.ap, vc("b_pool", t), vc("pool_scale", t), ALU.add, ALU.mult,
                  w=[b.made, *f.old])
            b.give(a)
            if t % 2:
                for q in pooled[2 * g:2 * g + 2]:
                    q.give(b.made)
            p = split(f.ap, a, lo_on="dve", hi_on="dve")
            f.give(p.lo_made)
            return p

        def branch_b(m):
            bg = group(kblocks("w_in", 26 + m, 8), h)
            f = take()
            f.made = act.op(A.activation, f.ap, bg.ap, ACT.Sigmoid, bias=vc("b_gate", 8 + m),
                            w=[bg.made, *f.old])
            bg.give(f.made)
            by = group(kblocks("p_b", m, 8), yb)
            f.made = d(TT, f.ap, by.ap, f.ap, ALU.mult, w=[f.made, by.made])
            by.give(f.made)
            return f

        def gate_a(m):
            bg = group(kblocks("w_in", 18 + m, 8), h)
            f = take()
            f.made = act.op(A.activation, f.ap, bg.ap, ACT.Sigmoid, bias=vc("b_gate", m),
                            w=[bg.made, *f.old])
            bg.give(f.made)
            return f

        hs, pooled, yb, tb, ga = [], [], [], [], []
        work = [lambda t=t: pooled.append(pool_tile(t)) for t in range(8)]
        work += [lambda t=t: yb.append(pool_mix(t)) for t in range(8)]
        work += [lambda m=m: tb.append(branch_b(m)) for m in range(8)]
        for m in range(8):
            x[m].give(*[e.now() for e in (act, dve)])
        todo = None
        for i in range(11):
            n = SHARE[i]
            for _ in range(GATES_A[i]):
                ga.append(gate_a(len(ga)))
            if n == 2 and len(work) > 8:
                work.pop(0)()
                n -= 1
            nxt = lru_in(i) if i < 10 else None
            for _ in range(n // 2):
                work.pop(0)()
            if todo is not None:
                hs.append(lru_gates(*todo))
            for _ in range(n - n // 2):
                work.pop(0)()
            todo = nxt
        assert not work
        for p in yb:
            p.give(pe.now())
        inv_p.give(dve.now())

        mag = sc(16)
        pc = [sc(16) for _ in range(9)]
        ps = [sc(16) for _ in range(9)]
        s5c = {}

        def bc(ap, n):
            return ap.unsqueeze(2).broadcast_to([128, 16, n])

        def s5_constants():
            are, aim = vc("ssm_a_re_2", 0, 16), vc("ssm_a_im_2", 0, 16)
            dt, ang, k_, r_, lre, lim, den, ta, tb_, cre, cim = (sc(16) for _ in range(11))
            m = act.op(A.activation, dt, vc("ssm_log_dt_2", 0, 16), ACT.Exp)
            yield
            m = d(TT, ang, are, dt, ALU.mult, w=[m])
            yield
            mg = act.op(A.activation, mag, ang, ACT.Exp, w=[m])
            yield
            m = d(TT, ang, aim, dt, ALU.mult, w=[mg])
            magic = 12582912.0
            p1, p2 = 6.28125, 0.00193500518798828125
            p3 = 2 * np.pi - p1 - p2
            m = d(TS, k_, ang, float(1.0 / (2 * np.pi)), magic, ALU.mult, ALU.add, w=[m])
            m = d(TS, k_, k_, -magic, None, ALU.add, w=[m])
            m = d(STT, r_, k_, -p1, ang, ALU.mult, ALU.add, w=[m])
            m = d(STT, r_, k_, -p2, r_, ALU.mult, ALU.add, w=[m])
            m = d(STT, r_, k_, -p3, r_, ALU.mult, ALU.add, w=[m])
            m = d(TS, r_, r_, 3.1415925, -3.1415925, ALU.min, ALU.max, w=[m])
            m = d(TS, k_, r_, -1.0, None, ALU.mult, w=[m])
            m = d(TT, k_, k_, r_, ALU.min, w=[m])
            m = d(TS, k_, k_, float(np.pi / 2), None, ALU.add, w=[m])
            yield
            s1 = act.op(A.activation, ps[0], r_, ACT.Sin, w=[m])
            s2 = act.op(A.activation, pc[0], k_, ACT.Sin, w=[m])
            yield
            m = d(TT, lre, mag, pc[0], ALU.mult, w=[s1, s2, mg])
            m = d(TT, lim, mag, ps[0], ALU.mult, w=[m])
            m = d(TS, lre, lre, -1.0, None, ALU.add, w=[m])
            m = d(TT, den, are, are, ALU.mult, w=[m])
            m = d(TT, ta, aim, aim, ALU.mult, w=[m])
            m = d(TT, den, den, ta, ALU.add, w=[m])
            m = d(V.reciprocal, den, den, w=[m])
            m = d(TT, ta, lre, are, ALU.mult, w=[m])
            m = d(TT, tb_, lim, aim, ALU.mult, w=[m])
            m = d(TT, ta, ta, tb_, ALU.add, w=[m])
            m = d(TT, cre, ta, den, ALU.mult, w=[m])
            m = d(TT, ta, lim, are, ALU.mult, w=[m])
            m = d(TT, tb_, lre, aim, ALU.mult, w=[m])
            m = d(TT, ta, ta, tb_, ALU.subtract, w=[m])
            m = d(TT, cim, ta, den, ALU.mult, w=[m])
            s5c["coef"] = cre, cim, m
            yield
            for l in range(8):
                m = d(TT, ta, pc[l], pc[l], ALU.mult, w=[m])
                m = d(TT, tb_, ps[l], ps[l], ALU.mult, w=[m])
                m = d(TT, pc[l + 1], ta, tb_, ALU.subtract, w=[m])
                m = d(STT, ps[l + 1], pc[l], 2.0, ps[l], ALU.mult, ALU.mult, w=[m])
                if l == 3:
                    yield
            yield

            tabp = places.run(2)
            tab = tabp.ap.rearrange("p (c s n) -> p c s n", c=2, s=16)
            ctab, stab = tab[:, 0], tab[:, 1]
            dve.wait(*tabp.old)
            m = d(V.memset, ctab[:, :, 0:1], 1.0, w=[m])
            m = d(V.memset, stab[:, :, 0:1], 0.0, w=[m])
            tf, t2f = take(), take()
            tv = tf.ap.rearrange("p (s n) -> p s n", s=16)
            t2v = t2f.ap.rearrange("p (s n) -> p s n", s=16)
            dve.wait(*tf.old, *t2f.old)
            for l in range(5):
                n = 1 << l
                lo_, hi_ = slice(0, n), slice(n, 2 * n)
                q1, q2 = tv[:, :, 0:n], t2v[:, :, 0:n]
                m = d(TT, ctab[:, :, hi_], ctab[:, :, lo_], bc(pc[l], n), ALU.mult, w=[m])
                m = d(TT, q1, stab[:, :, lo_], bc(ps[l], n), ALU.mult, w=[m])
                m = d(TT, ctab[:, :, hi_], ctab[:, :, hi_], q1, ALU.subtract, w=[m])
                m = d(TT, stab[:, :, hi_], stab[:, :, lo_], bc(pc[l], n), ALU.mult, w=[m])
                m = d(TT, q2, ctab[:, :, lo_], bc(ps[l], n), ALU.mult, w=[m])
                m = d(TT, stab[:, :, hi_], stab[:, :, hi_], q2, ALU.add, w=[m])
            yield
            b, q1, q2 = places.run(2), tf, t2f
            for s in range(16):
                old = [*b.old] if s == 0 else [(s_tw, 16 * s)]
                tc, ts = b.ap[:, 0:S], b.ap[:, S:2 * S]
                a = d(V.tensor_copy, tc[:, 0:32], ctab[:, s], w=[m, *old])
                b2 = d(V.tensor_copy, ts[:, 0:32], stab[:, s])
                for l in range(5, 9):
                    n = 1 << l
                    lo_, hi_ = slice(0, n), slice(n, 2 * n)
                    pcl, psl = pc[l][:, s:s + 1], ps[l][:, s:s + 1]
                    m1 = d(TS, q1.ap[:, lo_], ts[:, lo_], psl, None, ALU.mult, w=[a, b2])
                    m2 = d(TS, q2.ap[:, lo_], tc[:, lo_], psl, None, ALU.mult)
                    a = d(STT, tc[:, hi_], tc[:, lo_], pcl, q1.ap[:, lo_], ALU.mult,
                          ALU.subtract, w=[m1])
                    b2 = d(STT, ts[:, hi_], ts[:, lo_], pcl, q2.ap[:, lo_], ALU.mult,
                           ALU.add, w=[m2])
                yield
                sp.wait(a, b2)
                nc.sync.dma_start(tab_d[s], b.ap).then_inc(s_tw, 16)
            b.give((s_tw, 16 * 16))
            for f in (tf, t2f, tabp):
                f.give(b2)

        def s5_b():
            tf, t2f = take(), take()
            tv = tf.ap.rearrange("p (s n) -> p s n", s=16)
            t2v = t2f.ap.rearrange("p (s n) -> p s n", s=16)
            dve.wait(*tf.old, *t2f.old)
            cre, cim, m = s5c["coef"]
            bre, bim = ssm[:, 0], ssm[:, 1]
            m = d(TT, tv, bre, bc(cim, 32), ALU.mult, w=[m, ssm_in])
            m = d(TT, t2v, bim, bc(cim, 32), ALU.mult, w=[m])
            m = d(TT, bre, bre, bc(cre, 32), ALU.mult, w=[m])
            m = d(TT, bim, bim, bc(cre, 32), ALU.mult, w=[m])
            m = d(TT, bre, bre, t2v, ALU.subtract, w=[m])
            m = d(TT, bim, bim, tv, ALU.add, w=[m])
            m = d(TS, ssm[:, 3], ssm[:, 3], -1.0, None, ALU.mult, w=[m])
            tf.give(m)
            t2f.give(m)
            yield
            for c in range(2):
                b = banks.take()
                pe.wait(*b.old, m)
                for j in range(4):
                    mm = T.transpose(b.ap[:, 128 * j:128 * j + 128],
                                     ssm[:, c, 4 * j:4 * j + 4, :].rearrange("p s n -> p (s n)"),
                                     ident)
                a = act.op(A.activation, bt[:, c].rearrange("p j n -> p (j n)"), b.ap,
                           ACT.Copy, w=[pe.mark(mm), *(s5p.old if c == 0 else [])])
                b.give(a)
            s5c["bt"] = a
            yield

        consts = s5_constants()
        merged = []
        x = []
        for m in range(8):
            f = ga[m] if m < len(ga) else gate_a(m)
            by = group(kblocks("p_a", m, 10), hs)
            a = d(TT, f.ap, by.ap, f.ap, ALU.mult, w=[f.made, by.made])
            by.give(a)
            a = d(TT, f.ap, f.ap, tb[m].ap, ALU.add, w=[a])
            tb[m].give(a)
            p = split(f.ap, a, lo_on="dve", hi_on="dve")
            f.give(p.lo_made)
            merged.append(p)
            next(consts)
            q = take()
            sp.wait(*q.old)
            nc.sync.dma_start(q.ap, x_d[m]).then_inc(s_x[m], 16)
            q.made = (s_x[m], 32)
            x.append(q)
        for p in hs + h:
            p.give(pe.now())

        nrm = Norm()
        for m in range(8):
            b = group(kblocks("w_out", m, 8), merged)
            x[m].made = d(TT, x[m].ap, x[m].ap, b.ap, ALU.add, w=[b.made, x[m].made])
            b.give(x[m].made)
            nrm.add(x[m].ap, x[m].made, last=m == 7)
        for p in merged:
            p.give(pe.now())

        cond = sc(8)
        mod = sc(48)
        mod_used = {}
        mring, macc = places.run(4), places.run(2)
        mod_n, mod_asked = [0], [0]

        def load_mod(u):
            if u < 48 and u == mod_asked[0]:
                mod_asked[0] += 1
                sp.wait(*(mring.old if u < 2 else [mod_used[u - 2]]))
                nc.sync.dma_start(mring.ap[:, 1024 * (u % 2):1024 * (u % 2) + 1024],
                                  mod_d[u]).then_inc(s_mod[u % 2], 16)

        def next_mod():
            u = mod_n[0]
            if u == 48:
                return
            mod_n[0] += 1
            j, k = divmod(u, 8)
            r, c = mring.ap[:, 1024 * (u % 2):1024 * (u % 2) + 1024], cond[:, k:k + 1]
            landed = (s_mod[u % 2], 16 * (u // 2 + 1))
            if k == 0:
                mod_used[u] = d(TS, macc.ap, r, c, None, ALU.mult,
                                w=[landed, cond_m, macc.old if j == 0 else mod_summed[j - 1]])
            else:
                mod_used[u] = d(STT, macc.ap, r, c, macc.ap, ALU.mult, ALU.add,
                                w=[landed, mod_used[u - 1]])
            if k == 7:
                mod_todo.append(j)

        def sum_mod():
            if mod_todo:
                j = mod_todo.pop()
                pe.wait(mod_used[8 * j + 7])
                for q in range(8):
                    mm = T.matmul(misc[:, 8 * j + q:8 * j + q + 1],
                                  macc.ap[:, 128 * q:128 * q + 128], ones[:, 0:1],
                                  start=True, stop=True)
                mod_summed[j] = pe.mark(mm)

        def mod_step():
            if mod_todo:
                sum_mod()
            next_mod()

        mod_todo, mod_summed = [], {}
        load_mod(0)
        load_mod(1)
        rs = inv_rms(nrm, 1024)
        h = normed(x, lambda m: vc("g_ffn", m), rs,
                   [("w_up", 0), ("w_up", 22), ("w_up", 1), ("w_up", 23)])
        cond_m = act.op(A.activation, cond, vc("c_2", 0, 8), ACT.Silu)

        def up_tile(j):
            load_mod(mod_n[0])
            b = tile("w_up", j, 8, h)
            f = take()
            a = act.op(A.activation, f.ap, b.ap, ACT.Identity, bias=vc("conv_f_b", j),
                       scale=vc("conv_f_w", 44 + j), w=[b.made, *f.old])
            a = d(STT, f.ap[:, 1:S], b.ap[:, 0:S - 1], vc("conv_f_w", j), f.ap[:, 1:S], ALU.mult,
                  ALU.add, w=[a])
            a = d(STT, f.ap[:, 0:S - 1], b.ap[:, 1:S], vc("conv_f_w", 88 + j),
                  f.ap[:, 0:S - 1], ALU.mult, ALU.add, w=[a])
            b.give(a)
            f.made = a
            return f

        acts, late = [], []

        def glu_1(g, v):
            g.made = act.op(A.activation, g.ap, g.ap, ACT.Gelu_apprx_tanh, w=[g.made])
            a = d(TT, g.ap, g.ap, v.ap, ALU.mult, w=[g.made, v.made])
            v.give(a)
            p = split(g.ap, a, lo_on=GLU_ON[1], hi_on=GLU_ON[0])
            g.give(p.lo_made)
            acts.append(p)

        for j in range(22):
            g = up_tile(j)
            if late:
                glu_1(*late.pop())
            if j >= MOD_FROM:
                mod_step()
            v = up_tile(22 + j)
            if j >= MOD_FROM:
                mod_step()
            late.append((g, v))
            for _ in range(UP_STEPS[j]):
                next(consts, None)
        glu_1(*late.pop())
        for p in h:
            p.give(pe.now())
        s5p = places.run(6)
        ssm = s5p.ap[:, 0:2048].rearrange("p (c s n) -> p c s n", c=4, s=16)
        bt = s5p.ap[:, 2048:3072].rearrange("p (c j n) -> p c j n", c=2, j=4)
        ukp = places.run(2)
        uk = ukp.ap.rearrange("p (c n) -> p c n", c=2)
        sp.wait(*s5p.old, *ukp.old)
        dve.wait(*s5p.old)
        nc.sync.dma_start(ssm, ssm_d).then_inc(s_ssm, 16)
        nc.sync.dma_start(uk, uk_d).then_inc(s_ssm, 16)
        ssm_in = (s_ssm, 32)
        gs1, gs2 = sc(8), sc(8)
        s5_b_steps = s5_b()
        nrm, nrm_g = Norm(), Norm()
        for m in range(8):
            load_mod(mod_n[0])
            b = group(kblocks("w_down", m, 22), acts)
            x[m].made = d(TT, x[m].ap, x[m].ap, b.ap, ALU.add, w=[b.made, x[m].made])
            b.give(x[m].made)
            nrm_g.add(x[m].ap, x[m].made, scale=vc("g_final", m))
            nrm.add(x[m].ap, x[m].made, last=m == 7)
            if m < 6:
                mod_step()
                if m < MOD_TWICE:
                    load_mod(mod_n[0])
                    mod_step()
            if m == 6:
                sum_mod()
                mring.give(mod_used[47])
                macc.give(mod_summed[5])
                mod_m = d(TT, mod, misc[:, 0:48], vc("b_mod_2", 0, 48), ALU.add, w=[mod_summed[5]])
                banks.free.append((misc[:, :], [mod_m]))

                gs_m = d(STT, gs1, mod[:, 8:16], 1.0, vc("norm1_g_2", 0, 8), ALU.add, ALU.mult,
                         w=[mod_m])
                gs_m = d(TT, gs1, gs1, vc("g_final", 0, 8), ALU.mult, w=[gs_m])
                gs2_m = d(STT, gs2, mod[:, 32:40], 1.0, vc("norm2_g_2", 0, 8), ALU.add, ALU.mult,
                          w=[mod_m])
            if m < 3:
                next(consts, None)
                next(consts, None)
            if m > 3:
                next(s5_b_steps, None)
        for p in acts:
            p.give(pe.now())
        for _ in chain(consts, s5_b_steps):
            pass

        b = col_sums([nrm, nrm_g])
        r1, r2 = sc(4), sc(4)
        m = act.op(A.activation, r1, b.ap[:, 0:4], ACT.Sqrt, bias=EPS, scale=1.0 / 1024,
                   w=[b.made])
        m1 = d(V.reciprocal, r1, r1, w=[m])
        m = d(TT, r2, r1, r1, ALU.mult, w=[m1])
        m = d(TT, r2, b.ap[:, 4:8], r2, ALU.mult, w=[m])
        b.give(m)
        m = act.op(A.activation, r2, r2, ACT.Sqrt, bias=EPS, scale=1.0 / 1024, w=[m])
        m = d(V.reciprocal, r2, r2, w=[m])
        m = d(TT, r2, r2, r1, ALU.mult, w=[m])
        rs = rows_of(r2, m)
        dve.wait(gs_m)
        u = normed(x, lambda m: gs1[:, m:m + 1], rs, [("w_in_2", m) for m in range(4)],
                   shift=lambda m: mod[:, m:m + 1])
        rs = rows_of(r1, m1)
        for m in range(8):
            x[m].made = d(STT, x[m].ap, x[m].ap, vc("g_final", m), rs.ap, ALU.mult, ALU.mult,
                          w=[rs.made, x[m].made])
        rs.give(x[7].made)

        xs = []
        for j in range(4):
            b = tile("w_in_2", j, 8, u)
            f = take()
            f.made = act.op(A.activation, f.ap, b.ap, ACT.Copy, w=[b.made, *f.old])
            b.give(f.made)
            xs.append(f)
        ys = []

        tbuf = places.run(6)
        tab_used = {}

        def tables_load(s):
            if s < 16:
                sp.wait(tab_used[s - 3] if s > 2 else tbuf.old,
                        (s_tw, 16 * (s + 1)))
                nc.sync.dma_start(tbuf.ap[:, 2 * S * (s % 3):2 * S * (s % 3 + 1)],
                                  tab_d[s]).then_inc(s_tr[s % 3], 16)

        def tables(s):
            o = 2 * S * (s % 3)
            return (tbuf.ap[:, o:o + S], tbuf.ap[:, o + S:o + 2 * S],
                    (s_tr[s % 3], 16 * (s // 3 + 1)))

        def s5():
            ybank, late = [None], []

            def outputs(s, q1, q3, made):
                j, i = divmod(s, 4)
                rows = slice(32 * i, 32 * i + 32)
                if i == 0:
                    ybank[0] = banks.take()
                    pe.wait(*ybank[0].old)
                yb_ = ybank[0]
                pe.wait(*made)
                T.matmul(yb_.ap[rows], ssm[:, 2, s, :], q1.ap, start=True, stop=False,
                         tile_position=(0, 32 * i))
                mm = pe.mark(T.matmul(yb_.ap[rows], ssm[:, 3, s, :], q3.ap, start=False,
                                      stop=True, tile_position=(0, 32 * i)))
                q1.give(mm)
                q3.give(mm)
                if i == 3:
                    a = d(STT, xs[j].ap, xs[j].ap, vc("ssm_d_2", j), yb_.ap, ALU.mult,
                          ALU.add, w=[mm, xs[j].made])
                    yb_.give(a)
                    a = act.op(A.activation, xs[j].ap, xs[j].ap, ACT.Gelu_apprx_tanh, w=[a])
                    p = split(xs[j].ap, a, lo_on=YS_ON[1], hi_on=YS_ON[0])
                    xs[j].give(p.lo_made)
                    ys.append(p)

            tables_load(0)
            tables_load(1)
            for s in range(16):
                j, i = divmod(s, 4)
                rows = slice(32 * i, 32 * i + 32)
                tc, ts, landed = tables(s)
                tables_load(s + 2)
                q1, q2 = take(), take()
                bb = []
                for c in range(2):
                    b = banks.take()
                    pe.wait(*b.old, xs[j].made, s5c["bt"])
                    b.made = pe.mark(T.matmul(b.ap, bt[rows, c, j, :], xs[j].ap[rows],
                                              start=True, stop=True))
                    bb.append(b)
                yield
                q3, q4 = take(), take()
                a1 = d(TT, q1.ap, bb[0].ap, tc, ALU.mult, w=[bb[0].made, landed, *q1.old])
                a2 = d(TT, q2.ap, bb[1].ap, ts, ALU.mult, w=[bb[1].made, *q2.old])
                a3 = d(TT, q3.ap, bb[1].ap, tc, ALU.mult, w=[*q3.old])
                a4 = d(TT, q4.ap, bb[0].ap, ts, ALU.mult, w=[*q4.old])
                bb[0].give(a4)
                bb[1].give(a3)
                b1 = pool.op(P.tensor_tensor, q1.ap, q1.ap, q2.ap, ALU.add, w=[a1, a2])
                b3 = pool.op(P.tensor_tensor, q3.ap, q3.ap, q4.ap, ALU.subtract, w=[a3, a4])
                yield
                mg_b = mag[:, s:s + 1].broadcast_to([128, S])
                z1 = d(SCAN, q1.ap, mg_b, q1.ap, 0.0, ALU.mult, ALU.add, w=[b1])
                z2 = d(SCAN, q3.ap, mg_b, q3.ap, 0.0, ALU.mult, ALU.add, w=[b3])
                a2 = d(TT, q2.ap, ts, q3.ap, ALU.mult, w=[z2])
                a4 = d(TT, q4.ap, ts, q1.ap, ALU.mult, w=[z1])
                a1 = d(TT, q1.ap, tc, q1.ap, ALU.mult, w=[a4])
                a3 = d(TT, q3.ap, tc, q3.ap, ALU.mult, w=[a2])
                tab_used[s] = a3
                b1 = pool.op(P.tensor_tensor, q1.ap, q1.ap, q2.ap, ALU.subtract, w=[a1, a2])
                b3 = pool.op(P.tensor_tensor, q3.ap, q3.ap, q4.ap, ALU.add, w=[a3, a4])
                q2.give(b1)
                q4.give(b3)
                yield
                late.append((s, q1, q3, (b1, b3)))
                if len(late) > S5_LATE:
                    outputs(*late.pop(0))
                    yield
            for o in late:
                outputs(*o)
                yield
            s5p.give(pe.now(), dve.now(), act.now())
            tbuf.give(tab_used[15])

        att = []

        def proj(m, scale=1.0):
            b = tile("w_in_2", m, 8, u)
            f = take()
            f.made = act.op(A.activation, f.ap, b.ap, ACT.Copy, scale=scale, w=[b.made, *f.old])
            b.give(f.made)
            return f

        def dsa():
            qi = [proj(9, 0.125), proj(10, 0.125)]
            yield
            kw = proj(11)
            n2 = Norm()
            n2.add(kw.ap, kw.made)
            yield
            b = banks.take()
            pe.wait(*b.old, kw.made)
            for t in range(4):
                mm = T.transpose(b.ap[:, 128 * t:128 * t + 128], kw.ap[:, 128 * t:128 * t + 128],
                                 ident)
            mm = pe.mark(mm)
            wi_c = sc(16)
            wi = wi_c.rearrange("p (t n) -> p t n", t=4)
            wi_m = act.op(A.activation, wi, b.ap.rearrange("p (t n) -> p t n", t=4)[:, :, 64:68],
                          ACT.Copy, scale=0.5, w=[mm])
            b.give(wi_m)
            yield
            r = yield from inv_rms_steps(n2, 64, rows=64)
            ki_m = d(STT, kw.ap[0:64], kw.ap[0:64], vc("idx_k_norm_g_2")[0:64], r.ap[0:64],
                     ALU.mult, ALU.mult, w=[r.made, mm])
            r.give(ki_m)
            sp.wait(ki_m, wi_m, mm)
            nc.sync.dma_start(kw.ap[64:128], kw.ap[0:64]).then_inc(s_ki, 16)
            ki_m = (s_ki, 16)
            yield
            yield
            mp, pp = places.run(3), places.run(4)
            masks = mp.ap
            moff = [0, 128, 384, 768]
            m8 = sc(8)
            need = sc(1)
            mk_m = [d(TS, masks[:, 0:128], tri, 3.3e-9, None, ALU.mult, w=[*mp.old])]
            ck = nat = None
            qt = []
            for t in (3, 2, 1):
                kmax = 128 * (t + 1)
                scr, wk, e1 = take(), take(), take()
                am = None
                for hh in range(4):
                    rows = slice(64 * (hh % 2), 64 * (hh % 2) + 64)
                    b = banks.take()
                    pe.wait(*b.old, qi[hh // 2].made, ki_m)
                    mm = pe.mark(T.matmul(b.ap[:, 0:kmax],
                                          qi[hh // 2].ap[rows, 128 * t:128 * t + 128],
                                          kw.ap[rows, 0:kmax], start=True, stop=True))
                    wcol = wi_c[:, 4 * t + hh:4 * t + hh + 1]
                    f = scr if hh == 0 else take()
                    rm = act.op(A.activation, f.ap[:, 0:kmax], b.ap[:, 0:kmax], ACT.Relu,
                                w=[mm, *f.old])
                    b.give(rm)
                    if hh == 0:
                        am = d(TS, scr.ap[:, 0:kmax], scr.ap[:, 0:kmax], wcol, None, ALU.mult,
                               w=[rm, wi_m])
                    else:
                        am = d(STT, scr.ap[:, 0:kmax], f.ap[:, 0:kmax], wcol,
                               scr.ap[:, 0:kmax], ALU.mult, ALU.add, w=[rm, am])
                        f.give(am)
                am = d(TT, scr.ap[:, kmax - 128:kmax], scr.ap[:, kmax - 128:kmax], tri, ALU.add,
                       w=[am])
                cur = scr.ap[:, 0:kmax]
                dve.wait(*wk.old, *e1.old)
                for rnd in range(16):
                    am = d(V.max, m8, cur, w=[am])
                    if rnd < 15:
                        am = d(V.match_replace, wk.ap[:, 0:kmax], m8, cur, -3.4e38, w=[am])
                        cur = wk.ap[:, 0:kmax]
                    if rnd in (2, 5, 8, 11, 14):
                        if t == 3 and rnd == 2:
                            ck = proj(8)
                            n1 = Norm()
                            n1.add(ck.ap, ck.made)
                        elif t == 3 and rnd == 5:
                            r = yield from inv_rms_steps(n1, 128)
                            ck.made = d(STT, ck.ap, ck.ap, vc("kv_norm_g_2"), r.ap, ALU.mult,
                                        ALU.mult, w=[r.made])
                            r.give(ck.made)
                        elif t == 3 and rnd == 8:
                            b = banks.take()
                            pe.wait(*b.old, ck.made)
                            for k in range(4):
                                mm = T.transpose(b.ap[:, 128 * k:128 * k + 128],
                                                 ck.ap[:, 128 * k:128 * k + 128], ident)
                            nat = take()
                            nat.made = act.op(A.activation, nat.ap, b.ap, ACT.Copy,
                                              w=[pe.mark(mm), *nat.old])
                            b.give(nat.made)
                        yield
                thr = m8[:, 7:8]
                mk = masks[:, moff[t]:moff[t] + kmax]
                am = d(TS, mk, scr.ap[:, 0:kmax], thr, None, ALU.is_gt, ALU.add, accum_out=need,
                       w=[am])
                em = d(TS, e1.ap[:, 0:kmax], scr.ap[:, 0:kmax], thr, None, ALU.is_equal)
                am = d(TS, need, need, -1.0, 128.0, ALU.mult, ALU.add, w=[am])
                em = d(SCAN, wk.ap[:, 0:kmax], e1.ap[:, 0:kmax], e1.ap[:, 0:kmax], 0.0, ALU.add,
                       ALU.max, w=[em])
                em = d(STT, e1.ap[:, 0:kmax], wk.ap[:, 0:kmax], need, e1.ap[:, 0:kmax],
                       ALU.is_le, ALU.mult, w=[em, am])
                em = d(TT, mk, mk, e1.ap[:, 0:kmax], ALU.add, w=[em])
                em = d(TS, mk, mk, -1.0, BIG, ALU.add, ALU.mult, w=[em])
                mk_m.insert(1, em)
                for f in (scr, wk, e1):
                    f.give(em)
                qt.append(proj(4 + len(qt), 0.125))
                yield
            qt.append(proj(7, 0.125))
            for f in qi:
                f.give(pe.now())
            kw.give(pe.now())
            pt = pp.ap.rearrange("p (k n) -> p k n", k=4)
            pt_free = pp.old
            abank = None
            q_made = None

            def latent(hh):
                rows = slice(64 * (hh % 2), 64 * (hh % 2) + 64)
                b = banks.take()
                pe.wait(*b.old, qt[hh // 2].made, ssm_in)
                mm = pe.mark(T.matmul(b.ap, uk[rows, 0, 128 * (hh // 2):128 * (hh // 2) + 128],
                                      qt[hh // 2].ap[rows], start=True, stop=True))
                ql = take()
                ql.made = act.op(A.activation, ql.ap, b.ap, ACT.Copy, w=[mm, *ql.old])
                b.give(ql.made)
                if hh % 2:
                    qt[hh // 2].give(mm)
                return ql

            ql = latent(0)
            yield
            stat = [[sc(4) for _ in range(3)] for _ in range(2)]
            stat_free = [[], []]
            def scores(hh, ql):
                mx, nm, rsm = stat[hh % 2]
                fs = [None] * 4
                for tt in ((3, 2), (1, 0)):
                    bs = {}
                    for t in tt:
                        b = banks.take()
                        pe.wait(*b.old, ql.made, ck.made)
                        b.made = pe.mark(T.matmul(b.ap[:, 0:128 * (t + 1)],
                                                  ql.ap[:, 128 * t:128 * t + 128],
                                                  ck.ap[:, 0:128 * (t + 1)],
                                                  start=True, stop=True))
                        bs[t] = b
                    for t in tt:
                        kmax = 128 * (t + 1)
                        c = slice(t, t + 1)
                        f = fs[t] = take()
                        b = bs[t]
                        a = d(V.tensor_tensor_reduce, f.ap[:, 0:kmax], b.ap[:, 0:kmax],
                              masks[:, moff[t]:moff[t] + kmax], 1.0, NEG, ALU.add, ALU.max,
                              mx[:, c], w=[b.made, mk_m[t], *f.old, *stat_free[hh % 2]])
                        b.give(a)
                        a = d(TS, nm[:, c], mx[:, c], -1.0, None, ALU.mult, w=[a])
                        f.made = act.op(A.activation, f.ap[:, 0:kmax], f.ap[:, 0:kmax], ACT.Exp,
                                        bias=nm[:, c], accum_out=rsm[:, c], w=[a])
                    yield
                return fs

            fs = yield from scores(0, ql)
            for hh in range(8):
                rows = slice(64 * (hh % 2), 64 * (hh % 2) + 64)
                rsm = stat[hh % 2][2]
                for t in (3, 2, 1, 0):
                    c = slice(t, t + 1)
                    fs[t].made = d(V.reciprocal, rsm[:, c], rsm[:, c], w=[fs[t].made])
                for t in (3, 2, 1, 0):
                    kmax = 128 * (t + 1)
                    c = slice(t, t + 1)
                    fs[t].made = d(TS, fs[t].ap[:, 0:kmax], fs[t].ap[:, 0:kmax], rsm[:, c], None,
                                   ALU.mult, w=[fs[t].made])
                stat_free[hh % 2] = [fs[0].made, act.now()]
                ql.give(pe.now())
                if hh < 7:
                    ql = latent(hh + 1)
                    yield
                    nfs = yield from scores(hh + 1, ql)
                pv_w = []
                for t in (3, 2, 1, 0):
                    kmax = 128 * (t + 1)
                    b = banks.take()
                    pe.wait(*b.old, fs[t].made)
                    for k in range(t + 1):
                        mm = T.transpose(b.ap[:, 128 * k:128 * k + 128],
                                         fs[t].ap[:, 128 * k:128 * k + 128], ident)
                    mm = pe.mark(mm)
                    fs[t].give(mm)
                    a = act.op(A.activation, pt[:, 0:t + 1, 128 * t:128 * t + 128],
                               b.ap[:, 0:kmax].rearrange("p (k n) -> p k n", n=128), ACT.Copy,
                               w=[mm, *pt_free])
                    b.give(a)
                    pv_w.append(a)
                yield
                b = banks.take()
                pe.wait(*b.old, *pv_w, nat.made)
                for k in range(4):
                    mm = T.matmul(b.ap[:, 128 * k:S], nat.ap[:, 128 * k:128 * k + 128],
                                  pt[:, k, 128 * k:S], start=(k == 0), stop=(k == 3))
                mm = pe.mark(mm)
                pt_free = [mm]
                o_ = take()
                om = act.op(A.activation, o_.ap, b.ap, ACT.Copy, w=[mm, *o_.old])
                b.give(om)
                yield
                if hh % 2 == 0:
                    abank = banks.take()
                    pe.wait(*abank.old)
                pe.wait(om)
                mm = pe.mark(T.matmul(abank.ap[rows], uk[:, 1, 64 * hh:64 * hh + 64], o_.ap,
                                      start=True, stop=True, tile_position=(0, 64 * (hh % 2))))
                o_.give(mm)
                if hh % 2:
                    p = Pair(places)
                    p.hi_made = act.op(A.activation, p.hi.r, abank.ap, ACT.Copy,
                                       w=[mm, *p.hi.old])
                    p.lo_made = d(TT, p.lo.r, abank.ap, p.hi.r.bitcast(F32), ALU.subtract,
                                  w=[p.hi_made, *p.lo.old])
                    abank.give(p.lo_made)
                    att.append(p)
                fs = nfs
            ck.give(pe.now())
            nat.give(pe.now())
            pp.give(pt_free[0])
            ukp.give(pe.now())
            mp.give(dve.now())

        def gates():
            for k in range(16):
                b = banks.take()
                pe.wait(*b.old)
                for i in range(8):
                    b.made = block(("w_in_2", i, 12 + k), u[i], b.ap, i == 0, i == 7, i == 7)
                    if i in GATE_STOPS:
                        yield
                f = take()
                f.made = act.op(A.activation, f.ap, b.ap, ACT.Sigmoid, w=[b.made, *f.old])
                b.give(f.made)
                act.wait(f.made)
                A.dma_start(spill_d[k], f.ap).then_inc(s_sp[k], 16)
                f.give((s_sp[k], 16))
                yield

        def reload(k):
            f = take()
            sp.wait((s_sp[k], 16), *f.old)
            nc.sync.dma_start(f.ap, spill_d[k]).then_inc(s_sp[k], 16)
            f.made = (s_sp[k], 32)
            return f

        side = []

        def glu():
            for m in range(8):
                fa = reload(m)
                bs = [banks.take(), banks.take()]
                f = take()
                for b, o in zip(bs, (8, 0)):
                    pe.wait(*b.old)
                    for i in range(4):
                        b.made = block(("w_ssm_glu_2", i, o + m), ys[i], b.ap, i == 0, i == 3,
                                       i == 3)
                        if i == 1:
                            yield
                    if o:
                        a = act.op(A.activation, f.ap, b.ap, ACT.Sigmoid,
                                   bias=vc("b_ssm_glu_2", 8 + m), w=[b.made, *f.old])
                        b.give(a)
                        yield
                a = d(STT, f.ap, bs[1].ap, vc("b_ssm_glu_2", m), f.ap, ALU.add, ALU.mult,
                      w=[a, b.made])
                b.give(a)
                f.made = pool.op(P.tensor_tensor, f.ap, f.ap, fa.ap, ALU.mult, w=[a, fa.made])
                fa.give(f.made)
                side.append(f)
                yield

        schedule(dsa(), s5(), gates(), glu())
        for p in u + ys:
            p.give(pe.now())

        merged = []
        sg = {k: reload(8 + k) for k in (0, 1)}
        for m in range(8):
            if m + 2 < 8:
                sg[m + 2] = reload(m + 10)
            f, fb = side[m], sg[m]
            b = group(kblocks("w_attn_proj_2", m, 4), att)
            c = d(TT, fb.ap, b.ap, fb.ap, ALU.mult, w=[b.made, fb.made])
            b.give(c)
            a = d(TT, f.ap, f.ap, fb.ap, ALU.add, w=[f.made, c])
            fb.give(a)
            p = split(f.ap, a, lo_on="dve", hi_on=MERGE_HI)
            f.give(p.lo_made)
            merged.append(p)
        for p in att:
            p.give(pe.now())

        nrm = Norm()

        def gated_add(gcol, m, b):
            x[m].made = d(STT, x[m].ap, b.ap, mod[:, gcol + m:gcol + m + 1], x[m].ap, ALU.mult,
                          ALU.add, w=[b.made, x[m].made])
            b.give(x[m].made)
            nrm.add(x[m].ap, x[m].made, last=m == 7)

        for m in range(8):
            gated_add(16, m, group(kblocks("w_out_2", m, 8), merged))
        for p in merged:
            p.give(pe.now())
        rs = inv_rms(nrm, 1024)
        dve.wait(gs2_m)
        h = normed(x, lambda m: gs2[:, m:m + 1], rs,
                   [("w_ffn_gate_2", 0), ("w_ffn_up_2", 0), ("w_ffn_gate_2", 1),
                    ("w_ffn_up_2", 1)], shift=lambda m: mod[:, 24 + m:25 + m])
        acts = []
        for j in range(22):
            b = tile("w_ffn_gate_2", j, 8, h)
            f = take()
            a = act.op(A.activation, f.ap, b.ap, ACT.Silu, w=[b.made, *f.old])
            b.give(a)
            b = tile("w_ffn_up_2", j, 8, h)
            a = d(TT, f.ap, b.ap, f.ap, ALU.mult, w=[a, b.made])
            b.give(a)
            p = split(f.ap, a, lo_on="dve", hi_on=FFN2_HI)
            f.give(p.lo_made)
            acts.append(p)
        for p in h:
            p.give(pe.now())
        nrm = Norm()
        for m in range(8):
            gated_add(40, m, group(kblocks("w_ffn_down_2", m, 22), acts))
        rs = inv_rms(nrm, 1024)
        for m in range(8):
            a = d(STT, x[m].ap, x[m].ap, vc("final_g_2", m), rs.ap, ALU.mult, ALU.mult,
                  w=[rs.made, x[m].made])
            e, q = (act, A) if m % 2 else (sp, nc.sync)
            e.wait(a)
            q.dma_start(out_d[m], x[m].ap).then_inc(s_out, 16)
        for k in range(16):
            nc.sync.wait_ge(s_sp[k], 32)
        nc.sync.wait_ge(s_out, 16 * 8)
        assert len(plan) == NBLK, len(plan)


def schedule(dsa, s5, gates, glu):
    live = {dsa: 1.0, s5: 0.0}
    due = dict.fromkeys(live, 0.0)
    owed, turn = 0.0, 0
    more = [gates]
    while live:
        if s5 in live:
            live[s5] = S5_PACE[0] if turn < 18 else S5_PACE[1]
        turn += 1
        for g in list(live):
            due[g] += live[g]
            while due[g] >= 1 and g in live:
                due[g] -= 1
                if next(g, "end") == "end":
                    del live[g]
                    if g is s5:
                        more.append(glu)
                owed += FILL[0] if turn < 18 else FILL[1] if s5 in live else FILL[2]
                while owed >= 1 and more:
                    owed -= 1
                    if next(more[0], "end") == "end":
                        more.pop(0)
    for g in more:
        for _ in g:
            pass


def lay_out(inputs, plan):
    f = {k: np.asarray(v) for k, v in inputs.items()}
    one = {k: v[0] for k, v in f.items() if k not in ("x", "g_final", "final_g_2", "c_2")}

    ki = np.zeros((1024, 3584), np.float32)
    w = one["w_in_2"]
    ki[:, 0:1408] = w[:, 0:1408]
    ki[:, 1408:1476] = w[:, 1408:1476]
    ki[:, 1536:3584] = w[:, 1476:3524]
    mats = {n: one[n] for n in ("w_in", "p_a", "p_b", "w_out", "w_up", "w_down", "w_ssm_glu_2",
                                "w_attn_proj_2", "w_out_2", "w_ffn_gate_2", "w_ffn_up_2",
                                "w_ffn_down_2")}
    mats["w_in_2"] = ki
    stream = np.zeros((NUNIT, 128, UB * 128), np.float32)
    for n, (name, k, m) in enumerate(plan):
        u, j = divmod(n, UB)
        if name in ("wa_f", "wx_f", "wa_b", "wx_b"):
            blk = one[name][k]
        elif name == "w_pool":
            blk = one[name][k // 2, 128 * (k % 2):128 * (k % 2) + 128,
                            128 * (m % 2):128 * (m % 2) + 128]
        else:
            blk = mats[name][128 * k:128 * k + 128, 128 * m:128 * m + 128]
        stream[u, :, 128 * j:128 * j + 128] = blk

    vec = np.zeros((128, NV), np.float32)

    def put(name, a):
        a = np.asarray(a).reshape(-1, 128).T
        vec[:, VOFF[name]:VOFF[name] + a.shape[1]] = a

    for name, n in VECS:
        if name == "ssm_log_dt_2":
            put(name, np.repeat(one[name], 64))
        elif name == "idx_k_norm_g_2":
            vec[0:64, VOFF[name]] = one[name]
        elif name in ("g_final", "final_g_2", "c_2"):
            put(name, f[name])
        else:
            put(name, one[name])

    cst = np.zeros((2, 128, 128), np.float32)
    cst[0] = np.eye(128)
    cst[1] = np.where(np.arange(128)[None, :] <= np.arange(128)[:, None], 0.0, NEG)
    t = np.arange(S)
    inv = np.zeros((128, 4, S), np.float32)
    for g, wd in enumerate((2, 4, 8, 16)):
        lo = np.clip(t - wd // 2, 0, S - 1)
        hi = np.clip(t + wd // 2 - 1, 0, S - 1)
        inv[:, g, :] = (1.0 / (hi - lo + 1)).astype(np.float32)

    ssm = np.zeros((128, 4, 16, 32), np.float32)
    for c, name in enumerate(("ssm_b_re_2", "ssm_b_im_2", "ssm_c_re_2", "ssm_c_im_2")):
        a = one[name] if c < 2 else one[name].transpose(0, 2, 1)
        a = a.reshape(16, 2, 64, 16)
        for g in range(2):
            ssm[64 * g:64 * g + 64, c, :, 16 * g:16 * g + 16] = a[:, g].transpose(1, 0, 2)
    uk = np.zeros((128, 2, 512), np.float32)
    uk[:, 0, :] = one["w_uk_2"].transpose(1, 2, 0).reshape(4, 128, 128).transpose(1, 0, 2)\
        .reshape(128, 512)
    uk[:, 1, :] = one["w_uv_2"].reshape(128, 512)
    mod = one["w_mod_2"].reshape(8, 128, 6, 1024).transpose(2, 0, 1, 3).reshape(48, 128, 1024)
    x = f["x"][0].T.reshape(8, 128, S)
    arrays = {"x": x, "w": stream, "mod": mod, "vec": vec, "cst": cst, "inv": inv, "ssm": ssm,
              "uk": uk}
    return {k: np.ascontiguousarray(a) for k, a in arrays.items()}


SHAPES = {"x": (8, 128, S), "w": (NUNIT, 128, UB * 128), "mod": (48, 128, 1024),
          "vec": (128, NV), "cst": (2, 128, 128), "inv": (128, 4, S), "ssm": (128, 4, 16, 32),
          "uk": (128, 2, 512)}


def program(nc):
    aps = [nc.dram_tensor(f"in_{n}", s, F32, kind="ExternalInput").ap() for n, s in SHAPES.items()]
    out = nc.dram_tensor("out_t", (8, 128, S), F32, kind="ExternalOutput").ap()
    spill = nc.dram_tensor("spill", (16, 128, S), F32, kind="Internal").ap()
    plan = []
    tab = nc.dram_tensor("tab", (16, 128, 2 * S), F32, kind="Internal").ap()
    build(nc, *aps, spill, tab, out, plan)
    return plan


def kernel(**inputs):
    from concourse import bacc
    from concourse.bass_utils import run_bass_kernel_spmd

    nc = bacc.Bacc("TRN2", target_bir_lowering=False, num_devices=1)
    plan = program(nc)
    arrays = {f"in_{k}": v for k, v in lay_out(inputs, plan).items()}
    r = run_bass_kernel_spmd(nc, [arrays], core_ids=[0])
    y = r.results[0]["out_t"]
    return np.ascontiguousarray(np.asarray(y).reshape(1024, S).T)[None]
```
